# Optimizing a Trainium2 kernel written in Bass

```python
import jax, jax.numpy as jnp
from jax import lax
import numpy as np

D_MODEL = 1024
BATCH = 1
SEQ = 512
DEPTH = 1
DEC_BATCH = 8
DEC_SEQ = 1
PAST_LEN = 4096
PAGE_SIZE = 128

MIX_WIDTH = D_MODEL
GM_WIDTH = MIX_WIDTH // 2
CV_WIDTH = MIX_WIDTH - GM_WIDTH
GM_HEADS = 4
GM_HEAD_DIM = GM_WIDTH // GM_HEADS
CHUNK = 128
CV_GROUPS = 4
CONV_WIDTH = 31
IN_COLS = 2 * GM_WIDTH + 2 * CV_WIDTH
N_MEM = 256
XA_HEADS = 4
XA_HEAD_DIM = D_MODEL // XA_HEADS
N_GROUPS = 4
EXPERTS_PER_GROUP = 8
TOP_K_IN_GROUP = 2
EXPERT_FF = D_MODEL // 4
EPS = 1e-6

kernel_name = "hymba_gmlp_conformer_memxattn_hmoe_step"

def rms_norm(x, g):
    xf = x.astype(jnp.float32)
    y = xf * lax.rsqrt(jnp.mean(xf * xf, axis=-1, keepdims=True) + EPS)
    return (y * g.astype(jnp.float32)).astype(x.dtype)

def layer_norm(x, g, b):
    xf = x.astype(jnp.float32)
    mu = jnp.mean(xf, axis=-1, keepdims=True)
    var = jnp.mean(jnp.square(xf - mu), axis=-1, keepdims=True)
    y = (xf - mu) * lax.rsqrt(var + EPS)
    return (y * g.astype(jnp.float32) + b.astype(jnp.float32)).astype(x.dtype)

def chunk_spatial_mix(v, ws, bs):
    n, t, h, p = v.shape
    n_chunks = -(-t // CHUNK)
    pad = n_chunks * CHUNK - t
    vc = jnp.pad(v, ((0, 0), (0, pad), (0, 0), (0, 0))).reshape(n, n_chunks, CHUNK, h, p)
    mask = jnp.tril(jnp.ones((CHUNK, CHUNK), dtype=bool))
    w = jnp.where(mask[None], ws, 0).astype(v.dtype)
    mixed = jnp.einsum('hts,ncshp->ncthp', w, vc) + bs.T.astype(v.dtype)[None, None, :, :, None]
    return mixed.reshape(n, n_chunks * CHUNK, h, p)[:, :t]

def mixer_block(x, conv_past, norm_g, w_in, gm_ln_g, gm_ln_b, gm_ws, gm_bs,
                conv_w, conv_b, cv_ln_g, cv_ln_b, w_out):
    n, t, _ = x.shape
    z = rms_norm(x, norm_g) @ w_in
    gm_u, gm_v, cv_a, cv_b = jnp.split(z, [GM_WIDTH, 2 * GM_WIDTH, 2 * GM_WIDTH + CV_WIDTH], axis=-1)
    u = jax.nn.gelu(gm_u).reshape(n, t, GM_HEADS, GM_HEAD_DIM)
    v = layer_norm(jax.nn.gelu(gm_v).reshape(n, t, GM_HEADS, GM_HEAD_DIM), gm_ln_g, gm_ln_b)
    a_out = (u * chunk_spatial_mix(v, gm_ws, gm_bs)).reshape(n, t, GM_WIDTH)
    glu = cv_a * jax.nn.sigmoid(cv_b)
    full = jnp.concatenate([conv_past.astype(glu.dtype), glu], axis=1)
    conv = lax.conv_general_dilated(
        full, conv_w.astype(full.dtype)[:, None, :], window_strides=(1,), padding='VALID',
        dimension_numbers=('NWC', 'WIO', 'NWC'), feature_group_count=CV_WIDTH) + conv_b.astype(full.dtype)
    b_out = jax.nn.silu(layer_norm(conv, cv_ln_g, cv_ln_b))
    y = x + jnp.concatenate([a_out, b_out], axis=-1) @ w_out
    start = ((t - 1) // CHUNK) * CHUNK
    v_rows = v[:, start:].reshape(n, t - start, GM_WIDTH)
    return y, full[:, -(CONV_WIDTH - 1):], v_rows

def memory_kv(mem, norm_g, wk, wv):
    n = mem.shape[0]
    mn = rms_norm(mem, norm_g)
    k = (mn @ wk).reshape(n, N_MEM, XA_HEADS, XA_HEAD_DIM)
    v = (mn @ wv).reshape(n, N_MEM, XA_HEADS, XA_HEAD_DIM)
    return k, v

def memory_cross_attention(x, mem_k, mem_v, norm_g, wq, wo):
    n, t, _ = x.shape
    q = (rms_norm(x, norm_g) @ wq).reshape(n, t, XA_HEADS, XA_HEAD_DIM)
    s = jnp.einsum('nthd,nmhd->nhtm', q, mem_k.astype(q.dtype)).astype(jnp.float32) * (XA_HEAD_DIM ** -0.5)
    p = jax.nn.softmax(s, axis=-1).astype(x.dtype)
    o = jnp.einsum('nhtm,nmhd->nthd', p, mem_v.astype(x.dtype)).reshape(n, t, D_MODEL)
    return x + o @ wo

def hier_moe(x, norm_g, router_g, router_g_b, router_e, router_e_b, exp_w1, exp_w3, exp_w2):
    n, t, _ = x.shape
    xt = rms_norm(x, norm_g).reshape(n * t, D_MODEL)
    g_logits = (xt @ router_g).astype(jnp.float32) + router_g_b.astype(jnp.float32)
    g_prob = jax.nn.softmax(g_logits, axis=-1)
    g_idx = jnp.argmax(g_logits, axis=-1)
    p_g = jnp.take_along_axis(g_prob, g_idx[:, None], axis=-1)[:, 0]
    e_logits = jnp.einsum('td,dge->tge', xt, router_e).astype(jnp.float32) + router_e_b.astype(jnp.float32)
    e_sel = jnp.take_along_axis(e_logits, g_idx[:, None, None], axis=1)[:, 0]
    top_v, top_i = lax.top_k(e_sel, TOP_K_IN_GROUP)
    top_w = jax.nn.softmax(top_v, axis=-1) * p_g[:, None]
    within = jnp.sum(jax.nn.one_hot(top_i, EXPERTS_PER_GROUP, dtype=jnp.float32) * top_w[..., None], axis=1)
    comb = (jax.nn.one_hot(g_idx, N_GROUPS, dtype=jnp.float32)[:, :, None] * within[:, None, :]).astype(xt.dtype)
    out = jnp.zeros_like(xt)
    for g in range(N_GROUPS):
        h1 = jnp.einsum('td,edf->tef', xt, exp_w1[g])
        h3 = jnp.einsum('td,edf->tef', xt, exp_w3[g])
        act = jax.nn.silu(h1) * h3 * comb[:, g, :, None]
        out = out + jnp.einsum('tef,efd->td', act, exp_w2[g])
    return x + out.reshape(n, t, D_MODEL)

def setup_inputs(seed: int = 0) -> dict:
    key = jax.random.key(seed)
    k = jax.random.split(key, 40)
    f32 = jnp.float32

    def nrm(kk, shape, scale):
        return jax.random.normal(kk, shape, f32) * scale

    L = DEPTH
    H, P = GM_HEADS, GM_HEAD_DIM
    G, E, F = N_GROUPS, EXPERTS_PER_GROUP, EXPERT_FF
    return {
        "x_prompt": nrm(k[0], (BATCH, SEQ, D_MODEL), 1.0),
        "x_sample": nrm(k[1], (DEC_BATCH, DEC_SEQ, D_MODEL), 1.0),
        "mem_prompt": nrm(k[2], (BATCH, N_MEM, D_MODEL), 1.0),
        "cache_conv": nrm(k[3], (L, DEC_BATCH, CONV_WIDTH - 1, CV_WIDTH), 0.5),
        "cache_mem_k": nrm(k[4], (L, DEC_BATCH, N_MEM, XA_HEADS, XA_HEAD_DIM), 1.0),
        "cache_mem_v": nrm(k[5], (L, DEC_BATCH, N_MEM, XA_HEADS, XA_HEAD_DIM), 1.0),
        "norm_mix_g": 1.0 + nrm(k[6], (L, D_MODEL), 0.02),
        "w_in": nrm(k[7], (L, D_MODEL, IN_COLS), D_MODEL ** -0.5),
        "gm_ln_g": 1.0 + nrm(k[8], (L, H, P), 0.02),
        "gm_ln_b": nrm(k[9], (L, H, P), 0.02),
        "gm_ws": nrm(k[10], (L, H, CHUNK, CHUNK), CHUNK ** -0.5),
        "gm_bs": 1.0 + nrm(k[11], (L, H, CHUNK), 0.02),
        "conv_w": nrm(k[12], (L, CONV_WIDTH, CV_WIDTH), CONV_WIDTH ** -0.5),
        "conv_b": nrm(k[13], (L, CV_WIDTH), 0.02),
        "cv_ln_g": 1.0 + nrm(k[14], (L, CV_WIDTH), 0.02),
        "cv_ln_b": nrm(k[15], (L, CV_WIDTH), 0.02),
        "w_out": nrm(k[16], (L, MIX_WIDTH, D_MODEL), MIX_WIDTH ** -0.5),
        "norm_mem_g": 1.0 + nrm(k[17], (L, D_MODEL), 0.02),
        "norm_xa_g": 1.0 + nrm(k[18], (L, D_MODEL), 0.02),
        "xa_wq": nrm(k[19], (L, D_MODEL, D_MODEL), D_MODEL ** -0.5),
        "xa_wk": nrm(k[20], (L, D_MODEL, D_MODEL), D_MODEL ** -0.5),
        "xa_wv": nrm(k[21], (L, D_MODEL, D_MODEL), D_MODEL ** -0.5),
        "xa_wo": nrm(k[22], (L, D_MODEL, D_MODEL), D_MODEL ** -0.5),
        "norm_ffn_g": 1.0 + nrm(k[23], (L, D_MODEL), 0.02),
        "router_g": nrm(k[24], (L, D_MODEL, G), D_MODEL ** -0.5),
        "router_g_b": nrm(k[25], (L, G), 0.01),
        "router_e": nrm(k[26], (L, D_MODEL, G, E), D_MODEL ** -0.5),
        "router_e_b": nrm(k[27], (L, G, E), 0.01),
        "exp_w1": nrm(k[28], (L, G, E, D_MODEL, F), D_MODEL ** -0.5),
        "exp_w3": nrm(k[29], (L, G, E, D_MODEL, F), D_MODEL ** -0.5),
        "exp_w2": nrm(k[30], (L, G, E, F, D_MODEL), F ** -0.5),
        "final_norm_g": 1.0 + nrm(k[31], (D_MODEL,), 0.02),
    }

def reference(x_prompt, x_sample, mem_prompt, cache_conv, cache_mem_k, cache_mem_v,
              norm_mix_g, w_in, gm_ln_g, gm_ln_b, gm_ws, gm_bs, conv_w, conv_b, cv_ln_g, cv_ln_b, w_out,
              norm_mem_g, norm_xa_g, xa_wq, xa_wk, xa_wv, xa_wo,
              norm_ffn_g, router_g, router_g_b, router_e, router_e_b, exp_w1, exp_w3, exp_w2,
              final_norm_g):
    hp, hs = x_prompt, x_sample
    conv_p, conv_s, gmv_p, gmv_s, mk_p, mv_p = [], [], [], [], [], []
    for l in range(DEPTH):
        mk, mv = memory_kv(mem_prompt, norm_mem_g[l], xa_wk[l], xa_wv[l])
        zero_past = jnp.zeros((hp.shape[0], CONV_WIDTH - 1, CV_WIDTH), hp.dtype)
        hp, cp, vp = mixer_block(hp, zero_past, norm_mix_g[l], w_in[l], gm_ln_g[l], gm_ln_b[l], gm_ws[l], gm_bs[l],
                                 conv_w[l], conv_b[l], cv_ln_g[l], cv_ln_b[l], w_out[l])
        hs, cs, vs = mixer_block(hs, cache_conv[l], norm_mix_g[l], w_in[l], gm_ln_g[l], gm_ln_b[l], gm_ws[l], gm_bs[l],
                                 conv_w[l], conv_b[l], cv_ln_g[l], cv_ln_b[l], w_out[l])
        hp = memory_cross_attention(hp, mk, mv, norm_xa_g[l], xa_wq[l], xa_wo[l])
        hs = memory_cross_attention(hs, cache_mem_k[l], cache_mem_v[l], norm_xa_g[l], xa_wq[l], xa_wo[l])
        hp = hier_moe(hp, norm_ffn_g[l], router_g[l], router_g_b[l], router_e[l], router_e_b[l],
                      exp_w1[l], exp_w3[l], exp_w2[l])
        hs = hier_moe(hs, norm_ffn_g[l], router_g[l], router_g_b[l], router_e[l], router_e_b[l],
                      exp_w1[l], exp_w3[l], exp_w2[l])
        conv_p.append(cp)
        conv_s.append(cs)
        gmv_p.append(vp)
        gmv_s.append(vs)
        mk_p.append(mk)
        mv_p.append(mv)
    y_prompt = rms_norm(hp, final_norm_g)
    y_sample = rms_norm(hs, final_norm_g)
    return (y_prompt, y_sample, jnp.stack(conv_p), jnp.stack(conv_s), jnp.stack(gmv_p), jnp.stack(gmv_s),
            jnp.stack(mk_p), jnp.stack(mv_p))


_drawn_inputs = setup_inputs


def setup_inputs(seed=0):
    import zlib

    import numpy as np

    out = dict(_drawn_inputs(seed))
    spreads = {}
    factors = {'gm_ln_g': 8.091,
     'gm_ln_b': 13.832,
     'gm_bs': 2.83,
     'cv_ln_g': 3.712,
     'cv_ln_b': 3.742,
     'norm_mem_g': 2.869,
     'norm_xa_g': 5.724,
     'router_g_b': 14.806,
     'router_e_b': 4.368,
     'final_norm_g': 23.394}
    for name, (base, spread) in spreads.items():
        noise = np.random.default_rng([zlib.crc32(name.encode()), seed]).standard_normal(out[name].shape)
        drawn = base * np.exp(spread * noise) if base else spread * noise
        out[name] = __import__('jax').numpy.asarray(drawn.astype(out[name].dtype))
    for name, factor in factors.items():
        out[name] = (out[name] * factor).astype(out[name].dtype)
    return out
```

```python
from contextlib import ExitStack

import numpy as np

import concourse.bass as bass
from concourse import mybir

F32 = mybir.dt.float32
F32R = mybir.dt.float32r
I32 = mybir.dt.int32
ALU = mybir.AluOpType
ACT = mybir.ActivationFunctionType
AX_X = mybir.AxisListType.X

P = 128
D = 1024
KT_D = D // P
SEQ = 512
NS = 8
T = SEQ + NS
HT = T // 2
TILES = [(0, P), (P, P), (2 * P, P), (3 * P, P), (SEQ, NS)]
NT = len(TILES)
GM = 512
HEADS = 4
TAPS = 31
PAST = TAPS - 1
MEM = 256
XH_DIM = 256
NG, NE = 4, 8
EXPERTS = NG * NE
FF = 256
EPS = 1e-6
CHUNK = 2048
SLOT_BYTES = 4 * CHUNK
RAW = 5
LIST_ROWS = 5 * P
NOBODY = 1 << 20
SCALE = float(XH_DIM) ** -0.5

W_IN_COLS = [1024, 1536, 1280, 1792, 512, 768, 0, 256]
STREAM = ([("x", 0), ("x", 1)] + [("w_in", i) for i in range(8)] + [("mem", 0)]
          + [("wk", i) for i in range(4)] + [("wv", i) for i in range(4)] + [("w_out", i) for i in range(4)]
          + [("wq", i) for i in range(4)] + [("wo", 0), ("wo", 1)] + [("kc", i) for i in range(NS)]
          + [("vc", i) for i in range(NS)] + [("wo", 2), ("wo", 3)])
AT = {key: c for c, key in enumerate(STREAM)}
WEIGHTS = [key for key in STREAM if key[0][0] == "w"]
W_AT = {key: n for n, key in enumerate(WEIGHTS)}

MM_ORDER = ([("w_in", i) for i in range(16)] + [("wk", i) for i in range(8)] + [("wv", i) for i in range(8)]
            + [("w_out", i) for i in range(8)] + [("wq", i) for i in range(8)] + [("score", i) for i in range(4)]
            + [("pv", i) for i in range(4)] + [("wo", i) for i in range(8)])
MM_AT = {key: m for m, key in enumerate(MM_ORDER)}

TV_ORDER = (["cols_a", "cols_b"] + [f"x{j}" for j in range(NT)] + ["rs0", "rs1", "ws", "cc0", "cc1"]
            + [f"v{j}" for j in range(NT)] + [f"mem{i}" for i in range(4)] + ["vs"] + [f"mix{h}" for h in range(4)]
            + [f"kt{h}" for h in range(4)] + [f"cf{j}" for j in range(NT)] + ["rs2", "rs3"]
            + [f"qb{s}{b}" for s in range(NS) for b in range(2)] + ["ss", "sp", "so", "r2", "lg"]
            + [f"t{j}" for j in range(NT)] + ["pos", "cnt"])
TV_AT = {key: v for v, key in enumerate(TV_ORDER)}
TA_ORDER = ([f"x{j}" for j in range(NT)] + ["tail"] + [f"cb{j}" for j in range(NT)] + ["qs0", "qs1"]
            + [f"pt{j}{b}" for j in range(4) for b in range(2)] + [f"t{j}" for j in range(NT)])
TA_AT = {key: a for a, key in enumerate(TA_ORDER)}

ROWS_A = {"mix_g": 0, "mem_g": 8, "xa_g": 16, "ffn_g": 24, "conv_b": 32, "cv_g": 36, "cv_b": 40}
N_ROWS_A = 44
N_ROWS_B = TAPS * 4


def mm_after(n):
    kind, i = WEIGHTS[n]
    return MM_AT[(kind, 2 * i + 1)] + 1


def trunk_kernel(nc, a, outs):
    (y_prompt, y_sample, conv_prompt, conv_sample, gmv_prompt, gmv_sample, mem_k_out, mem_v_out) = outs

    xn_rows = nc.dram_tensor("xn_rows", (T, D), F32, kind="Internal").ap()
    y_rows = nc.dram_tensor("y_rows", (2 * T, D), F32, kind="Internal").ap()
    id_list = nc.dram_tensor("id_list", (LIST_ROWS * EXPERTS, 1), I32, kind="Internal").ap()

    with ExitStack() as ctx:
        def sem(name):
            return ctx.enter_context(nc.semaphore(name))

        base = (nc.sbuf_base + 63) // 64 * 64
        top = [base]

        def room(nbytes):
            at = top[0]
            top[0] += (nbytes + 31) // 32 * 32
            assert top[0] <= base + 212600, top[0]
            return at

        def at(name, shape, dt, offset):
            return nc.alloc_sbuf_tensor_at(name, shape, dt, offset=offset)

        def sb(name, shape, dt=F32):
            return at(name, shape, dt, room(4 * int(np.prod(shape[1:]))))

        raw_at = [room(SLOT_BYTES) for _ in range(RAW)]
        raw = [at(f"raw{i}", [P, CHUNK], F32, o) for i, o in enumerate(raw_at)]
        hl_at = [room(2 * SLOT_BYTES) for _ in range(2)]
        w_h = [at(f"w_h{i}", [P, CHUNK], F32R, o) for i, o in enumerate(hl_at)]
        w_l = [at(f"w_l{i}", [P, CHUNK], F32R, o + SLOT_BYTES) for i, o in enumerate(hl_at)]
        ROW = 4 * T
        x_at, xh_at, xl_at, ch_at, cl_at = (room(8 * ROW) for _ in range(5))
        xT = at("xT", [P, 8, T], F32, x_at)
        xH = at("xH", [P, 8, T], F32R, xh_at)
        xL = at("xL", [P, 8, T], F32R, xl_at)
        cH = at("cH", [P, 8, T], F32R, ch_at)
        cL = at("cL", [P, 8, T], F32R, cl_at)
        glu_at = room(4 * 4 * (PAST + SEQ + NS))
        glu = at("glu", [P, 4, PAST + T], F32, glu_at)
        kT_at = room(SLOT_BYTES)
        v_at = room(SLOT_BYTES)
        kT = at("kT", [P, 8, MEM], F32, kT_at)
        vm = at("vm", [P, 2, D], F32, v_at)
        ident = sb("ident", [P, P])
        ones = sb("ones", [P, P])
        upper = sb("upper", [P, P])
        g1_at = room(4 * D)
        wsT = at("wsT", [P, HEADS, P], F32, g1_at)
        bs_all = at("bs_all", [P, HEADS, P], F32, g1_at + 2 * D)
        g2_at = room(4 * D)
        ln_g = at("ln_g", [P, GM], F32, g2_at)
        ln_b = at("ln_b", [P, GM], F32, g2_at + 2 * D)
        cols_a = sb("cols_a", [P, N_ROWS_A])
        cols_b = sb("cols_b", [P, TAPS, 4])
        rstd = sb("rstd", [P, 2, HT])
        sumsq = sb("sumsq", [P, T])
        z_at = room(2 * ROW)
        zt = [at(f"zt{i}", [P, T], F32, z_at + i * ROW) for i in range(2)]
        s_at = room(2048 + 4 * 4 * NS * TAPS)
        v_s = at("v_s", [P, GM], F32, s_at)
        conv_s = at("conv_s", [P, 4, NS, TAPS], F32, s_at + 2048)
        stats = sb("stats", [P, NT, 4, 6])
        mv = sb("mv", [P, NT, 4, 2])
        ws00 = sb("ws00", [P, HEADS])
        vsT = sb("vsT", [P, HEADS, NS])
        m_ss = sb("m_ss", [P, 2])
        pmax = sb("pmax", [P, 4, 4])
        psum_p = sb("psum_p", [P, 4, 4])
        s_sc = sb("s_sc", [P, 2, NS * HEADS])
        s_mx = sb("s_mx", [P, 4])
        s_pT = sb("s_pT", [P, 2, NS * HEADS])
        rs5 = sb("rs5", [P, NT])
        ids = sb("ids", [P, LIST_ROWS // P, EXPERTS], I32)
        gids = sb("gids", [P, LIST_ROWS // P, EXPERTS], I32)
        g_idx = [sb(f"g_idx{i}", [P, 1], I32) for i in range(2)]
        s_idx = [sb(f"s_idx{i}", [P, 1], I32) for i in range(2)]
        wgt = sb("wgt", [P, 2, NT])
        more = sb("more", [P, 1], I32)
        fin_ss = sb("fin_ss", [P, NT])

        cHf = at("cHf", [P, 8, T], F32, ch_at)
        cLf = at("cLf", [P, 8, T], F32, cl_at)
        rows_a = at("rows_a", [N_ROWS_A, P], F32, glu_at)
        rows_b = at("rows_b", [N_ROWS_B, P], F32, glu_at + 512)
        xs_rows = at("xs_rows", [NS, D], F32, cl_at)
        ws_rows = at("ws_rows", [P, HEADS, P], F32, kT_at)
        cache_rows = at("cache_rows", [4 * PAST, 2, GM], F32, v_at)
        tail = at("tail", [PAST + NS, GM], F32, kT_at)
        list_init = at("list_init", [P, LIST_ROWS // P * EXPERTS // 2], I32, v_at + 4096)
        v_raw = cHf[:, 0:4, :]
        v_tok = at("v_tok", [P, 4, GM], F32, ch_at + 4 * ROW)
        scaled = [at(f"scaled{i}", [P, SEQ], F32, ch_at + 4 * ROW + 4 * SEQ * i) for i in range(4)]
        u_act = cLf[:, 0:4, :]
        conv = cLf[:, 4:8, :]
        qT = cHf
        probs = [at(f"probs{i}", [P, HEADS, MEM], F32, glu_at + 4096 * i) for i in range(2)]
        pT = at("pT", [P, HEADS, 2, SEQ], F32, cl_at)
        q_s = at("q_s", [NS, D], F32, z_at)
        pick = at("pick", [NS, NS, P], F32, s_at)
        ttr_out = at("ttr_out", [P, MEM], F32, g2_at)
        s_p = at("s_p", [NS * HEADS, MEM], F32, g2_at + 1024)
        router = at("router", [P, KT_D, NG + EXPERTS], F32, s_at + 4096)
        mem_junk = at("mem_junk", [P, D], F32, kT_at + 4096)
        x2 = at("x2", [P, NT, D], F32, ch_at)
        xn = [at(f"xn{i}", [P, D], F32, ch_at + 20480 + 4096 * i) for i in range(2)]
        ffn_g = at("ffn_g", [P, D], F32, g2_at)
        fin_g = at("fin_g", [P, D], F32, g1_at)
        r_at = [glu_at]

        def route(name, shape, dt=F32):
            o = r_at[0]
            r_at[0] += (4 * int(np.prod(shape[1:])) + 31) // 32 * 32
            assert r_at[0] <= kT_at
            return at(name, shape, dt, o)

        r_bias = route("r_bias", [P, NG + EXPERTS])
        logits = route("logits", [P, NT, NG + EXPERTS])
        prio = route("prio", [P, 8])
        e_num = route("e_num", [P, EXPERTS])
        valid = route("valid", [P, NT])
        g_max = route("g_max", [P, NT])
        g_ex = route("g_ex", [P, NT, NG])
        g_sum = route("g_sum", [P, NT])
        g_sel = route("g_sel", [P, NT, NG])
        e_all = route("e_all", [P, NT, NG, NE])
        e_sel = route("e_sel", [P, NT, NE])
        e_max = route("e_max", [P, 2, NT])
        e_tmp = route("e_tmp", [P, NT, NE])
        e_one = route("e_one", [P, 2, NT, NE])
        e_m = route("e_m", [P, NT])
        who = [route(f"who{i}", [P, NT, EXPERTS]) for i in range(2)]
        both = route("both", [P, NT, EXPERTS])
        ptmp = route("ptmp", [P, NT, EXPERTS])
        place = route("place", [P, 2, NT])
        place_i = route("place_i", [P, 2, NT], I32)
        ident_no = route("ident_no", [P, 2, NT], I32)
        w_ex = route("w_ex", [P, 3, NT])
        c_max = route("c_max", [P, 2])

        raw_e = [raw[(len(STREAM) + m) % RAW] for m in range(RAW)] + [at("raw_e5", [P, CHUNK], F32, xh_at)]
        xe = [at(f"xe{i}", [P, D], F32, xh_at + SLOT_BYTES + 4096 * i) for i in range(2)]
        xeH = at("xeH", [P, KT_D, P], F32R, xl_at)
        xeL = at("xeL", [P, KT_D, P], F32R, xl_at + 4096)
        ye = [at(f"ye{i}", [P, D], F32, xl_at + SLOT_BYTES + 4096 * i) for i in range(2)]
        e_h = w_h + [at("e_h2", [P, CHUNK], F32R, kT_at)]
        e_l = w_l + [at("e_l2", [P, CHUNK], F32R, v_at)]
        silu = at("silu", [P, FF], F32, s_at)
        gated = at("gated", [P, FF], F32, s_at + 1024)
        aH = at("aH", [P, 2, P], F32R, s_at + 2048)
        aL = at("aL", [P, 2, P], F32R, s_at + 3072)
        yr = [at(f"yr{i}", [P, 2, D], F32, hl_at[0] + SLOT_BYTES * i) for i in range(2)]
        yo = [at(f"yo{i}", [P, D], F32, hl_at[1] + 4096 * i) for i in range(2)]
        sq_junk = at("sq_junk", [P, D], F32, hl_at[1] + 8192)

        ps = [ctx.enter_context(nc.psum_tensor(f"ps{i}", [P, 2, 512], F32)) for i in range(4)]
        mm = ps[0:2]
        tv = [ps[2][:, b, :] for b in range(2)]
        ta = [ps[3][:, b, :] for b in range(2)]

        landed = [sem(f"landed{i}") for i in range(RAW)]
        params_in = sem("params_in")
        consts_in = sem("consts_in")
        rows_in = sem("rows_in")
        pool_made = sem("pool_made")
        dve_made = sem("dve_made")
        h_ready = sem("h_ready")
        l_ready = sem("l_ready")
        mm_ready = sem("mm_ready")
        mm_used = sem("mm_used")
        tv_ready = sem("tv_ready")
        tv_used = sem("tv_used")
        ta_ready = sem("ta_ready")
        ta_used = sem("ta_used")
        own = sem("own")
        xh_ready = sem("xh_ready")
        xl_ready = sem("xl_ready")
        sq_ready = sem("sq_ready")
        sq_added = sem("sq_added")
        rs_root = sem("rs_root")
        rs_ready = sem("rs_ready")
        z_act = sem("z_act")
        glu_ready = sem("glu_ready")
        conv_v = sem("conv_v")
        tap_scaled = sem("tap_scaled")
        conv_p = sem("conv_p")
        convs_done = sem("convs_done")
        v_mean = sem("v_mean")
        v_root = sem("v_root")
        v_norm = sem("v_norm")
        v_ready = sem("v_ready")
        v_scaled = sem("v_scaled")
        a_ready = sem("a_ready")
        ttr_done = sem("ttr_done")
        mem_sq = sem("mem_sq")
        k_stored = [sem(f"k_stored{i}") for i in range(2)]
        tail_stored = sem("tail_stored")
        gmv_stored = sem("gmv_stored")
        vm_stored = sem("vm_stored")
        m_mean = sem("m_mean")
        m_root = sem("m_root")
        masked = sem("masked")
        pick_made = sem("pick_made")
        route_made = sem("route_made")
        c_mean = sem("c_mean")
        c_root = sem("c_root")
        cn_ready = sem("cn_ready")
        p_max = sem("p_max")
        p_exp = sem("p_exp")
        p_ready = sem("p_ready")
        vc_used = sem("vc_used")
        s_max = sem("s_max")
        s_exp = sem("s_exp")
        s_norm = sem("s_norm")
        s_ready = sem("s_ready")
        oh_ready = sem("oh_ready")
        r_in = sem("r_in")
        r_w_in = sem("r_w_in")
        rg_ready = sem("rg_ready")
        r_root = sem("r_root")
        r_ready = sem("r_ready")
        xn_ready = sem("xn_ready")
        xn_stored = [sem(f"xn_stored{i}") for i in range(2)]
        g_exp = sem("g_exp")
        g_dif = sem("g_dif")
        who_ready = sem("who_ready")
        place_ready = sem("place_ready")
        pass_ready = sem("pass_ready")
        list_blank = sem("list_blank")
        list_made = sem("list_made")
        list_in = sem("list_in")
        gids_ready = sem("gids_ready")
        xe_zero = sem("xe_zero")
        out_stored = sem("out_stored")
        e_landed = [sem(f"e_landed{i}") for i in range(6)]
        eh_ready = [sem(f"eh_ready{r}") for r in range(3)]
        el_ready = [sem(f"el_ready{r}") for r in range(3)]
        e_used = sem("e_used")
        gi_made = [sem(f"gi_made{i}") for i in range(2)]
        si_made = [sem(f"si_made{i}") for i in range(2)]
        xe_landed = [sem(f"xe_landed{i}") for i in range(2)]
        xt_done = sem("xt_done")
        xeh_ready = sem("xeh_ready")
        xel_ready = sem("xel_ready")
        hid_ready = sem("hid_ready")
        silu_ready = sem("silu_ready")
        gated_ready = sem("gated_ready")
        at_done = sem("at_done")
        ah_ready = sem("ah_ready")
        al_ready = sem("al_ready")
        y_done = sem("y_done")
        ya_ready = sem("ya_ready")
        yv_ready = sem("yv_ready")
        y_stored = [sem(f"y_stored{i}") for i in range(2)]
        pool_waits = sem("pool_waits")
        sp_waits = sem("sp_waits")
        yr_in = [sem(f"yr_in{i}") for i in range(2)]
        y_sum = sem("y_sum")
        y_sq = sem("y_sq")
        y_ms = sem("y_ms")
        y_root = sem("y_root")
        y_out = sem("y_out")
        y_saved = [sem(f"y_saved{i}") for i in range(2)]
        fg_in = sem("fg_in")

        def raw_in(eng, key):
            c = AT[key]
            eng.wait_ge(landed[c % RAW], 16 * (c // RAW + 1))
            return raw[c % RAW]

        w2d = {k: a[k][0] for k in ("w_in", "w_out", "xa_wq", "xa_wk", "xa_wv", "xa_wo")}
        SOURCE = {"w_in": w2d["w_in"], "wk": w2d["xa_wk"], "wv": w2d["xa_wv"], "w_out": w2d["w_out"],
                  "wq": w2d["xa_wq"], "wo": w2d["xa_wo"]}
        w1 = a["exp_w1"][0].rearrange("g e (p k) f -> (g e) p k f", k=KT_D)
        w3 = a["exp_w3"][0].rearrange("g e (p k) f -> (g e) p k f", k=KT_D)
        w2 = a["exp_w2"][0].rearrange("g e (p k) f -> (g e) p (k f)", k=2)

        def vc_free(eng, s):
            if s < NS - 1:
                eng.wait_ge(vc_used, s + 1)
            else:
                eng.wait_ge(tv_ready, TV_AT["so"] + 1)

        block = ctx.enter_context(nc.Block())

        @block.sync
        def _(sp):
            def load(c):
                kind, i = STREAM[c]
                slot = raw[c % RAW]
                if c >= RAW:
                    was, wi = STREAM[c - RAW]
                    if was == "x":
                        sp.wait_ge(tv_ready, TV_AT[f"x{2 * wi + 1}"] + 1)
                        sp.wait_ge(ta_ready, TA_AT[f"x{2 * wi + 1}"] + 1)
                    elif was == "mem":
                        sp.wait_ge(tv_ready, TV_AT["mem3"] + 1)
                        sp.wait_ge(mem_sq, 2)
                    elif was == "kc":
                        sp.wait_ge(tv_used, TV_AT[f"qb{wi}1"] + 1)
                    elif was == "vc":
                        vc_free(sp, wi)
                    else:
                        sp.wait_ge(l_ready, W_AT[(was, wi)] + 1)
                if kind == "x":
                    src = a["x_prompt"][0].rearrange("(c t p) d -> c p t d", c=2, p=P)[i]
                elif kind == "mem":
                    src = a["mem_prompt"][0].rearrange("(t p) d -> p t d", p=P)
                elif kind in ("kc", "vc"):
                    src = a["cache_mem_k" if kind == "kc" else "cache_mem_v"][0, i].rearrange(
                        "(t p) h d -> p t (h d)", p=P)
                else:
                    col = W_IN_COLS[i] if kind == "w_in" else 256 * i
                    src = SOURCE[kind][:, col:col + 256].rearrange("(k p) n -> p k n", p=P)
                w = src.shape[2]
                sp.dma_start(slot[:].rearrange("p (t w) -> p t w", w=w), src).then_inc(landed[c % RAW], 16)

            for c in range(len(STREAM)):
                load(c)
                if c == 1:
                    sp.dma_start(conv_sample[0, :, 0:PAST - 1, :], a["cache_conv"][0, :, 1:PAST, :]).then_inc(out_stored, 16)
                if c == 16:
                    sp.wait_ge(ta_used, TA_AT["tail"] + 1)
                    sp.dma_start(conv_prompt[0, 0], tail[0:PAST, :]).then_inc(tail_stored, 16)
                    sp.dma_start(conv_sample[0, :, PAST - 1, :], tail[PAST:PAST + NS, :]).then_inc(tail_stored, 16)
                if c == 18:
                    sp.wait_ge(v_ready, NT)
                    sp.dma_start(gmv_prompt[0, 0], v_tok[:, 3, :]).then_inc(gmv_stored, 16)
                    sp.dma_start(gmv_sample[0, :, 0, :], v_s[0:NS, :]).then_inc(gmv_stored, 16)
                if 19 <= c < 23:
                    h = c - 19
                    sp.wait_ge(mm_used, MM_AT[("wk", 2 * h + 1)] + 1)
                    sp.dma_start(mem_k_out[0, 0, :, h, :].rearrange("(t p) d -> p t d", p=P),
                                 zt[h % 2][:, 0:2 * XH_DIM].rearrange("p (t d) -> p t d", t=2)).then_inc(k_stored[h % 2], 16)
                if c == 24:
                    sp.wait_ge(mm_used, MM_AT[("wv", 7)] + 1)
                    sp.dma_start(mem_v_out[0, 0].rearrange("(t p) h d -> p t (h d)", p=P), vm[:]).then_inc(vm_stored, 16)

            def wait(s, value):
                sp.wait_ge(s, value)
                sp.sem_inc(sp_waits, 1)

            def load_expert(q, e, j, first):
                for r in range(3):
                    m = 3 * j + r
                    if first:
                        if m < RAW:
                            was, wi = STREAM[len(STREAM) - RAW + m]
                            if was == "vc":
                                vc_free(sp, wi)
                            else:
                                sp.wait_ge(l_ready, W_AT[(was, wi)] + 1)
                        else:
                            sp.wait_ge(mm_ready, len(MM_ORDER))
                    else:
                        wait(el_ready[r], q - 1)
                    if r < 2:
                        dst = raw_e[m][:].rearrange("p (k w f) -> p k w f", k=4, w=2)
                        for n, src in enumerate((w1, w3)):
                            sp.dma_start(dst[:, :, n, :], src[bass.ds(e, 1), :, 4 * r:4 * r + 4, :].rearrange(
                                "o p k f -> p (o k) f")).then_inc(e_landed[m], 16)
                    else:
                        sp.dma_start(raw_e[m][:].rearrange("p (o f) -> p o f", o=1),
                                     w2[bass.ds(e, 1)].rearrange("o p f -> p o f")).then_inc(e_landed[m], 16)

            for j in range(2):
                load_expert(j, j, j, True)
            sp.wait_ge(pass_ready, 1)
            extra = sp.value_load(more[0:1, 0:1], min_val=0, max_val=LIST_ROWS // P - 1)
            with sp.Fori(1, extra * (EXPERTS // 2) + EXPERTS // 2) as it:
                for j in range(2):
                    load_expert(2 * it + j, (2 * it + j) & (EXPERTS - 1), j, False)

            def store_y(sp, t):
                t0, n = TILES[t]
                sp.wait_ge(y_out, t + 1)
                dst = y_prompt[0, t0:t0 + n, :] if t < 4 else y_sample[:, 0, :]
                sp.dma_start(dst, yo[t % 2][0:n]).then_inc(y_saved[t % 2], 16)

            for i in range(2):
                wait(y_stored[i], extra * (EXPERTS // 2 * 16) + (EXPERTS // 2 + i) * 16)
            rows = y_rows.rearrange("(t k) d -> t k d", k=2)
            for t, (t0, n) in enumerate(TILES):
                if t >= 2:
                    sp.wait_ge(y_sum, t - 1)
                sp.dma_start(yr[t % 2][0:n], rows[t0:t0 + n]).then_inc(yr_in[t % 2], 16)
                if t >= 1:
                    store_y(sp, t - 1)
            store_y(sp, NT - 1)
            sp.wait_ge(y_saved[0], 16 * 3)
            sp.wait_ge(y_saved[1], 16 * 2)
            sp.wait_ge(out_stored, 16)
            sp.wait_ge(tail_stored, 32)
            sp.wait_ge(gmv_stored, 32)
            sp.wait_ge(vm_stored, 16)
            for i in range(2):
                sp.wait_ge(k_stored[i], 32)

        @block.scalar
        def _(act):
            for name, key in (("mix_g", "norm_mix_g"), ("mem_g", "norm_mem_g"), ("xa_g", "norm_xa_g"),
                              ("ffn_g", "norm_ffn_g"), ("conv_b", "conv_b"), ("cv_g", "cv_ln_g"), ("cv_b", "cv_ln_b")):
                src = a[key][0].rearrange("(r p) -> r p", p=P)
                act.dma_start(rows_a[ROWS_A[name]:ROWS_A[name] + src.shape[0], :], src).then_inc(params_in, 16)
            act.dma_start(rows_b[:], a["conv_w"][0].rearrange("k (i p) -> (k i) p", p=P)).then_inc(params_in, 16)
            act.dma_start(xs_rows[:], a["x_sample"][:, 0, :]).then_inc(params_in, 16)
            act.dma_start(ws_rows[:], a["gm_ws"][0].rearrange("h i j -> i h j")).then_inc(rows_in, 16)
            act.dma_start(cache_rows[:], a["cache_conv"][0].rearrange("(c s) k w -> (s k) c w", c=2)).then_inc(rows_in, 16)
            for dst, src in ((bs_all[:], a["gm_bs"]), (ln_g[:].rearrange("p (h c) -> p h c", h=HEADS), a["gm_ln_g"]),
                             (ln_b[:].rearrange("p (h c) -> p h c", h=HEADS), a["gm_ln_b"])):
                act.dma_start(dst, src[0:1].broadcast_to([P, HEADS, P])).then_inc(consts_in, 16)
            act.dma_start(ws00[:], a["gm_ws"][0:1, :, 0, 0].broadcast_to([P, HEADS]),
                          allow_slow_non_contiguous=True).then_inc(consts_in, 16)

            ta_n = [0]

            def take(name):
                assert TA_ORDER[ta_n[0]] == name
                ta_n[0] += 1
                act.wait_ge(ta_ready, ta_n[0])
                return ta[(ta_n[0] - 1) % 2]

            def split_h(n):
                slot = raw_in(act, WEIGHTS[n])
                if n >= 2:
                    act.wait_ge(mm_ready, mm_after(n - 2))
                act.activation(w_h[n % 2][:], slot[:], ACT.Copy).then_inc(h_ready, 1)

            def square(k, n0):
                if n0 + k >= 2:
                    act.wait_ge(sq_added, n0 + k - 1)
                act.activation(zt[k % 2][:], xT[:, k, :], ACT.Square).then_inc(sq_ready, 1)

            def root(n):
                act.wait_ge(tv_used, TV_AT[f"rs{2 * n + 1}"] + 1)
                act.activation(rstd[:], rstd[:], ACT.Sqrt).then_inc(rs_root, 1)

            def products(n0, n1):
                for n in range(n0, n1):
                    i, k = 1 + 2 * (n // TAPS), n % TAPS
                    src = glu[:, i, k:k + SEQ]
                    w = cols_b[:, k, i:i + 1]
                    if k == 0:
                        act.wait_ge(glu_ready, i + 1)
                        b = ROWS_A["conv_b"] + i
                        ins = act.activation(conv[:, i, 0:SEQ], src, ACT.Identity, bias=cols_a[:, b:b + 1], scale=w)
                    else:
                        p = n - n // TAPS - 1
                        if p >= 4:
                            act.wait_ge(conv_p, p - 3)
                        ins = act.activation(scaled[p % 4][:], src, ACT.Copy, scale=w)
                    ins.then_inc(tap_scaled, 1)

            for j, (t0, n) in enumerate(TILES):
                src = take(f"x{j}")
                act.activation(xT[:, 4:8, t0:t0 + n], src.rearrange("p (k t) -> p k t", k=4)[:, :, 0:n],
                               ACT.Copy).then_inc(ta_used, 1)
            split_h(0)
            act.wait_ge(tv_used, TV_AT[f"x{NT - 1}"] + 1)
            act.wait_ge(ta_used, NT)
            for k in range(8):
                act.activation(xH[:, k, :], xT[:, k, :], ACT.Copy,
                               scale=cols_a[:, ROWS_A["mix_g"] + k:ROWS_A["mix_g"] + k + 1]).then_inc(xh_ready, 1)
            for k in range(8):
                square(k, 0)
            split_h(1)
            root(0)

            for n in range(8):
                if n >= 1:
                    split_h(n + 1)
                for m in (2 * n, 2 * n + 1):
                    if m in (2, 3, 6, 7):
                        g = {2: 0, 3: 1, 6: 2, 7: 3}[m]
                        act.wait_ge(mm_used, MM_AT[("w_in", m)] + 1)
                        act.activation(zt[g % 2][:], zt[g % 2][:], ACT.Sigmoid).then_inc(z_act, 1)
                    if m >= 8:
                        i = m - 8
                        act.wait_ge(mm_used, MM_AT[("w_in", m)] + 1)
                        dst = v_raw[:, i, :] if i < 4 else u_act[:, i - 4, :]
                        act.activation(dst, zt[i % 2][:], ACT.Gelu_apprx_tanh).then_inc(z_act, 1)
                    if m == 10:
                        src = take("tail")
                        act.activation(tail[:], src[0:PAST + NS, 0:GM], ACT.Copy).then_inc(ta_used, 1)
                    if 4 <= m < 12:
                        products(6 * (m - 4), 6 * (m - 3))

            act.wait_ge(v_mean, 1)
            act.activation(mv[:, :, :, 1], mv[:, :, :, 1], ACT.Sqrt).then_inc(v_root, 1)
            slot = raw_in(act, ("mem", 0))
            for t in range(2):
                if t:
                    act.wait_ge(mem_sq, 1)
                act.activation(mem_junk[:], slot[:, t * D:(t + 1) * D], ACT.Square,
                               accum_out=m_ss[:, t:t + 1]).then_inc(mem_sq, 1)
            act.wait_ge(m_mean, 1)
            act.activation(m_ss[:], m_ss[:], ACT.Sqrt).then_inc(m_root, 1)
            for i in range(4):
                act.wait_ge(tv_ready, TV_AT[f"mem{i}"] + 1)
                src = tv[TV_AT[f"mem{i}"] % 2].rearrange("p (k t) -> p k t", k=2)
                for kk in range(2):
                    k = 2 * i + kk
                    act.activation(xH[:, k, 0:MEM], src[:, kk, :], ACT.Copy,
                                   scale=cols_a[:, ROWS_A["mem_g"] + k:ROWS_A["mem_g"] + k + 1]).then_inc(xh_ready, 1)

            for n in range(8, 16):
                split_h(n + 1)
                if n == 10:
                    act.wait_ge(gmv_stored, 32)
                    act.wait_ge(tv_ready, TV_AT["mix3"] + 1)
                if 10 <= n < 15:
                    products(min(48 + 3 * (n - 10), 2 * TAPS), min(48 + 3 * (n - 9), 2 * TAPS))
                if n == 9:
                    for h in range(4):
                        act.wait_ge(a_ready, h + 1)
                        act.activation(cH[:, h, :], cLf[:, h, :], ACT.Copy).then_inc(xh_ready, 1)
            act.wait_ge(c_mean, 1)
            act.activation(mv[:, :, 0, 1], mv[:, :, 0, 1], ACT.Sqrt).then_inc(c_root, 1)
            for j, (t0, n) in enumerate(TILES):
                src = take(f"cb{j}")
                for i in range(4):
                    last = act.activation(conv[:, i, t0:t0 + n], src[:, i * P:i * P + n], ACT.Silu,
                                          scale=cols_a[:, ROWS_A["cv_g"] + i:ROWS_A["cv_g"] + i + 1],
                                          bias=cols_a[:, ROWS_A["cv_b"] + i:ROWS_A["cv_b"] + i + 1])
                last.then_inc(ta_used, 1)
            act.wait_ge(ta_used, TA_AT[f"cb{NT - 1}"] + 1)
            for i in range(4):
                act.activation(cH[:, 4 + i, :], conv[:, i, :], ACT.Copy).then_inc(xh_ready, 1)

            act.dma_start(router[:, :, 0:NG], a["router_g"][0].rearrange("(k p) g -> p k g", p=P)).then_inc(r_w_in, 16)
            act.dma_start(router[:, :, NG:], a["router_e"][0].rearrange("(k p) g e -> p k (g e)", p=P)).then_inc(r_w_in, 16)
            for n in range(16, 20):
                split_h(n + 1)
                for k in (2 * (n - 16), 2 * (n - 16) + 1):
                    act.wait_ge(mm_used, MM_AT[("w_out", k)] + 1)
                    act.activation(xH[:, k, :], xT[:, k, :], ACT.Copy,
                                   scale=cols_a[:, ROWS_A["xa_g"] + k:ROWS_A["xa_g"] + k + 1]).then_inc(xh_ready, 1)
                    if k == 0:
                        for i in range(2):
                            act.wait_ge(k_stored[i], 32)
                    square(k, 8)
            root(1)
            for n in range(20, 24):
                split_h(n + 1)
            split_h(25)
            for b in range(2):
                src = take(f"qs{b}")
                act.activation(q_s[:, 512 * b:512 * b + 512], src[0:NS, :], ACT.Copy).then_inc(ta_used, 1)
            for j in range(4 + 1):
                if j < 4:
                    act.wait_ge(p_max, j + 1)
                    if j >= 2:
                        act.wait_ge(ta_ready, TA_AT[f"pt{j - 2}1"] + 1)
                    src = mm[MM_AT[("score", j)] % 2]
                    for h in range(HEADS):
                        last = act.activation(probs[j % 2][:, h, :], src[:, h // 2, (h % 2) * MEM:(h % 2 + 1) * MEM],
                                              ACT.Exp, bias=pmax[:, j, h:h + 1], scale=SCALE,
                                              accum_out=psum_p[:, j, h:h + 1])
                    last.then_inc(mm_used, 1)
                if j >= 1:
                    for b in range(2):
                        src = take(f"pt{j - 1}{b}").rearrange("p (h t w) -> p h t w", h=2, t=2)
                        act.activation(pT[:, 2 * b:2 * b + 2, :, (j - 1) * P:j * P], src, ACT.Copy).then_inc(ta_used, 1)
            act.wait_ge(s_max, 1)
            act.activation(s_p[:], s_p[:], ACT.Exp, bias=s_mx[0:NS * HEADS, 1:2], scale=SCALE,
                           accum_out=s_mx[0:NS * HEADS, 2:3]).then_inc(s_exp, 1)
            for h in range(4):
                m = MM_AT[("pv", h)]
                act.wait_ge(mm_ready, m + 1)
                act.activation(xH[:, 2 * h:2 * h + 2, 0:SEQ], mm[m % 2][:], ACT.Copy).then_inc(oh_ready, 1)
            act.wait_ge(tv_ready, TV_AT["so"] + 1)
            act.dma_start(ffn_g[:], a["norm_ffn_g"][0:1, :].broadcast_to([P, D])).then_inc(r_in, 16)
            act.dma_start(fin_g[:], a["final_norm_g"].rearrange("(o d) -> o d", o=1).broadcast_to([P, D])).then_inc(r_in, 16)
            act.dma_start(r_bias[:, 0:NG], a["router_g_b"][0:1, :].broadcast_to([P, NG])).then_inc(r_in, 16)
            act.dma_start(r_bias[:, NG:], a["router_e_b"][0:1].rearrange("o g e -> o (g e)").broadcast_to(
                [P, EXPERTS])).then_inc(r_in, 16)
            act.activation(xH[:, :, SEQ:T], tv[TV_AT["so"] % 2][:, 0:8 * NS].rearrange("p (k s) -> p k s", k=8),
                           ACT.Copy).then_inc(oh_ready, 1)
            for n in range(24, 28):
                if 24 < n < 27:
                    split_h(n + 1)
                for k in (2 * (n - 24), 2 * (n - 24) + 1):
                    act.wait_ge(mm_used, MM_AT[("wo", k)] + 1)
                    square(k, 16)
            act.wait_ge(tv_used, TV_AT["r2"] + 1)
            act.activation(rs5[:], rs5[:], ACT.Sqrt).then_inc(r_root, 1)
            for j, (t0, n) in enumerate(TILES):
                src = take(f"t{j}")
                act.activation(x2[0:n, j, 512:D], src[0:n, :], ACT.Copy).then_inc(ta_used, 1)
                if j == 1:
                    act.wait_ge(g_dif, 1)
                    act.activation(g_ex[:], g_ex[:], ACT.Exp).then_inc(g_exp, 1)
                    act.wait_ge(g_dif, 2)
                    act.activation(w_ex[:, 0, :], w_ex[:, 0, :], ACT.Exp).then_inc(g_exp, 1)

            def split_e(q, it, j, r, free):
                act.wait_ge(e_landed[3 * j + r], (it + 1) * (16 * (2 if r < 2 else 1)))
                if free:
                    act.wait_ge((e_used, hid_ready, y_done)[r], q)
                act.activation(e_h[r][:], raw_e[3 * j + r][:], ACT.Copy).then_inc(eh_ready[r], 1)

            def columns_h(q):
                act.wait_ge(xt_done, q + 1)
                for b in range(2):
                    last = act.activation(xeH[:, 4 * b:4 * b + 4, :], tv[b].rearrange("p (k t) -> p k t", k=4), ACT.Copy)
                last.then_inc(xeh_ready, 1)

            def act_h(q, old=True):
                act.wait_ge(at_done, q + 1)
                if old:
                    act.wait_ge(y_done, q)
                act.activation(aH[:], ta[0][:, 0:2 * P].rearrange("p (k t) -> p k t", k=2), ACT.Copy).then_inc(ah_ready, 1)

            def y_left(q, j, it, stored):
                act.wait_ge(y_done, q + 1)
                if stored:
                    act.wait_ge(y_stored[j], (it + j) * 16)
                act.activation(ye[j][:, 0:512], mm[1][:, 0, :], ACT.Copy).then_inc(ya_ready, 1)

            def step(q, it, j, first, last):
                prev = (q - 1, 1 - j, it if j else it - 1)
                if not (first and j == 0):
                    act_h(prev[0], not (first and j == 1))
                if not (last and j == 1):
                    for r in range(2):
                        split_e(q + 1, it if j == 0 else it + 1, 1 - j, r, True)
                act.wait_ge(hid_ready, q + 1)
                if not (first and j == 0):
                    act.wait_ge(gated_ready, q)
                act.activation(silu[:], mm[0][:, j, 0:FF], ACT.Silu).then_inc(silu_ready, 1)
                if not (last and j == 1):
                    columns_h(q + 1)
                if not (first and j == 0):
                    y_left(prev[0], prev[1], prev[2], not first)
                if first and j == 0:
                    act.wait_ge(vm_stored, 16)
                split_e(q, it, j, 2, not (first and j == 0))

            for r in range(2):
                if r == 0:
                    act.wait_ge(mm_ready, len(MM_ORDER))
                split_e(0, 0, 0, r, False)
            columns_h(0)
            for j in range(2):
                step(j, 0, j, True, False)
            act.wait_ge(pass_ready, 1)
            extra = act.value_load(more[0:1, 0:1], min_val=0, max_val=LIST_ROWS // P - 1)
            last_it = extra * (EXPERTS // 2) + (EXPERTS // 2 - 1)
            with act.Fori(1, last_it) as it:
                for j in range(2):
                    step(it * 2 + j, it, j, False, False)
            for j in range(2):
                step(last_it * 2 + j, last_it, j, False, True)
            act_h(last_it * 2 + 1)
            y_left(last_it * 2 + 1, 1, last_it, True)

            for t, (t0, n) in enumerate(TILES):
                act.wait_ge(y_sum, t + 1)
                if t:
                    act.wait_ge(y_sq, t)
                act.activation(sq_junk[0:n], x2[0:n, t, :], ACT.Square, accum_out=fin_ss[0:n, t:t + 1]).then_inc(y_sq, 1)
                act.wait_ge(y_ms, t + 1)
                act.activation(fin_ss[0:n, t:t + 1], fin_ss[0:n, t:t + 1], ACT.Sqrt).then_inc(y_root, 1)

        @block.vector
        def _(dve):
            own_n = [0]

            def link(ins):
                own_n[0] += 1
                ins.then_inc(own, 1)
                dve.wait_ge(own, own_n[0])

            tv_n = [0]

            def take(name):
                assert TV_ORDER[tv_n[0]] == name, (name, TV_ORDER[tv_n[0]])
                tv_n[0] += 1
                dve.wait_ge(tv_ready, tv_n[0])
                return tv[(tv_n[0] - 1) % 2]

            def split_l(n):
                dve.wait_ge(h_ready, n + 1)
                slot = raw_in(dve, WEIGHTS[n])
                if n >= 2:
                    dve.wait_ge(mm_ready, mm_after(n - 2))
                dve.tensor_tensor(w_l[n % 2][:], slot[:], w_h[n % 2][:].bitcast(F32), ALU.subtract).then_inc(l_ready, 1)

            def mm_take(key):
                m = MM_AT[key]
                dve.wait_ge(mm_ready, m + 1)
                return mm[m % 2]

            def mean(n):
                for b in range(2):
                    src = take(f"rs{2 * n + b}")
                    dve.tensor_scalar(rstd[:, b, :], src[:, 0:HT], 1.0 / D, EPS, ALU.mult, ALU.add).then_inc(tv_used, 1)
                dve.wait_ge(rs_root, n + 1)
                dve.reciprocal(rstd[:], rstd[:]).then_inc(rs_ready, 1)
                dve.wait_ge(rs_ready, n + 1)

            dve.memset(ones[:], 1.0).then_inc(dve_made, 1)
            dve.memset(mv[:], 1.0).then_inc(dve_made, 1)
            dve.memset(rs5[:], 1.0).then_inc(dve_made, 1)
            src = take("cols_a")
            dve.tensor_copy(cols_a[:], src[:, 0:N_ROWS_A]).then_inc(tv_used, 1)
            src = take("cols_b")
            dve.tensor_copy(cols_b[:].rearrange("p k i -> p (k i)"), src[:, 0:N_ROWS_B]).then_inc(tv_used, 1)
            dve.memset(glu[:, :, 0:PAST], 0.0).then_inc(dve_made, 1)
            for j, (t0, n) in enumerate(TILES):
                src = take(f"x{j}")
                dve.tensor_copy(xT[:, 0:4, t0:t0 + n],
                                src.rearrange("p (k t) -> p k t", k=4)[:, :, 0:n]).then_inc(tv_used, 1)
            split_l(0)
            dve.wait_ge(tv_used, TV_AT[f"x{NT - 1}"] + 1)
            dve.wait_ge(ta_used, NT)

            def moving_l(k, n_h, row):
                dve.wait_ge(xh_ready, n_h)
                g = ROWS_A[row] + k
                dve.scalar_tensor_tensor(xL[:, k, :], xT[:, k, :], cols_a[:, g:g + 1], xH[:, k, :].bitcast(F32),
                                         ALU.mult, ALU.subtract).then_inc(xl_ready, 1)

            for k in range(8):
                moving_l(k, k + 1, "mix_g")
            split_l(1)
            mean(0)

            def taps(first, last):
                for n in range(first, min(last, 2 * TAPS)):
                    i, k = 2 * (n // TAPS), n % TAPS
                    w = cols_b[:, k, i:i + 1]
                    src = glu[:, i, k:k + SEQ]
                    if k == 0:
                        dve.wait_ge(glu_ready, i + 1)
                        b = ROWS_A["conv_b"] + i
                        ins = dve.tensor_scalar(conv[:, i, 0:SEQ], src, w, cols_a[:, b:b + 1], ALU.mult, ALU.add)
                    else:
                        dve.wait_ge(conv_v, n)
                        ins = dve.scalar_tensor_tensor(conv[:, i, 0:SEQ], src, w, conv[:, i, 0:SEQ], ALU.mult, ALU.add)
                    ins.then_inc(conv_v, 1)

            def samples_conv(i):
                w = cols_b[:, :, i].rearrange("p (o k) -> p o k", o=1).broadcast_to([P, NS, TAPS])
                link(dve.tensor_copy(conv_s[:, i, :, PAST], glu[:, i, PAST + SEQ:PAST + T]))
                link(dve.tensor_tensor(conv_s[:, i], conv_s[:, i], w, ALU.mult))
                link(dve.tensor_reduce(conv[:, i, SEQ:T], conv_s[:, i], AX_X, ALU.add))
                b = ROWS_A["conv_b"] + i
                dve.tensor_scalar(conv[:, i, SEQ:T], conv[:, i, SEQ:T], cols_a[:, b:b + 1], None, ALU.add).then_inc(convs_done, 1)

            def gate(g):
                dve.wait_ge(z_act, g + 1)
                dve.wait_ge(mm_used, MM_AT[("w_in", LINEAR[g])] + 1)
                dve.tensor_tensor(glu[:, g, PAST:PAST + T], glu[:, g, PAST:PAST + T], zt[g % 2][:],
                                  ALU.mult).then_inc(glu_ready, 1)

            LINEAR, GATES = (0, 1, 4, 5), (2, 3, 6, 7)

            for n in range(8):
                if n >= 1:
                    split_l(n + 1)
                for m in (2 * n, 2 * n + 1):
                    src = mm_take(("w_in", m))[:, :, 0:HT]
                    if m in LINEAR:
                        if m == 0:
                            dve.wait_ge(dve_made, 4)
                        dst = glu[:, LINEAR.index(m), PAST:PAST + T]
                    else:
                        c = GATES.index(m) if m in GATES else m - 4
                        if 2 <= c < 6:
                            dve.wait_ge(glu_ready, c - 1)
                        if c >= 6:
                            dve.wait_ge(z_act, c - 1)
                        dst = zt[c % 2][:]
                    dve.tensor_tensor(dst.rearrange("p (b t) -> p b t", b=2), src, rstd[:], ALU.mult).then_inc(mm_used, 1)
                    if m - 1 in GATES:
                        gate(GATES.index(m - 1))
                    if m == 1:
                        src = take("ws")
                        dve.wait_ge(consts_in, 16 * 4)
                        dve.tensor_copy(wsT[:].rearrange("p h i -> p (h i)"), src).then_inc(tv_used, 1)
                        for c in range(2):
                            src = take(f"cc{c}")
                            dve.tensor_copy(conv_s[:, :, 4 * c:4 * c + 4, 0:PAST],
                                            src[:, 0:16 * PAST].rearrange("p (i s k) -> p i s k", i=4, s=4)).then_inc(tv_used, 1)
                    if m >= 5:
                        taps(3 * (m - 5), 3 * (m - 4))
                    if m >= 12:
                        for j in ((0, 1), (2, 3), (4,), ())[m - 12]:
                            t0, n_t = TILES[j]
                            src = take(f"v{j}")[0:n_t]
                            if j == 0:
                                dve.wait_ge(conv_p, 46)
                            dve.tensor_copy(v_tok[:, j, :] if j < 4 else v_s[0:n_t], src)
                            for h in range(HEADS):
                                last = dve.bn_stats(stats[0:n_t, j, h, :], src[:, h * P:(h + 1) * P])
                            last.then_inc(tv_used, 1)
                            dve.wait_ge(tv_used, TV_AT[f"v{j}"] + 1)
                            for h in range(HEADS):
                                last = dve.bn_aggr(mv[0:n_t, j, h, :], stats[0:n_t, j, h, :])
                            link(last)
            dve.tensor_scalar(mv[:, :, :, 1], mv[:, :, :, 1], EPS, None, ALU.add).then_inc(v_mean, 1)
            dve.wait_ge(v_root, 1)
            link(dve.reciprocal(mv[:, :, :, 1], mv[:, :, :, 1]))
            for j, (t0, n_t) in enumerate(TILES):
                for h in range(HEADS):
                    row = (v_tok[:, j, :] if j < 4 else v_s[0:n_t])[:, h * P:(h + 1) * P]
                    last = dve.tensor_scalar(row, row, mv[0:n_t, j, h, 0:1], mv[0:n_t, j, h, 1:2], ALU.subtract, ALU.mult)
                last.then_inc(v_norm, 1)

            dve.wait_ge(mem_sq, 2)
            dve.tensor_scalar(m_ss[:], m_ss[:], 1.0 / D, EPS, ALU.mult, ALU.add).then_inc(m_mean, 1)
            for i in range(4):
                src = take(f"mem{i}").rearrange("p (k t) -> p k t", k=2)
                for kk in range(2):
                    k = 2 * i + kk
                    dve.wait_ge(xh_ready, 8 + 2 * i + 2)
                    g = ROWS_A["mem_g"] + k
                    last = dve.scalar_tensor_tensor(xL[:, k, 0:MEM], src[:, kk, :], cols_a[:, g:g + 1],
                                                    xH[:, k, 0:MEM].bitcast(F32), ALU.mult, ALU.subtract)
                last.then_inc(tv_used, 1)
            dve.wait_ge(m_root, 1)
            link(dve.reciprocal(m_ss[:], m_ss[:]))

            def keys_in(h):
                src = take(f"kt{h}")
                if h == 0:
                    dve.wait_ge(tail_stored, 32)
                dve.tensor_copy(kT[:, 2 * h:2 * h + 2, :], src.rearrange("p (k t) -> p k t", k=2)).then_inc(tv_used, 1)

            def gated_mix(h):
                src = take(f"mix{h}")
                bias = bs_all[:, h:h + 1, :].broadcast_to([P, 4, P])
                tmp = sumsq[:, 0:SEQ]
                dve.tensor_tensor(tmp.rearrange("p (c t) -> p c t", c=4), src.rearrange("p (c t) -> p c t", c=4),
                                  bias, ALU.add).then_inc(tv_used, 1)
                dve.wait_ge(tv_used, TV_AT[f"mix{h}"] + 1)
                dve.wait_ge(z_act, 8 + h + 1)
                link(dve.tensor_tensor(u_act[:, h, 0:SEQ], u_act[:, h, 0:SEQ], tmp, ALU.mult))
                dve.tensor_tensor(u_act[:, h, SEQ:T], u_act[:, h, SEQ:T], vsT[:, h, :], ALU.mult).then_inc(a_ready, 1)

            for n in range(8, 16):
                split_l(n + 1)
                for t in range(2):
                    m = 2 * (n - 8) + t
                    if n < 12:
                        h = n - 8
                        src = mm_take(("wk", m))
                        if h >= 2 and t == 0:
                            dve.wait_ge(k_stored[h % 2], 16)
                            dve.wait_ge(tv_ready, TV_AT[f"kt{h - 2}"] + 1)
                        dst = zt[h % 2][:, t * XH_DIM:(t + 1) * XH_DIM]
                    else:
                        src = mm_take(("wv", m - 8))
                        h = n - 12
                        dst = vm[:, t, h * XH_DIM:(h + 1) * XH_DIM]
                        if m == 8:
                            dve.wait_ge(list_blank, 16)
                            dve.wait_ge(y_stored[1], 16)
                    dve.tensor_scalar(dst, src[:, 0, 0:MEM], m_ss[:, t:t + 1], None, ALU.mult).then_inc(mm_used, 1)
                    taps(33 + 2 * m, 33 + 2 * m + 2)
                    if m < 4:
                        samples_conv(m)
                if n == 8:
                    src = take("vs")
                    for h in range(HEADS):
                        last = dve.tensor_scalar(vsT[:, h, :], src[:, h * NS:(h + 1) * NS], ws00[:, h:h + 1],
                                                 bs_all[:, h, 0:1], ALU.mult, ALU.add)
                    last.then_inc(tv_used, 1)
                    dve.wait_ge(tv_used, TV_AT["vs"] + 1)
                    for h in range(HEADS):
                        gated_mix(h)
                if n == 9:
                    for h in range(HEADS):
                        dve.wait_ge(xh_ready, 16 + h + 1)
                        dve.tensor_tensor(cL[:, h, :], cLf[:, h, :], cH[:, h, :].bitcast(F32), ALU.subtract).then_inc(xl_ready, 1)
                if 9 <= n < 13:
                    keys_in(n - 9)
            dve.wait_ge(gmv_stored, 32)
            for j, (t0, n_t) in enumerate(TILES):
                src = take(f"cf{j}")[0:n_t]
                dve.tensor_copy(v_tok[:, j, :] if j < 4 else v_s[0:n_t], src)
                dve.bn_stats(stats[0:n_t, j, 0, :], src).then_inc(tv_used, 1)
                dve.wait_ge(tv_used, TV_AT[f"cf{j}"] + 1)
                link(dve.bn_aggr(mv[0:n_t, j, 0, :], stats[0:n_t, j, 0, :]))
            dve.tensor_scalar(mv[:, :, 0, 1], mv[:, :, 0, 1], EPS, None, ALU.add).then_inc(c_mean, 1)
            dve.wait_ge(c_root, 1)
            link(dve.reciprocal(mv[:, :, 0, 1], mv[:, :, 0, 1]))
            for j, (t0, n_t) in enumerate(TILES):
                row = v_tok[:, j, :] if j < 4 else v_s[0:n_t]
                dve.tensor_scalar(row, row, mv[0:n_t, j, 0, 0:1], mv[0:n_t, j, 0, 1:2], ALU.subtract,
                                  ALU.mult).then_inc(cn_ready, 1)
            for i in range(4):
                dve.wait_ge(xh_ready, 20 + i + 1)
                dve.tensor_tensor(cL[:, 4 + i, :], conv[:, i, :], cH[:, 4 + i, :].bitcast(F32), ALU.subtract).then_inc(xl_ready, 1)

            for n in range(16, 20):
                split_l(n + 1)
                for k in (2 * (n - 16), 2 * (n - 16) + 1):
                    src = mm_take(("w_out", k))[:, :, 0:HT]
                    xk = xT[:, k, :].rearrange("p (b t) -> p b t", b=2)
                    dve.tensor_tensor(xk, src, xk, ALU.add).then_inc(mm_used, 1)
                    if k:
                        moving_l(k - 1, 24 + k, "xa_g")
            moving_l(7, 32, "xa_g")
            mean(1)
            dve.wait_ge(r_w_in, 32)
            fg = cols_a[:, ROWS_A["ffn_g"]:ROWS_A["ffn_g"] + 8].rearrange("p (k o) -> p k o", o=1).broadcast_to(
                [P, 8, NG + EXPERTS])
            dve.tensor_tensor(router[:], router[:], fg, ALU.mult).then_inc(rg_ready, 1)
            for n in range(20, 24):
                split_l(n + 1)
                for k in (2 * (n - 20), 2 * (n - 20) + 1):
                    src = mm_take(("wq", k))[:, :, 0:HT]
                    dve.tensor_tensor(qT[:, k, :].rearrange("p (b t) -> p b t", b=2), src, rstd[:], ALU.mult).then_inc(mm_used, 1)
            split_l(25)

            def score_max(j):
                src = mm_take(("score", j))
                link(dve.tensor_reduce(pmax[:, j, :], src[:].rearrange("p b (h m) -> p (b h) m", h=2), AX_X, ALU.max))
                dve.tensor_scalar(pmax[:, j, :], pmax[:, j, :], -SCALE, None, ALU.mult).then_inc(p_max, 1)

            def score_norm(j):
                dve.wait_ge(mm_used, MM_AT[("score", j)] + 1)
                link(dve.reciprocal(psum_p[:, j, :], psum_p[:, j, :]))
                for h in range(HEADS):
                    last = dve.tensor_scalar(probs[j % 2][:, h, :], probs[j % 2][:, h, :], psum_p[:, j, h:h + 1], None, ALU.mult)
                last.then_inc(p_ready, 1)

            def sample_scores(s):
                keys = raw_in(dve, ("kc", s))
                for b in range(2):
                    src = take(f"qb{s}{b}")
                    for h in (2 * b, 2 * b + 1):
                        for t in range(2):
                            if ttr_n[0]:
                                dve.wait_ge(ttr_done, ttr_n[0])
                            last = dve.tensor_tensor_reduce(
                                ttr_out[:], keys[:, t * D + h * XH_DIM:t * D + (h + 1) * XH_DIM],
                                src[:, (h % 2) * XH_DIM:(h % 2 + 1) * XH_DIM], 1.0, 0.0, ALU.mult, ALU.add,
                                s_sc[:, t, s * HEADS + h:s * HEADS + h + 1])
                            if (h, t) != (2 * b + 1, 1):
                                ttr_n[0] += 1
                                last.then_inc(ttr_done, 1)
                    last.then_inc(tv_used, 1)
                    dve.wait_ge(tv_used, TV_AT[f"qb{s}{b}"] + 1)

            ttr_n = [0]
            score_max(0)
            score_max(1)
            for j in range(4):
                score_norm(j)
                sample_scores(2 * j)
                sample_scores(2 * j + 1)
                if j < 2:
                    score_max(j + 2)
            R = NS * HEADS
            src = take("ss")
            dve.tensor_reduce(s_mx[0:R, 0:1], src[0:R, 0:MEM], AX_X, ALU.max)
            dve.tensor_copy(s_p[:], src[0:R, 0:MEM]).then_inc(tv_used, 1)
            dve.wait_ge(tv_used, TV_AT["ss"] + 1)
            dve.tensor_scalar(s_mx[0:R, 1:2], s_mx[0:R, 0:1], -SCALE, None, ALU.mult).then_inc(s_max, 1)
            dve.wait_ge(s_exp, 1)
            link(dve.reciprocal(s_mx[0:R, 3:4], s_mx[0:R, 2:3]))
            dve.tensor_scalar(s_p[:], s_p[:], s_mx[0:R, 3:4], None, ALU.mult).then_inc(s_norm, 1)
            src = take("sp")
            dve.tensor_copy(s_pT[:].rearrange("p t r -> p (t r)"), src[:, 0:2 * R]).then_inc(tv_used, 1)
            for h in range(HEADS):
                m = MM_AT[("pv", h)]
                dve.wait_ge(oh_ready, h + 1)
                dve.tensor_tensor(xL[:, 2 * h:2 * h + 2, 0:SEQ], mm[m % 2][:], xH[:, 2 * h:2 * h + 2, 0:SEQ].bitcast(F32),
                                  ALU.subtract).then_inc(mm_used, 1)
            src = take("so")[:, 0:8 * NS].rearrange("p (k s) -> p k s", k=8)
            dve.wait_ge(oh_ready, 5)
            dve.tensor_tensor(xL[:, :, SEQ:T], src, xH[:, :, SEQ:T].bitcast(F32), ALU.subtract).then_inc(tv_used, 1)
            for n in range(24, 28):
                if 24 < n < 27:
                    split_l(n + 1)
                for k in (2 * (n - 24), 2 * (n - 24) + 1):
                    src = mm_take(("wo", k))[:, :, 0:HT]
                    xk = xT[:, k, :].rearrange("p (b t) -> p b t", b=2)
                    dve.tensor_tensor(xk, src, xk, ALU.add).then_inc(mm_used, 1)
            src = take("r2")
            dve.tensor_scalar(rs5[:, 0:4], src[:, 0:4], 1.0 / D, EPS, ALU.mult, ALU.add)
            dve.tensor_scalar(rs5[0:NS, 4:5], src[0:NS, 4:5], 1.0 / D, EPS, ALU.mult, ALU.add).then_inc(tv_used, 1)
            link(dve.memset(logits[:], 0.0))
            dve.wait_ge(r_root, 1)
            link(dve.reciprocal(rs5[:], rs5[:]))
            dve.wait_ge(r_in, 16 * 4)
            W = NG + EXPERTS
            src = take("lg")
            for j, (t0, n_t) in enumerate(TILES):
                last = dve.scalar_tensor_tensor(logits[0:n_t, j, :], src[0:n_t, j * W:(j + 1) * W], rs5[0:n_t, j:j + 1],
                                                r_bias[0:n_t], ALU.mult, ALU.add)
            last.then_inc(tv_used, 1)
            dve.wait_ge(tv_used, TV_AT["lg"] + 1)
            def over(x, w):
                return x.rearrange("p (t o) -> p t o", o=1).broadcast_to([P, NT, w])

            g_log = logits[:, :, 0:NG]
            link(dve.tensor_reduce(g_max[:], g_log, AX_X, ALU.max))
            dve.tensor_tensor(g_ex[:], g_log, over(g_max[:], NG), ALU.subtract).then_inc(g_dif, 1)

            def first_of(out, values, largest, tmp, w):
                dve.wait_ge(route_made, 3)
                pr = prio[:, 8 - w:8].rearrange("p (o w) -> p o w", o=1).broadcast_to([P, NT, w])
                link(dve.tensor_tensor(tmp, values, over(largest, w), ALU.is_equal))
                link(dve.tensor_tensor(tmp, tmp, pr, ALU.mult))
                link(dve.tensor_reduce(e_m[:], tmp, AX_X, ALU.max))
                link(dve.tensor_tensor(out, tmp, over(e_m[:], w), ALU.is_equal))

            first_of(g_sel[:], g_log, g_max[:], e_tmp[:, :, 0:NG], NG)
            e_log = logits[:, :, NG:].rearrange("p t (g e) -> p t g e", g=NG)
            sel4 = g_sel[:].rearrange("p t (g o) -> p t g o", o=1).broadcast_to([P, NT, NG, NE])
            for j in range(NT):
                last = dve.tensor_tensor(e_all[:, j], e_log[:, j], sel4[:, j], ALU.mult)
            link(last)
            link(dve.tensor_reduce(e_sel[:], e_all[:].rearrange("p t g e -> p t e g"), AX_X, ALU.add))
            link(dve.tensor_reduce(e_max[:, 0, :], e_sel[:], AX_X, ALU.max))
            first_of(e_one[:, 0], e_sel[:], e_max[:, 0, :], e_tmp[:], NE)
            link(dve.scalar_tensor_tensor(e_sel[:], e_one[:, 0], -1e30, e_sel[:], ALU.mult, ALU.add))
            link(dve.tensor_reduce(e_max[:, 1, :], e_sel[:], AX_X, ALU.max))
            first_of(e_one[:, 1], e_sel[:], e_max[:, 1, :], e_tmp[:], NE)
            dve.wait_ge(g_exp, 1)
            dve.tensor_tensor(w_ex[:, 0, :], e_max[:, 1, :], e_max[:, 0, :], ALU.subtract).then_inc(g_dif, 1)
            for i in range(2):
                for j in range(NT):
                    one = e_one[:, i, j:j + 1, :].broadcast_to([P, NG, NE])
                    last = dve.tensor_tensor(who[i][:, j, :].rearrange("p (g e) -> p g e", g=NG), one, sel4[:, j], ALU.mult)
                link(last)
            dve.tensor_tensor(both[:], who[0][:], who[1][:], ALU.add).then_inc(who_ready, 1)
            link(dve.tensor_reduce(g_sum[:], g_ex[:], AX_X, ALU.add))
            dve.wait_ge(g_exp, 2)
            link(dve.tensor_scalar(w_ex[:, 1, :], w_ex[:, 0, :], 1.0, None, ALU.add))
            link(dve.tensor_tensor(w_ex[:, 1, :], w_ex[:, 1, :], g_sum[:], ALU.mult))
            link(dve.reciprocal(wgt[:, 0, :], w_ex[:, 1, :]))
            link(dve.tensor_tensor(wgt[:, 1, :], wgt[:, 0, :], w_ex[:, 0, :], ALU.mult))
            for j, (t0, n_t) in enumerate(TILES):
                src = take(f"t{j}")
                dve.tensor_copy(x2[0:n_t, j, 0:512], src[0:n_t, :]).then_inc(tv_used, 1)
                dve.wait_ge(tv_used, TV_AT[f"t{j}"] + 1)
                dve.wait_ge(ta_used, TA_AT[f"t{j}"] + 1)
                if j >= 2:
                    dve.wait_ge(xn_stored[j % 2], 16 * (j // 2))
                dve.scalar_tensor_tensor(xn[j % 2][0:n_t], x2[0:n_t, j, :], rs5[0:n_t, j:j + 1], ffn_g[0:n_t],
                                         ALU.mult, ALU.mult).then_inc(xn_ready, 1)
            src = take("pos")[:, 0:NT * EXPERTS].rearrange("p (t e) -> p t e", t=NT)
            e_b = e_num[:].rearrange("p (o e) -> p o e", o=1).broadcast_to([P, NT, EXPERTS])
            link(dve.tensor_scalar(ptmp[:], src, float(EXPERTS), None, ALU.mult))
            dve.tensor_tensor(ptmp[:], ptmp[:], e_b, ALU.add).then_inc(tv_used, 1)
            dve.wait_ge(tv_used, TV_AT["pos"] + 1)
            for i in range(2):
                link(dve.tensor_tensor(who[i][:], who[i][:], ptmp[:], ALU.mult))
                link(dve.tensor_reduce(place[:, i, :], who[i][:], AX_X, ALU.add))
            dve.tensor_copy(place_i[:], place[:]).then_inc(place_ready, 1)
            src = take("cnt")
            dve.tensor_reduce(c_max[:, 0:1], src[:, 0:EXPERTS], AX_X, ALU.max).then_inc(tv_used, 1)
            dve.wait_ge(tv_used, TV_AT["cnt"] + 1)
            link(dve.memset(c_max[:, 1:2], 0.0))
            for i in range(1, LIST_ROWS // P):
                link(dve.scalar_tensor_tensor(c_max[:, 1:2], c_max[:, 0:1], float(P * i), c_max[:, 1:2], ALU.is_gt, ALU.add))
            dve.tensor_copy(more[:], c_max[:, 1:2]).then_inc(pass_ready, 1)
            dve.wait_ge(list_in, 16)
            dve.tensor_scalar(gids[:], ids[:], 1, None, ALU.arith_shift_right).then_inc(gids_ready, 1)

            def split_e(q, it, j, r):
                dve.wait_ge(eh_ready[r], q + 1)
                dve.tensor_tensor(e_l[r][:], raw_e[3 * j + r][:], e_h[r][:].bitcast(F32), ALU.subtract).then_inc(el_ready[r], 1)

            def columns_l(q):
                dve.wait_ge(xeh_ready, q + 1)
                for b in range(2):
                    last = dve.tensor_tensor(xeL[:, 4 * b:4 * b + 4, :], tv[b].rearrange("p (k t) -> p k t", k=4),
                                             xeH[:, 4 * b:4 * b + 4, :].bitcast(F32), ALU.subtract)
                last.then_inc(xel_ready, 1)

            def act_l(q):
                dve.wait_ge(ah_ready, q + 1)
                dve.tensor_tensor(aL[:], ta[0][:, 0:2 * P].rearrange("p (k t) -> p k t", k=2), aH[:].bitcast(F32),
                                  ALU.subtract).then_inc(al_ready, 1)

            def y_right(q, j, it, stored):
                dve.wait_ge(y_done, q + 1)
                if stored:
                    dve.wait_ge(y_stored[j], (it + j) * 16)
                dve.tensor_copy(ye[j][:, 512:D], mm[1][:, 1, :]).then_inc(yv_ready, 1)

            def step(q, it, j, first, last):
                prev = (q - 1, 1 - j, it if j else it - 1)
                if not (first and j == 0):
                    act_l(prev[0])
                if not (last and j == 1):
                    for r in range(2):
                        split_e(q + 1, it if j == 0 else it + 1, 1 - j, r)
                dve.wait_ge(silu_ready, q + 1)
                if not (first and j == 0):
                    dve.wait_ge(at_done, q)
                dve.tensor_tensor(gated[:], mm[0][:, j, FF:2 * FF], silu[:], ALU.mult).then_inc(gated_ready, 1)
                if not (last and j == 1):
                    columns_l(q + 1)
                if not (first and j == 0):
                    y_right(prev[0], prev[1], prev[2], not first)
                split_e(q, it, j, 2)

            for r in range(2):
                split_e(0, 0, 0, r)
            columns_l(0)
            for j in range(2):
                step(j, 0, j, True, False)
            extra = dve.value_load(more[0:1, 0:1], min_val=0, max_val=LIST_ROWS // P - 1)
            last_it = extra * (EXPERTS // 2) + (EXPERTS // 2 - 1)
            with dve.Fori(1, last_it) as it:
                for j in range(2):
                    step(it * 2 + j, it, j, False, False)
            for j in range(2):
                step(last_it * 2 + j, last_it, j, False, True)
            act_l(last_it * 2 + 1)
            y_right(last_it * 2 + 1, 1, last_it, True)

            for t, (t0, n) in enumerate(TILES):
                dve.wait_ge(yr_in[t % 2], 16 * (t // 2 + 1))
                link(dve.scalar_tensor_tensor(x2[0:n, t, :], yr[t % 2][0:n, 0, :], wgt[0:n, 0, t:t + 1], x2[0:n, t, :],
                                              ALU.mult, ALU.add))
                dve.scalar_tensor_tensor(x2[0:n, t, :], yr[t % 2][0:n, 1, :], wgt[0:n, 1, t:t + 1], x2[0:n, t, :],
                                         ALU.mult, ALU.add).then_inc(y_sum, 1)
                dve.wait_ge(y_sq, t + 1)
                dve.tensor_scalar(fin_ss[0:n, t:t + 1], fin_ss[0:n, t:t + 1], 1.0 / D, EPS, ALU.mult, ALU.add).then_inc(y_ms, 1)
                dve.wait_ge(y_root, t + 1)
                link(dve.reciprocal(fin_ss[0:n, t:t + 1], fin_ss[0:n, t:t + 1]))
                if t >= 2:
                    dve.wait_ge(y_saved[t % 2], 16 * (t // 2))
                dve.scalar_tensor_tensor(yo[t % 2][0:n], x2[0:n, t, :], fin_ss[0:n, t:t + 1], fin_g[0:n],
                                         ALU.mult, ALU.mult).then_inc(y_out, 1)

        @block.tensor
        def _(pe):
            tv_n, ta_n = [0], [0]

            def open_tv(name):
                assert TV_ORDER[tv_n[0]] == name, (name, TV_ORDER[tv_n[0]])
                if tv_n[0] >= 2:
                    pe.wait_ge(tv_used, tv_n[0] - 1)
                tv_n[0] += 1
                return tv[(tv_n[0] - 1) % 2]

            def open_ta(name):
                assert TA_ORDER[ta_n[0]] == name, (name, TA_ORDER[ta_n[0]])
                if ta_n[0] >= 2:
                    pe.wait_ge(ta_used, ta_n[0] - 1)
                ta_n[0] += 1
                return ta[(ta_n[0] - 1) % 2]

            def open_mm(key):
                m = MM_AT[key]
                if m >= 2:
                    pe.wait_ge(mm_used, m - 1)
                return mm[m % 2]

            def turn(out, src, n=P):
                return pe.transpose(out, src, ident[0:n, 0:n])

            def three(out, h1, l1, h2, l2, start, stop):
                pe.matmul(out, h1, h2, start=start, stop=False)
                pe.matmul(out, l1, h2, start=False, stop=False)
                return pe.matmul(out, h1, l2, start=False, stop=stop)

            def project(kind, i, mH, mL, ready=None):
                key = (kind, i // 2)
                n = W_AT[key]
                pe.wait_ge(l_ready, n + 1)
                out = open_mm((kind, i))
                wh = w_h[n % 2][:].rearrange("p (k c) -> p k c", k=8)
                wl = w_l[n % 2][:].rearrange("p (k c) -> p k c", k=8)
                c = slice((i % 2) * P, (i % 2 + 1) * P)
                for k in range(8):
                    if ready:
                        ready(k)
                    for b in range(2):
                        tok = slice(b * HT, (b + 1) * HT)
                        last = three(out[:, b, 0:HT], wh[:, k, c], wl[:, k, c], mH[:, k, tok], mL[:, k, tok],
                                     k == 0, k == 7)
                last.then_inc(mm_ready, 1)

            def sums(n):
                pe.wait_ge(sq_added, 8 * (n + 1))
                for b in range(2):
                    out = open_tv(f"rs{2 * n + b}")
                    pe.matmul(out[:, 0:HT], ones[:], sumsq[:, b * HT:(b + 1) * HT], start=True, stop=True).then_inc(tv_ready, 1)

            pe.wait_ge(pool_made, 2)
            pe.wait_ge(dve_made, 1)
            pe.wait_ge(params_in, 16 * 9)
            out = open_tv("cols_a")
            turn(out[:, 0:N_ROWS_A], rows_a[:], N_ROWS_A).then_inc(tv_ready, 1)
            out = open_tv("cols_b")
            turn(out[:, 0:N_ROWS_B], rows_b[:], N_ROWS_B).then_inc(tv_ready, 1)
            for j, (t0, n) in enumerate(TILES):
                src = xs_rows[:] if j == 4 else raw_in(pe, ("x", j // 2))[:, (j % 2) * D:(j % 2 + 1) * D]
                for half, (openb, done) in enumerate(((open_tv, tv_ready), (open_ta, ta_ready))):
                    out = openb(f"x{j}")
                    for k in range(4):
                        c = (4 * half + k) * P
                        last = turn(out[:, k * P:k * P + n], src[:, c:c + P], n)
                    last.then_inc(done, 1)

            for m in range(16):
                project("w_in", m, xH, xL, (lambda k: pe.wait_ge(xl_ready, k + 1)) if m == 0 else None)
                if m == 0:
                    sums(0)
                if m == 1:
                    pe.wait_ge(masked, 1)
                    out = open_tv("ws")
                    for h in range(HEADS):
                        last = turn(out[:, h * P:(h + 1) * P], ws_rows[:, h, :])
                    last.then_inc(tv_ready, 1)
                    pe.wait_ge(rows_in, 32)
                    for c in range(2):
                        out = open_tv(f"cc{c}")
                        for i in range(4):
                            last = turn(out[:, i * 4 * PAST:(i + 1) * 4 * PAST], cache_rows[:, c, i * P:(i + 1) * P], 4 * PAST)
                        last.then_inc(tv_ready, 1)
                if m == 9:
                    pe.wait_ge(glu_ready, 4)
                    out = open_ta("tail")
                    for i in range(4):
                        last = turn(out[0:PAST + NS, i * P:(i + 1) * P], glu[:, i, SEQ:PAST + T])
                    last.then_inc(ta_ready, 1)
                if m >= 12:
                    if m == 12:
                        pe.wait_ge(z_act, 8)
                    for j in ((0, 1), (2, 3), (4,), ())[m - 12]:
                        t0, n = TILES[j]
                        out = open_tv(f"v{j}")
                        for i in range(4):
                            last = turn(out[0:n, i * P:(i + 1) * P], v_raw[:, i, t0:t0 + n])
                        last.then_inc(tv_ready, 1)
            slot = raw_in(pe, ("mem", 0))
            for i in range(4):
                out = open_tv(f"mem{i}")
                for kk in range(2):
                    for t in range(2):
                        c = t * D + (2 * i + kk) * P
                        last = turn(out[:, (2 * kk + t) * P:(2 * kk + t + 1) * P], slot[:, c:c + P])
                last.then_inc(tv_ready, 1)

            def conv_rows(j):
                t0, n = TILES[j]
                out = open_tv(f"cf{j}")
                for i in range(4):
                    last = turn(out[0:n, i * P:(i + 1) * P], conv[:, i, t0:t0 + n])
                last.then_inc(tv_ready, 1)

            def keys_turned(h):
                out = open_tv(f"kt{h}")
                for kk in range(2):
                    for t in range(2):
                        c = t * XH_DIM + kk * P
                        last = turn(out[:, (2 * kk + t) * P:(2 * kk + t + 1) * P], zt[h % 2][:, c:c + P])
                last.then_inc(tv_ready, 1)

            pe.wait_ge(tv_used, TV_AT["mem3"] + 1)
            for n in range(8, 16):
                pe.wait_ge(l_ready, n + 1)
                wh = w_h[n % 2][:].rearrange("p (k c) -> p k c", k=8)
                wl = w_l[n % 2][:].rearrange("p (k c) -> p k c", k=8)
                for t in range(2):
                    m = 2 * (n - 8) + t
                    out = open_mm(("wk", m) if n < 12 else ("wv", m - 8))
                    for k in range(8):
                        last = three(out[:, 0, 0:MEM], xH[:, k, t * P:(t + 1) * P], xL[:, k, t * P:(t + 1) * P],
                                     wh[:, k, :], wl[:, k, :], k == 0, k == 7)
                    last.then_inc(mm_ready, 1)
                if n == 8:
                    pe.wait_ge(v_ready, NT)
                    out = open_tv("vs")
                    for h in range(HEADS):
                        last = turn(out[:, h * NS:(h + 1) * NS], v_s[0:NS, h * P:(h + 1) * P], NS)
                    last.then_inc(tv_ready, 1)
                    for h in range(HEADS):
                        out = open_tv(f"mix{h}")
                        for c in range(4):
                            last = pe.matmul(out[:, c * P:(c + 1) * P], v_tok[:, c, h * P:(h + 1) * P], wsT[:, h, :],
                                             start=True, stop=True)
                        last.then_inc(tv_ready, 1)
                if 9 <= n < 13:
                    pe.wait_ge(mm_used, MM_AT[("wk", 2 * (n - 9) + 1)] + 1)
                    keys_turned(n - 9)
            pe.wait_ge(conv_v, 2 * TAPS)
            pe.wait_ge(conv_p, 2 * TAPS - 2)
            pe.wait_ge(convs_done, 4)
            for j in range(NT):
                conv_rows(j)
            for j, (t0, n) in enumerate(TILES):
                pe.wait_ge(cn_ready, j + 1)
                out = open_ta(f"cb{j}")
                row = v_tok[:, j, :] if j < 4 else v_s[0:n]
                for i in range(4):
                    last = turn(out[:, i * P:i * P + n], row[:, i * P:(i + 1) * P], n)
                last.then_inc(ta_ready, 1)
            for k in range(8):
                project("w_out", k, cH, cL, (lambda kk: pe.wait_ge(xl_ready, 8 + kk + 1)) if k == 0 else None)
            for k in range(8):
                project("wq", k, xH, xL, (lambda kk: pe.wait_ge(xl_ready, 16 + kk + 1)) if k == 0 else None)
                if k == 0:
                    sums(1)
            pe.wait_ge(mm_used, MM_AT[("wq", 7)] + 1)
            for b in range(2):
                out = open_ta(f"qs{b}")
                for k in range(4):
                    last = turn(out[0:NS, k * P:(k + 1) * P], qT[:, 4 * b + k, SEQ:T])
                last.then_inc(ta_ready, 1)

            def scores(j):
                out = open_mm(("score", j))
                for h in range(HEADS):
                    for kk in range(2):
                        last = pe.matmul(out[:, h // 2, (h % 2) * MEM:(h % 2 + 1) * MEM],
                                         qT[:, 2 * h + kk, j * P:(j + 1) * P], kT[:, 2 * h + kk, :],
                                         start=kk == 0, stop=kk == 1)
                last.then_inc(mm_ready, 1)

            def query_rows(s):
                for b in range(2):
                    out = open_tv(f"qb{s}{b}")
                    pe.matmul(out, pick[:, s, :], q_s[:, 512 * b:512 * b + 512], start=True, stop=True).then_inc(tv_ready, 1)

            scores(0)
            scores(1)
            pe.wait_ge(ta_used, TA_AT["qs1"] + 1)
            pe.wait_ge(pick_made, 2)
            for j in range(4):
                query_rows(2 * j)
                pe.wait_ge(p_ready, j + 1)
                for b in range(2):
                    out = open_ta(f"pt{j}{b}")
                    for hh in range(2):
                        for t in range(2):
                            last = turn(out[:, (2 * hh + t) * P:(2 * hh + t + 1) * P],
                                        probs[j % 2][:, 2 * b + hh, t * P:(t + 1) * P])
                    last.then_inc(ta_ready, 1)
                query_rows(2 * j + 1)
                if j < 2:
                    scores(j + 2)
            def values(h):
                out = open_mm(("pv", h))
                for kk in range(2):
                    for t in range(2):
                        c = (2 * h + kk) * P
                        last = pe.matmul(out[:, kk, :], vm[:, t, c:c + P], pT[:, h, t, :], start=t == 0, stop=t == 1)
                last.then_inc(mm_ready, 1)

            R = NS * HEADS
            pe.wait_ge(tv_used, TV_AT["qb71"] + 1)
            out = open_tv("ss")
            for t in range(2):
                last = turn(out[0:R, t * P:(t + 1) * P], s_sc[:, t, :])
            last.then_inc(tv_ready, 1)
            pe.wait_ge(ta_used, TA_AT["pt31"] + 1)
            values(0)
            values(1)
            pe.wait_ge(s_norm, 1)
            out = open_tv("sp")
            for t in range(2):
                last = turn(out[:, t * R:(t + 1) * R], s_p[:, t * P:(t + 1) * P], R)
            last.then_inc(tv_ready, 1)
            values(2)
            values(3)
            pe.wait_ge(tv_used, TV_AT["sp"] + 1)
            out = open_tv("so")
            for s in range(NS):
                slot = raw_in(pe, ("vc", s))
                for k in range(8):
                    for t in range(2):
                        c = t * D + k * P
                        last = pe.matmul(out[:, k * NS + s:k * NS + s + 1], slot[:, c:c + P],
                                         s_pT[:, t, s * HEADS + k // 2:s * HEADS + k // 2 + 1], start=t == 0, stop=t == 1)
                last.then_inc(vc_used if s < NS - 1 else tv_ready, 1)
            pe.wait_ge(mm_used, MM_AT[("pv", 3)] + 1)
            pe.wait_ge(tv_used, TV_AT["so"] + 1)
            for k in range(8):
                project("wo", k, xH, xL)
            pe.wait_ge(sq_added, 24)
            out = open_tv("r2")
            for j, (t0, n) in enumerate(TILES):
                last = pe.matmul(out[0:n, j:j + 1], sumsq[:, t0:t0 + n], ones[:, 0:1], start=True, stop=True)
            last.then_inc(tv_ready, 1)
            pe.wait_ge(rg_ready, 1)
            out = open_tv("lg")
            W = NG + EXPERTS
            for j, (t0, n) in enumerate(TILES):
                for k in range(8):
                    last = pe.matmul(out[0:n, j * W:(j + 1) * W], xT[:, k, t0:t0 + n], router[:, k, :],
                                     start=k == 0, stop=k == 7)
            last.then_inc(tv_ready, 1)
            for j, (t0, n) in enumerate(TILES):
                for half, (openb, done) in enumerate(((open_tv, tv_ready), (open_ta, ta_ready))):
                    out = openb(f"t{j}")
                    for k in range(4):
                        last = turn(out[0:n, k * P:(k + 1) * P], xT[:, 4 * half + k, t0:t0 + n])
                    last.then_inc(done, 1)
            pe.wait_ge(who_ready, 1)
            out = open_tv("pos")
            for j, (_, n) in enumerate(TILES):
                o = out[:, j * EXPERTS:(j + 1) * EXPERTS]
                for i in range(j):
                    pe.matmul(o, ones[:], both[:, i, :], start=i == 0, stop=False)
                last = pe.matmul(o, upper[0:n, :], both[0:n, j, :], start=j == 0, stop=True)
            last.then_inc(tv_ready, 1)
            out = open_tv("cnt")
            for j, (_, n) in enumerate(TILES):
                last = pe.matmul(out[:, 0:EXPERTS], ones[0:n, :], both[0:n, j, :], start=j == 0, stop=j == NT - 1)
            last.then_inc(tv_ready, 1)

            def hidden(q, j, r, old):
                if r == 0:
                    pe.wait_ge(xel_ready, q + 1)
                    if old:
                        pe.wait_ge(gated_ready, q - 1)
                pe.wait_ge(el_ready[r], q + 1)
                wh = e_h[r][:].rearrange("p (k c) -> p k c", k=4)
                wl = e_l[r][:].rearrange("p (k c) -> p k c", k=4)
                for kk in range(4):
                    k = 4 * r + kk
                    last = three(mm[0][:, j, :], xeH[:, k, :], xeL[:, k, :], wh[:, kk, :], wl[:, kk, :], k == 0, k == 7)
                last.then_inc(hid_ready if r else e_used, 1)

            def gathered_columns(q, it, j, old):
                pe.wait_ge(xe_landed[j], (it + 1) * 16)
                if old:
                    pe.wait_ge(xel_ready, q)
                rows = xe[j][:].rearrange("s (p k) -> s k p", k=KT_D)
                for k in range(KT_D):
                    last = turn(tv[k // 4][:, (k % 4) * P:(k % 4 + 1) * P], rows[:, k, :])
                last.then_inc(xt_done, 1)

            def act_columns(q, old):
                pe.wait_ge(gated_ready, q + 1)
                if old:
                    pe.wait_ge(al_ready, q)
                rows = gated[:].rearrange("s (p k) -> s k p", k=2)
                for k in range(2):
                    last = turn(ta[0][:, k * P:(k + 1) * P], rows[:, k, :])
                last.then_inc(at_done, 1)

            def down(q, old):
                pe.wait_ge(al_ready, q + 1)
                pe.wait_ge(el_ready[2], q + 1)
                if old:
                    pe.wait_ge(ya_ready, q)
                    pe.wait_ge(yv_ready, q)
                wh = e_h[2][:].rearrange("p (k d) -> p k d", k=2)
                wl = e_l[2][:].rearrange("p (k d) -> p k d", k=2)
                for b in range(2):
                    c = slice(512 * b, 512 * b + 512)
                    for k in range(2):
                        last = three(mm[1][:, b, :], aH[:, k, :], aL[:, k, :], wh[:, k, c], wl[:, k, c], k == 0, k == 1)
                last.then_inc(y_done, 1)

            def step(q, it, j, first, last):
                lag = not (first and j == 0)
                if lag:
                    act_columns(q - 1, not (first and j == 1))
                hidden(q, j, 0, not first)
                hidden(q, j, 1, not first)
                if not (last and j == 1):
                    gathered_columns(q + 1, it if j == 0 else it + 1, 1 - j, True)
                if lag:
                    down(q - 1, not (first and j == 1))

            pe.wait_ge(tv_used, len(TV_ORDER))
            pe.wait_ge(ta_used, len(TA_ORDER))
            gathered_columns(0, 0, 0, False)
            for j in range(2):
                step(j, 0, j, True, False)
            pe.wait_ge(pass_ready, 1)
            extra = pe.value_load(more[0:1, 0:1], min_val=0, max_val=LIST_ROWS // P - 1)
            last_it = extra * (EXPERTS // 2) + (EXPERTS // 2 - 1)
            with pe.Fori(1, last_it) as it:
                for j in range(2):
                    step(it * 2 + j, it, j, False, False)
            for j in range(2):
                step(last_it * 2 + j, last_it, j, False, True)
            act_columns(last_it * 2 + 1, True)
            down(last_it * 2 + 1, True)

        @block.gpsimd
        def _(pool):
            def wait(s, value):
                pool.wait_ge(s, value)
                pool.sem_inc(pool_waits, 1)

            pool.memset(ident[:], 0.0).then_inc(pool_made, 1)
            pool.wait_ge(pool_made, 1)
            pool.affine_select(out=ident[:], in_=ident[:], compare_op=ALU.not_equal, fill=1.0, base=0,
                               pattern=[[-1, P]], channel_multiplier=1).then_inc(pool_made, 1)
            pool.memset(upper[:], 1.0).then_inc(pool_made, 1)
            pool.wait_ge(pool_made, 3)
            pool.affine_select(out=upper[:], in_=upper[:], compare_op=ALU.is_gt, fill=0.0, base=0,
                               pattern=[[1, P]], channel_multiplier=-1).then_inc(pool_made, 1)
            pool.memset(list_init[:], NOBODY).then_inc(pool_made, 1)
            pool.wait_ge(pool_made, 5)
            blank = id_list.rearrange("(c p n) o -> c p (n o)", c=2, p=P)
            pool.dma_start(blank[0], list_init[:]).then_inc(list_blank, 16)
            pool.dma_start(blank[1], list_init[:]).then_inc(y_stored[1], 16)
            pool.wait_ge(rows_in, 32)
            pool.affine_select(out=ws_rows[:], in_=ws_rows[:], compare_op=ALU.is_ge, fill=0.0, base=0,
                               pattern=[[0, HEADS], [-1, P]], channel_multiplier=1).then_inc(masked, 1)

            def add_squares(n):
                for k in range(8):
                    pool.wait_ge(sq_ready, 8 * n + k + 1)
                    if k == 0:
                        ins = pool.tensor_copy(sumsq[:], zt[0][:])
                    else:
                        pool.wait_ge(sq_added, 8 * n + k)
                        ins = pool.tensor_tensor(sumsq[:], sumsq[:], zt[k % 2][:], ALU.add)
                    ins.then_inc(sq_added, 1)

            add_squares(0)
            def add_products(n0, n1):
                for n in range(n0, n1):
                    i, k = 1 + 2 * (n // TAPS), n % TAPS
                    if k:
                        p = n - n // TAPS - 1
                        pool.wait_ge(tap_scaled, n + 1)
                        if p:
                            pool.wait_ge(conv_p, p)
                        pool.tensor_tensor(conv[:, i, 0:SEQ], conv[:, i, 0:SEQ], scaled[p % 4][:], ALU.add).then_inc(conv_p, 1)

            add_products(0, 48)
            pool.wait_ge(consts_in, 16 * 4)
            for j, (_, n) in enumerate(TILES):
                row = v_tok[:, j, :] if j < 4 else v_s[0:n]
                pool.wait_ge(v_norm, j + 1)
                pool.tensor_tensor(row, row, ln_g[0:n], ALU.mult).then_inc(v_scaled, 1)
                pool.wait_ge(v_scaled, j + 1)
                pool.tensor_tensor(row, row, ln_b[0:n], ALU.add).then_inc(v_ready, 1)
            add_products(48, 2 * TAPS)
            pool.wait_ge(ta_ready, TA_AT[f"cb{NT - 1}"] + 1)
            pool.memset(pick[:], 0.0).then_inc(pick_made, 1)
            pool.wait_ge(pick_made, 1)
            pool.affine_select(out=pick[:], in_=pick[:], compare_op=ALU.not_equal, fill=1.0, base=0,
                               pattern=[[-1, NS], [0, P]], channel_multiplier=1).then_inc(pick_made, 1)
            add_squares(1)
            pool.wait_ge(ta_ready, TA_AT["pt31"] + 1)
            pool.iota(prio[:], pattern=[[-1, 8]], base=8, channel_multiplier=0,
                      allow_small_or_imprecise_dtypes=True).then_inc(route_made, 1)
            pool.iota(e_num[:], pattern=[[1, EXPERTS]], base=0, channel_multiplier=0,
                      allow_small_or_imprecise_dtypes=True).then_inc(route_made, 1)
            pool.iota(ident_no[:], pattern=[[1, 2], [2 * P, NT]], base=0, channel_multiplier=2).then_inc(route_made, 1)
            add_squares(2)
            for j, (t0, n) in enumerate(TILES):
                pool.wait_ge(xn_ready, j + 1)
                pool.dma_start(xn_rows[t0:t0 + n, :], xn[j % 2][0:n]).then_inc(xn_stored[j % 2], 16)
            pool.wait_ge(place_ready, 1)
            pool.wait_ge(route_made, 3)
            pool.wait_ge(list_blank, 16)
            pool.wait_ge(y_stored[1], 16)
            for i in range(2):
                for j, (_, n) in enumerate(TILES):
                    pool.indirect_dma_start(
                        out=id_list, out_offset=bass.IndirectOffsetOnAxis(ap=place_i[0:n, i, j:j + 1], axis=0),
                        in_=ident_no[0:n, i, j:j + 1], in_offset=None, bounds_check=LIST_ROWS * EXPERTS - 1,
                        oob_is_err=False).then_inc(list_made, 16)
            pool.wait_ge(mm_ready, len(MM_ORDER))
            pool.memset(xe[0][:], 0.0).then_inc(xe_zero, 1)
            pool.memset(xe[1][:], 0.0).then_inc(xe_zero, 1)
            pool.wait_ge(list_made, 16 * 2 * NT)
            pool.dma_start(ids[:], id_list.rearrange("(c s e) o -> s c (e o)", c=LIST_ROWS // P, e=EXPERTS)).then_inc(list_in, 16)
            pool.wait_ge(gids_ready, 1)
            pool.wait_ge(xn_stored[0], 16 * 3)
            pool.wait_ge(xn_stored[1], 16 * 2)
            pool.wait_ge(xe_zero, 2)
            pool.wait_ge(pass_ready, 1)
            extra = pool.value_load(more[0:1, 0:1], min_val=0, max_val=LIST_ROWS // P - 1)
            last_it = extra * (EXPERTS // 2) + (EXPERTS // 2 - 1)
            ids_f = ids[:].rearrange("p c e -> p (c e)")
            gids_f = gids[:].rearrange("p c e -> p (c e)")

            def gather_go(j):
                pool.indirect_dma_start(out=xe[j][:], out_offset=None, in_=xn_rows,
                                        in_offset=bass.IndirectOffsetOnAxis(ap=g_idx[j][:], axis=0),
                                        bounds_check=T - 1, oob_is_err=False).then_inc(xe_landed[j], 16)

            def scatter_go(j):
                pool.indirect_dma_start(out=y_rows, out_offset=bass.IndirectOffsetOnAxis(ap=s_idx[j][:], axis=0),
                                        in_=ye[j][:], in_offset=None, bounds_check=2 * T - 1,
                                        oob_is_err=False).then_inc(y_stored[j], 16)

            def step(q, it, j, first, last):
                if not last:
                    wait(xt_done, q + 1)
                    pool.tensor_copy(g_idx[j][:], gids_f[:, bass.ds(q + 2, 1)]).then_inc(gi_made[j], 1)
                    wait(gi_made[j], it + 2)
                    gather_go(j)
                if not (first and j == 0):
                    scatter(q - 1, it if j else it - 1, 1 - j, not first)

            def scatter(q, it, j, old):
                if old:
                    wait(y_stored[j], (it + j) * 16)
                pool.tensor_copy(s_idx[j][:], ids_f[:, bass.ds(q, 1)]).then_inc(si_made[j], 1)
                wait(si_made[j], it + 1)
                wait(ya_ready, q + 1)
                wait(yv_ready, q + 1)
                scatter_go(j)

            for j in range(2):
                pool.tensor_copy(g_idx[j][:], gids_f[:, j:j + 1]).then_inc(gi_made[j], 1)
                pool.wait_ge(gi_made[j], 1)
                gather_go(j)
            for j in range(2):
                step(j, 0, j, True, False)
            with pool.Fori(1, last_it) as it:
                for j in range(2):
                    step(it * 2 + j, it, j, False, False)
            for j in range(2):
                step(last_it * 2 + j, last_it, j, False, True)
            scatter(last_it * 2 + 1, last_it, 1, True)


_IN = ["x_prompt", "x_sample", "mem_prompt", "cache_conv", "cache_mem_k", "cache_mem_v", "norm_mix_g", "w_in",
       "gm_ln_g", "gm_ln_b", "gm_ws", "gm_bs", "conv_w", "conv_b", "cv_ln_g", "cv_ln_b", "w_out", "norm_mem_g",
       "norm_xa_g", "xa_wq", "xa_wk", "xa_wv", "xa_wo", "norm_ffn_g", "router_g", "router_g_b", "router_e",
       "router_e_b", "exp_w1", "exp_w3", "exp_w2", "final_norm_g"]
_OUT = [("y_prompt", (1, SEQ, D)), ("y_sample", (NS, 1, D)), ("conv_prompt", (1, 1, PAST, GM)),
        ("conv_sample", (1, NS, PAST, GM)), ("gmv_prompt", (1, 1, P, GM)), ("gmv_sample", (1, NS, 1, GM)),
        ("mem_k_prompt", (1, 1, MEM, HEADS, XH_DIM)), ("mem_v_prompt", (1, 1, MEM, HEADS, XH_DIM))]


def kernel(**inputs):
    import concourse.bacc as bacc
    from concourse.bass_utils import run_bass_kernel_spmd

    nc = bacc.Bacc("TRN2", target_bir_lowering=False, num_devices=1)
    arrays, args = {}, {}
    for name in _IN:
        arrays[name] = np.ascontiguousarray(inputs[name])
        args[name] = nc.dram_tensor(name, arrays[name].shape, F32, kind="ExternalInput").ap()
    outs = [nc.dram_tensor(f"out_{name}", shape, F32, kind="ExternalOutput").ap() for name, shape in _OUT]
    trunk_kernel(nc, args, outs)
    r = run_bass_kernel_spmd(nc, [arrays], core_ids=[0])
    return tuple(r.results[0][f"out_{name}"] for name, _ in _OUT)
```

```python
from contextlib import ExitStack

import numpy as np

import concourse.bass as bass
from concourse import mybir

F32 = mybir.dt.float32
F32R = mybir.dt.float32r
I32 = mybir.dt.int32
ALU = mybir.AluOpType
ACT = mybir.ActivationFunctionType
AX_X = mybir.AxisListType.X

P = 128
D = 1024
KT_D = D // P
SEQ = 512
NS = 8
T = SEQ + NS
HT = T // 2
TILES = [(0, P), (P, P), (2 * P, P), (3 * P, P), (SEQ, NS)]
NT = len(TILES)
GM = 512
HEADS = 4
TAPS = 31
PAST = TAPS - 1
MEM = 256
XH_DIM = 256
NG, NE = 4, 8
EXPERTS = NG * NE
FF = 256
EPS = 1e-6
CHUNK = 2048
SLOT_BYTES = 4 * CHUNK
RAW = 4
CONV_V = TAPS + 16
CONV_P = 4 * TAPS - CONV_V
LAST_BY_DVE = (3, 4)
LIST_ROWS = 5 * P
NOBODY = 1 << 20
SCALE = float(XH_DIM) ** -0.5

W_IN_COLS = [1024, 1536, 1280, 1792, 512, 768, 0, 256]
STREAM = ([("x", 0), ("x", 1)] + [("w_in", i) for i in range(8)] + [("mem", 0)]
          + [("wk", i) for i in range(4)] + [("wv", i) for i in range(4)] + [("w_out", i) for i in range(4)]
          + [("wq", i) for i in range(4)] + [("wo", 0), ("wo", 1)] + [("kc", i) for i in range(NS)]
          + [("vc", i) for i in range(NS)] + [("wo", 2), ("wo", 3)])
AT = {key: c for c, key in enumerate(STREAM)}
WEIGHTS = [key for key in STREAM if key[0][0] == "w"]
W_AT = {key: n for n, key in enumerate(WEIGHTS)}

MM_ORDER = ([("w_in", i) for i in range(16)] + [("wk", i) for i in range(8)] + [("wv", i) for i in range(8)]
            + [("w_out", i) for i in range(8)] + [("wq", i) for i in range(8)] + [("score", i) for i in range(4)]
            + [("pv", i) for i in range(4)] + [("wo", i) for i in range(8)])
MM_AT = {key: m for m, key in enumerate(MM_ORDER)}

TV_ORDER = ([f"x{j}" for j in range(NT - 1)] + ["cols_a", "cols_b", f"x{NT - 1}"] + ["rs0", "rs1", "ws", "cc0", "cc1"]
            + [f"v{j}" for j in range(NT)] + [f"mem{i}" for i in range(4)] + ["vs"] + [f"mix{h}" for h in range(4)]
            + [f"kt{h}" for h in range(4)] + [f"cf{j}" for j in range(NT)] + ["rs2", "rs3"]
            + [f"qb{s}{b}" for s in range(NS) for b in range(2)] + ["ss", "sp", "or0", "or1", "so", "lg0", "lg1", "r2",
                                                             "lg", "pos", "cnt"])
TV_AT = {key: v for v, key in enumerate(TV_ORDER)}
TA_ORDER = ([f"x{j}" for j in range(NT)] + ["tail"] + [f"cb{j}" for j in range(NT)] + ["qs0", "qs1"]
            + [f"pt{j}{b}" for j in range(4) for b in range(2)] 
            + [f"t{j}{b}" for j in range(NT) for b in range(2)])
TA_AT = {key: a for a, key in enumerate(TA_ORDER)}

ROWS_A = {"mix_g": 0, "mem_g": 8, "xa_g": 16, "ffn_g": 24, "conv_b": 32, "cv_g": 36, "cv_b": 40}
N_ROWS_A = 44
N_ROWS_B = TAPS * 4


def tap_p(n):
    return (1 + 2 * (n // TAPS), n % TAPS) if n < 2 * TAPS else (2, n - 2 * TAPS + CONV_V - TAPS)


def mm_after(n):
    kind, i = WEIGHTS[n]
    return MM_AT[(kind, 2 * i + 1)] + 1


def trunk_kernel(nc, a, outs):
    (y_prompt, y_sample, conv_prompt, conv_sample, gmv_prompt, gmv_sample, mem_k_out, mem_v_out) = outs

    xn_rows = nc.dram_tensor("xn_rows", (T, D), F32, kind="Internal").ap()
    y_rows = nc.dram_tensor("y_rows", (2 * T, D), F32, kind="Internal").ap()
    id_list = nc.dram_tensor("id_list", (LIST_ROWS * EXPERTS, 1), I32, kind="Internal").ap()

    with ExitStack() as ctx:
        def sem(name):
            return ctx.enter_context(nc.semaphore(name))

        base = (nc.sbuf_base + 63) // 64 * 64
        top = [base]

        def room(nbytes):
            at = top[0]
            top[0] += (nbytes + 31) // 32 * 32
            assert top[0] <= base + 212600, top[0]
            return at

        def at(name, shape, dt, offset):
            return nc.alloc_sbuf_tensor_at(name, shape, dt, offset=offset)

        def sb(name, shape, dt=F32):
            return at(name, shape, dt, room(4 * int(np.prod(shape[1:]))))

        raw_at = [room(SLOT_BYTES) for _ in range(RAW)]
        extra_at = room(SLOT_BYTES)
        raw = [at(f"raw{i}", [P, CHUNK], F32, o) for i, o in enumerate(raw_at)]
        hl_at = [room(2 * SLOT_BYTES) for _ in range(2)]
        w_h = [at(f"w_h{i}", [P, CHUNK], F32R, o) for i, o in enumerate(hl_at)]
        w_l = [at(f"w_l{i}", [P, CHUNK], F32R, o + SLOT_BYTES) for i, o in enumerate(hl_at)]
        ROW = 4 * T
        x_at, xh_at, xl_at, ch_at, cl_at = (room(8 * ROW) for _ in range(5))
        xT = at("xT", [P, 8, T], F32, x_at)
        xH = at("xH", [P, 8, T], F32R, xh_at)
        xL = at("xL", [P, 8, T], F32R, xl_at)
        cH = at("cH", [P, 8, T], F32R, ch_at)
        cL = at("cL", [P, 8, T], F32R, cl_at)
        glu_at = room(4 * 4 * (PAST + SEQ + NS))
        glu = at("glu", [P, 4, PAST + T], F32, glu_at)
        kT_at = room(SLOT_BYTES)
        v_at = room(SLOT_BYTES)
        kT = at("kT", [P, 8, MEM], F32, kT_at)
        vm = at("vm", [P, 2, D], F32, v_at)
        ident = sb("ident", [P, P])
        ones = sb("ones", [P, P])
        upper = sb("upper", [P, P])
        g1_at = room(4 * D)
        wsT = at("wsT", [P, HEADS, P], F32, g1_at)
        bs_all = at("bs_all", [P, HEADS, P], F32, g1_at + 2 * D)
        g2_at = room(4 * D)
        ln_g = at("ln_g", [P, GM], F32, g2_at)
        ln_b = at("ln_b", [P, GM], F32, g2_at + 2 * D)
        cols_a = sb("cols_a", [P, N_ROWS_A])
        cols_b = sb("cols_b", [P, TAPS, 4])
        rstd = sb("rstd", [P, 2, HT])
        sumsq = sb("sumsq", [P, T])
        z_at = room(2 * ROW)
        zt = [at(f"zt{i}", [P, T], F32, z_at + i * ROW) for i in range(2)]
        s_at = room(2048 + 4 * 4 * NS * TAPS)
        v_s = at("v_s", [P, GM], F32, s_at)
        conv_s = at("conv_s", [P, 4, NS, TAPS], F32, s_at + 2048)
        stats = sb("stats", [P, NT, 4, 6])
        mv = sb("mv", [P, NT, 4, 2])
        ws00 = sb("ws00", [P, HEADS])
        vsT = sb("vsT", [P, HEADS, NS])
        m_ss = sb("m_ss", [P, 2])
        pmax = sb("pmax", [P, 4, 4])
        psum_p = sb("psum_p", [P, 4, 4])
        s_sc = sb("s_sc", [P, 2, NS * HEADS])
        s_mx = sb("s_mx", [P, 4])
        s_pT = sb("s_pT", [P, 2, NS * HEADS])
        rs5 = sb("rs5", [P, NT])
        one_col = sb("one_col", [P, NS, NS])
        ids = sb("ids", [P, LIST_ROWS // P, EXPERTS], I32)
        gids = sb("gids", [P, LIST_ROWS // P, EXPERTS], I32)
        g_idx = [sb(f"g_idx{i}", [P, 1], I32) for i in range(2)]
        s_idx = [sb(f"s_idx{i}", [P, 1], I32) for i in range(2)]
        wgt = sb("wgt", [P, 2, NT])
        more = sb("more", [P, 1], I32)
        one_junk = sb("one_junk", [NS, 1])
        fin_ss = sb("fin_ss", [P, NT])
        full = sb("full", [P, LIST_ROWS // P, EXPERTS], I32)

        cHf = at("cHf", [P, 8, T], F32, ch_at)
        cLf = at("cLf", [P, 8, T], F32, cl_at)
        rows_a = at("rows_a", [N_ROWS_A, P], F32, glu_at)
        rows_b = at("rows_b", [N_ROWS_B, P], F32, glu_at + 512)
        xs_rows = at("xs_rows", [NS, D], F32, cl_at)
        ws_rows = at("ws_rows", [P, HEADS, P], F32, kT_at)
        cache_rows = at("cache_rows", [4 * PAST, 2, GM], F32, v_at)
        tail = at("tail", [PAST + NS, GM], F32, kT_at)
        list_init = at("list_init", [P, LIST_ROWS // P * EXPERTS // 2], I32, v_at + 4096)
        v_raw = cHf[:, 0:4, :]
        v_tok = at("v_tok", [P, 4, GM], F32, ch_at + 4 * ROW)
        scaled = [at(f"scaled{i}", [P, SEQ], F32, extra_at + 4 * SEQ * i) for i in range(4)]
        u_act = cLf[:, 0:4, :]
        conv = cLf[:, 4:8, :]
        qT = cHf
        probs = [at(f"probs{i}", [P, HEADS, MEM], F32, glu_at + 4096 * i) for i in range(2)]
        pT = at("pT", [P, HEADS, 2, SEQ], F32, cl_at)
        q_s = at("q_s", [NS, D], F32, z_at)
        o_s = at("o_s", [NS, D], F32, z_at)
        v_part = [at(f"v_part{i}", [P, D], F32, ch_at + 4096 * i) for i in range(2)]
        pick = at("pick", [NS, NS, P], F32, s_at)
        ttr_out = at("ttr_out", [P, MEM], F32, g2_at)
        s_p = at("s_p", [NS * HEADS, MEM], F32, g2_at + 1024)
        router = at("router", [P, KT_D, NG + EXPERTS], F32, s_at + 4096)
        lg_rows = at("lg_rows", [NG + EXPERTS, T], F32, s_at + 8192)
        mem_junk = at("mem_junk", [P, D], F32, kT_at + 4096)
        x2 = at("x2", [P, NT, D], F32, ch_at)
        xn = [at(f"xn{i}", [P, D], F32, ch_at + 20480 + 4096 * i) for i in range(3)]
        ffn_g = at("ffn_g", [P, D], F32, g2_at)
        fin_g = at("fin_g", [P, D], F32, g1_at)
        r_at = [glu_at]

        def route(name, shape, dt=F32):
            o = r_at[0]
            r_at[0] += (4 * int(np.prod(shape[1:])) + 31) // 32 * 32
            assert r_at[0] <= kT_at
            return at(name, shape, dt, o)

        r_bias = route("r_bias", [P, NG + EXPERTS])
        logits = route("logits", [P, NT, NG + EXPERTS])
        prio = route("prio", [P, 8])
        e_num = route("e_num", [P, EXPERTS])
        valid = route("valid", [P, NT])
        g_max = route("g_max", [P, NT])
        g_ex = route("g_ex", [P, NT, NG])
        g_sum = route("g_sum", [P, NT])
        g_sel = route("g_sel", [P, NT, NG])
        e_all = route("e_all", [P, NT, NG, NE])
        e_sel = route("e_sel", [P, NT, NE])
        e_max = route("e_max", [P, 2, NT])
        e_tmp = route("e_tmp", [P, NT, NE])
        e_one = route("e_one", [P, 2, NT, NE])
        e_m = route("e_m", [P, NT])
        who = [route(f"who{i}", [P, NT, EXPERTS]) for i in range(2)]
        both = route("both", [P, NT, EXPERTS])
        ptmp = route("ptmp", [P, NT, EXPERTS])
        place = route("place", [P, 2, NT])
        place_i = route("place_i", [P, 2, NT], I32)
        ident_no = route("ident_no", [P, 2, NT], I32)
        w_ex = route("w_ex", [P, 3, NT])
        c_max = route("c_max", [P, 2])
        full_f = route("full_f", [P, LIST_ROWS // P, EXPERTS])

        raw_e = ([raw[(len(STREAM) + m) % RAW] for m in range(RAW)] + [at("raw_e4", [P, CHUNK], F32, extra_at),
                                                                       at("raw_e5", [P, CHUNK], F32, xh_at)])
        xe = [at(f"xe{i}", [P, D], F32, xh_at + SLOT_BYTES + 4096 * i) for i in range(2)]
        xeH = [at(f"xeH{i}", [P, KT_D, P], F32R, (xl_at, x_at)[i]) for i in range(2)]
        xeL = [at(f"xeL{i}", [P, KT_D, P], F32R, (xl_at, x_at)[i] + 4096) for i in range(2)]
        ye = [at(f"ye{i}", [P, D], F32, xl_at + SLOT_BYTES + 4096 * i) for i in range(2)]
        e_h = w_h + [at("e_h2", [P, CHUNK], F32R, kT_at)]
        e_l = w_l + [at("e_l2", [P, CHUNK], F32R, v_at)]
        silu = at("silu", [P, FF], F32, s_at)
        gated = at("gated", [P, FF], F32, s_at + 1024)
        aH = at("aH", [P, 2, P], F32R, s_at + 2048)
        aL = at("aL", [P, 2, P], F32R, s_at + 3072)
        yr = [at(f"yr{i}", [P, 2, D], F32, (raw_at + [extra_at])[i]) for i in range(NT)]
        yo = [at(f"yo{i}", [P, D], F32, hl_at[0] + 4096 * i) for i in range(NT)]
        sq_junk = at("sq_junk", [P, D], F32, hl_at[0] + 4096 * NT)

        ps = [ctx.enter_context(nc.psum_tensor(f"ps{i}", [P, 2, 512], F32)) for i in range(4)]
        mm = ps[0:2]
        tv = [ps[2][:, b, :] for b in range(2)]
        ta = [ps[3][:, b, :] for b in range(2)]

        landed = [sem(f"landed{i}") for i in range(RAW)]
        params_in = sem("params_in")
        consts_in = sem("consts_in")
        rows_in = sem("rows_in")
        pool_made = sem("pool_made")
        dve_made = sem("dve_made")
        h_ready = sem("h_ready")
        l_ready = sem("l_ready")
        mm_ready = sem("mm_ready")
        mm_used = sem("mm_used")
        tv_ready = sem("tv_ready")
        tv_used = sem("tv_used")
        ta_ready = sem("ta_ready")
        ta_used = sem("ta_used")
        own = sem("own")
        xh_ready = sem("xh_ready")
        xl_ready = sem("xl_ready")
        sq_ready = sem("sq_ready")
        sq_added = sem("sq_added")
        rs_root = sem("rs_root")
        rs_ready = sem("rs_ready")
        z_act = sem("z_act")
        glu_ready = sem("glu_ready")
        conv_v = sem("conv_v")
        tap_scaled = sem("tap_scaled")
        conv_p = sem("conv_p")
        convs_done = sem("convs_done")
        v_mean = sem("v_mean")
        v_root = sem("v_root")
        v_norm = sem("v_norm")
        v_ready = sem("v_ready")
        v_scaled = sem("v_scaled")
        a_ready = sem("a_ready")
        ttr_done = sem("ttr_done")
        mem_sq = sem("mem_sq")
        k_stored = [sem(f"k_stored{i}") for i in range(2)]
        tail_stored = sem("tail_stored")
        gmv_stored = sem("gmv_stored")
        vm_stored = sem("vm_stored")
        m_mean = sem("m_mean")
        m_root = sem("m_root")
        masked = sem("masked")
        pick_made = sem("pick_made")
        route_made = sem("route_made")
        c_mean = sem("c_mean")
        c_root = sem("c_root")
        cn_ready = sem("cn_ready")
        p_max = sem("p_max")
        p_exp = sem("p_exp")
        p_ready = sem("p_ready")
        v_half = sem("v_half")
        v_both = sem("v_both")
        v_added = sem("v_added")
        os_ready = sem("os_ready")
        col_made = sem("col_made")
        s_max = sem("s_max")
        s_exp = sem("s_exp")
        s_norm = sem("s_norm")
        s_ready = sem("s_ready")
        oh_ready = sem("oh_ready")
        r_in = sem("r_in")
        r_w_in = sem("r_w_in")
        rg_ready = sem("rg_ready")
        r_root = sem("r_root")
        r_ready = sem("r_ready")
        xn_ready = sem("xn_ready")
        xn_stored = [sem(f"xn_stored{i}") for i in range(3)]
        g_exp = sem("g_exp")
        g_dif = sem("g_dif")
        who_ready = sem("who_ready")
        place_ready = sem("place_ready")
        pass_ready = sem("pass_ready")
        list_made = sem("list_made")
        list_in = sem("list_in")
        gids_ready = sem("gids_ready")
        xe_zero = sem("xe_zero")
        out_stored = sem("out_stored")
        e_landed = [sem(f"e_landed{i}") for i in range(6)]
        eh_ready = [sem(f"eh_ready{r}") for r in range(3)]
        el_ready = [sem(f"el_ready{r}") for r in range(3)]
        e_used = sem("e_used")
        gi_made = [sem(f"gi_made{i}") for i in range(2)]
        si_made = [sem(f"si_made{i}") for i in range(2)]
        xe_landed = [sem(f"xe_landed{i}") for i in range(2)]
        xt_done = sem("xt_done")
        xeh_ready = sem("xeh_ready")
        xel_ready = sem("xel_ready")
        hid_ready = sem("hid_ready")
        silu_ready = sem("silu_ready")
        gated_ready = sem("gated_ready")
        at_done = sem("at_done")
        ah_ready = sem("ah_ready")
        al_ready = sem("al_ready")
        y_done = sem("y_done")
        ya_ready = sem("ya_ready")
        yv_ready = sem("yv_ready")
        y_stored = [sem(f"y_stored{i}") for i in range(2)]
        pool_waits = sem("pool_waits")
        sp_waits = sem("sp_waits")
        yr_in = [sem(f"yr_in{i}") for i in range(NT)]
        y_sum = sem("y_sum")
        y_sq = sem("y_sq")
        y_ms = sem("y_ms")
        y_root = sem("y_root")
        y_scaled = sem("y_scaled")
        y_out = [sem(f"y_out{i}") for i in range(NT)]
        y_saved = sem("y_saved")
        fg_in = sem("fg_in")

        def raw_in(eng, key):
            c = AT[key]
            eng.wait_ge(landed[c % RAW], 16 * (c // RAW + 1))
            return raw[c % RAW]

        w2d = {k: a[k][0] for k in ("w_in", "w_out", "xa_wq", "xa_wk", "xa_wv", "xa_wo")}
        SOURCE = {"w_in": w2d["w_in"], "wk": w2d["xa_wk"], "wv": w2d["xa_wv"], "w_out": w2d["w_out"],
                  "wq": w2d["xa_wq"], "wo": w2d["xa_wo"]}
        w1 = a["exp_w1"][0].rearrange("g e (p k) f -> (g e) p k f", k=KT_D)
        w3 = a["exp_w3"][0].rearrange("g e (p k) f -> (g e) p k f", k=KT_D)
        w2 = a["exp_w2"][0].rearrange("g e (p k) f -> (g e) p (k f)", k=2)

        def vc_free(eng, s):
            eng.wait_ge(v_both, s + 1)

        block = ctx.enter_context(nc.Block())

        @block.sync
        def _(sp):
            def load(c):
                kind, i = STREAM[c]
                slot = raw[c % RAW]
                if c >= RAW:
                    was, wi = STREAM[c - RAW]
                    if was == "x":
                        sp.wait_ge(tv_ready, TV_AT[f"x{2 * wi + 1}"] + 1)
                        sp.wait_ge(ta_ready, TA_AT[f"x{2 * wi + 1}"] + 1)
                    elif was == "mem":
                        sp.wait_ge(tv_ready, TV_AT["mem3"] + 1)
                        sp.wait_ge(mem_sq, 2)
                    elif was == "kc":
                        sp.wait_ge(tv_used, TV_AT[f"qb{wi}1"] + 1)
                    elif was == "vc":
                        vc_free(sp, wi)
                    else:
                        sp.wait_ge(l_ready, W_AT[(was, wi)] + 1)
                if kind == "x":
                    src = a["x_prompt"][0].rearrange("(c t p) d -> c p t d", c=2, p=P)[i]
                elif kind == "mem":
                    src = a["mem_prompt"][0].rearrange("(t p) d -> p t d", p=P)
                elif kind in ("kc", "vc"):
                    src = a["cache_mem_k" if kind == "kc" else "cache_mem_v"][0, i].rearrange(
                        "(t p) h d -> p t (h d)", p=P)
                else:
                    col = W_IN_COLS[i] if kind == "w_in" else 256 * i
                    src = SOURCE[kind][:, col:col + 256].rearrange("(k p) n -> p k n", p=P)
                w = src.shape[2]
                sp.dma_start(slot[:].rearrange("p (t w) -> p t w", w=w), src).then_inc(landed[c % RAW], 16)

            for c in range(len(STREAM)):
                load(c)
                if c == 1:
                    sp.dma_start(conv_sample[0, :, 0:PAST - 1, :], a["cache_conv"][0, :, 1:PAST, :]).then_inc(out_stored, 16)
                if c == 16:
                    sp.wait_ge(ta_used, TA_AT["tail"] + 1)
                    sp.dma_start(conv_prompt[0, 0], tail[0:PAST, :]).then_inc(tail_stored, 16)
                    sp.dma_start(conv_sample[0, :, PAST - 1, :], tail[PAST:PAST + NS, :]).then_inc(tail_stored, 16)
                if c == 18:
                    sp.wait_ge(v_ready, NT)
                    sp.dma_start(gmv_prompt[0, 0], v_tok[:, 3, :]).then_inc(gmv_stored, 16)
                    sp.dma_start(gmv_sample[0, :, 0, :], v_s[0:NS, :]).then_inc(gmv_stored, 16)
                if 17 <= c < 21:
                    h = c - 17
                    sp.wait_ge(mm_used, MM_AT[("wk", 2 * h + 1)] + 1)
                    sp.dma_start(mem_k_out[0, 0, :, h, :].rearrange("(t p) d -> p t d", p=P),
                                 zt[h % 2][:, 0:2 * XH_DIM].rearrange("p (t d) -> p t d", t=2)).then_inc(k_stored[h % 2], 16)
                if c == 24:
                    sp.wait_ge(mm_used, MM_AT[("wv", 7)] + 1)
                    sp.dma_start(mem_v_out[0, 0].rearrange("(t p) h d -> p t (h d)", p=P), vm[:]).then_inc(vm_stored, 16)

            def wait(s, value):
                sp.wait_ge(s, value)
                sp.sem_inc(sp_waits, 1)

            def load_expert(q, e, j, first):
                for r in range(3):
                    m = 3 * j + r
                    if first:
                        if m < RAW:
                            was, wi = STREAM[len(STREAM) - RAW + m]
                            if was == "vc":
                                vc_free(sp, wi)
                            else:
                                sp.wait_ge(l_ready, W_AT[(was, wi)] + 1)
                        elif m == RAW:
                            sp.wait_ge(conv_p, CONV_P - 2)
                        else:
                            sp.wait_ge(mm_ready, len(MM_ORDER))
                    else:
                        wait(el_ready[r], q - 1)
                    if r < 2:
                        dst = raw_e[m][:].rearrange("p (k w f) -> p k w f", k=4, w=2)
                        for n, src in enumerate((w1, w3)):
                            sp.dma_start(dst[:, :, n, :], src[bass.ds(e, 1), :, 4 * r:4 * r + 4, :].rearrange(
                                "o p k f -> p (o k) f")).then_inc(e_landed[m], 16)
                    else:
                        sp.dma_start(raw_e[m][:].rearrange("p (o f) -> p o f", o=1),
                                     w2[bass.ds(e, 1)].rearrange("o p f -> p o f")).then_inc(e_landed[m], 16)

            for j in range(2):
                load_expert(j, j, j, True)
            for j, (t0, n) in enumerate(TILES):
                sp.wait_ge(xn_ready, j + 1)
                sp.dma_start(xn_rows[t0:t0 + n, :], xn[j % 3][0:n]).then_inc(xn_stored[j % 3], 16)
            sp.wait_ge(pass_ready, 1)
            extra = sp.value_load(more[0:1, 0:1], min_val=0, max_val=LIST_ROWS // P - 1)
            with sp.Fori(1, extra * (EXPERTS // 2) + EXPERTS // 2) as it:
                for j in range(2):
                    load_expert(2 * it + j, (2 * it + j) & (EXPERTS - 1), j, False)

            for i in range(2):
                wait(y_stored[i], extra * (EXPERTS // 2 * 16) + (EXPERTS // 2 + 1) * 16)
            rows = y_rows.rearrange("(t k) d -> t k d", k=2)
            for t, (t0, n) in enumerate(TILES):
                sp.dma_start(yr[t][0:n], rows[t0:t0 + n]).then_inc(yr_in[t], 16)
            for t, (t0, n) in enumerate(TILES):
                sp.wait_ge(y_out[t], 1)
                dst = y_prompt[0, t0:t0 + n, :] if t < 4 else y_sample[:, 0, :]
                sp.dma_start(dst, yo[t][0:n]).then_inc(y_saved, 16)
            sp.wait_ge(y_saved, 16 * NT)
            sp.wait_ge(out_stored, 16)
            sp.wait_ge(tail_stored, 32)
            sp.wait_ge(gmv_stored, 32)
            sp.wait_ge(vm_stored, 16)
            for i in range(2):
                sp.wait_ge(k_stored[i], 32)

        @block.scalar
        def _(act):
            for name, key in (("mix_g", "norm_mix_g"), ("mem_g", "norm_mem_g"), ("xa_g", "norm_xa_g"),
                              ("ffn_g", "norm_ffn_g"), ("conv_b", "conv_b"), ("cv_g", "cv_ln_g"), ("cv_b", "cv_ln_b")):
                src = a[key][0].rearrange("(r p) -> r p", p=P)
                act.dma_start(rows_a[ROWS_A[name]:ROWS_A[name] + src.shape[0], :], src).then_inc(params_in, 16)
            act.dma_start(rows_b[:], a["conv_w"][0].rearrange("k (i p) -> (k i) p", p=P)).then_inc(params_in, 16)
            act.dma_start(xs_rows[:], a["x_sample"][:, 0, :]).then_inc(params_in, 16)
            act.dma_start(ws_rows[:], a["gm_ws"][0].rearrange("h i j -> i h j")).then_inc(rows_in, 16)
            act.dma_start(cache_rows[:], a["cache_conv"][0].rearrange("(c s) k w -> (s k) c w", c=2)).then_inc(rows_in, 16)
            for dst, src in ((bs_all[:], a["gm_bs"]), (ln_g[:].rearrange("p (h c) -> p h c", h=HEADS), a["gm_ln_g"]),
                             (ln_b[:].rearrange("p (h c) -> p h c", h=HEADS), a["gm_ln_b"])):
                act.dma_start(dst, src[0:1].broadcast_to([P, HEADS, P])).then_inc(consts_in, 16)
            act.dma_start(ws00[:], a["gm_ws"][0:1, :, 0, 0].broadcast_to([P, HEADS]),
                          allow_slow_non_contiguous=True).then_inc(consts_in, 16)

            ta_n = [0]

            def take(name):
                assert TA_ORDER[ta_n[0]] == name
                ta_n[0] += 1
                act.wait_ge(ta_ready, ta_n[0])
                return ta[(ta_n[0] - 1) % 2]

            def split_h(n):
                slot = raw_in(act, WEIGHTS[n])
                if n >= 2:
                    act.wait_ge(mm_ready, mm_after(n - 2))
                act.activation(w_h[n % 2][:], slot[:], ACT.Copy).then_inc(h_ready, 1)

            def square(k, n0):
                if n0 + k >= 2:
                    act.wait_ge(sq_added, n0 + k - 1)
                act.activation(zt[k % 2][:], xT[:, k, :], ACT.Square).then_inc(sq_ready, 1)

            def root(n):
                act.wait_ge(tv_used, TV_AT[f"rs{2 * n + 1}"] + 1)
                act.activation(rstd[:], rstd[:], ACT.Sqrt).then_inc(rs_root, 1)

            def products(n0, n1):
                for n in range(n0, n1):
                    i, k = tap_p(n)
                    src = glu[:, i, k:k + SEQ]
                    w = cols_b[:, k, i:i + 1]
                    if k == 0:
                        act.wait_ge(glu_ready, i + 1)
                        b = ROWS_A["conv_b"] + i
                        ins = act.activation(conv[:, i, 0:SEQ], src, ACT.Identity, bias=cols_a[:, b:b + 1], scale=w)
                    else:
                        p = n - min(n // TAPS, 1) - 1
                        if p >= 4:
                            act.wait_ge(conv_p, p - 3)
                        ins = act.activation(scaled[p % 4][:], src, ACT.Copy, scale=w)
                    ins.then_inc(tap_scaled, 1)

            for j, (t0, n) in enumerate(TILES):
                src = take(f"x{j}")
                act.activation(xT[:, 4:8, t0:t0 + n], src.rearrange("p (k t) -> p k t", k=4)[:, :, 0:n],
                               ACT.Copy).then_inc(ta_used, 1)
            split_h(0)
            act.wait_ge(tv_used, TV_AT[f"x{NT - 1}"] + 1)
            act.wait_ge(ta_used, NT)
            for k in range(8):
                act.activation(xH[:, k, :], xT[:, k, :], ACT.Copy,
                               scale=cols_a[:, ROWS_A["mix_g"] + k:ROWS_A["mix_g"] + k + 1]).then_inc(xh_ready, 1)
                square(k, 0)
            split_h(1)
            root(0)

            for n in range(8):
                if n >= 1:
                    split_h(n + 1)
                for m in (2 * n, 2 * n + 1):
                    if m in (2, 3, 6, 7):
                        g = {2: 0, 3: 1, 6: 2, 7: 3}[m]
                        act.wait_ge(mm_used, MM_AT[("w_in", m)] + 1)
                        act.activation(zt[g % 2][:], zt[g % 2][:], ACT.Sigmoid).then_inc(z_act, 1)
                    if m >= 8:
                        i = m - 8
                        act.wait_ge(mm_used, MM_AT[("w_in", m)] + 1)
                        dst = v_raw[:, i, :] if i < 4 else u_act[:, i - 4, :]
                        act.activation(dst, zt[i % 2][:], ACT.Gelu_apprx_tanh).then_inc(z_act, 1)
                    if m == 11:
                        src = take("tail")
                        act.activation(tail[:], src[0:PAST + NS, 0:GM], ACT.Copy).then_inc(ta_used, 1)
                    if m >= 4:
                        products(4 * (m - 4), 4 * (m - 3))

            act.wait_ge(v_mean, 1)
            act.activation(mv[:, :, :, 1], mv[:, :, :, 1], ACT.Sqrt).then_inc(v_root, 1)
            for i in range(4):
                act.wait_ge(tv_ready, TV_AT[f"mem{i}"] + 1)
                src = tv[TV_AT[f"mem{i}"] % 2].rearrange("p (k t) -> p k t", k=2)
                for kk in range(2):
                    k = 2 * i + kk
                    act.activation(xH[:, k, 0:MEM], src[:, kk, :], ACT.Copy,
                                   scale=cols_a[:, ROWS_A["mem_g"] + k:ROWS_A["mem_g"] + k + 1]).then_inc(xh_ready, 1)
            slot = raw_in(act, ("mem", 0))
            for t in range(2):
                if t:
                    act.wait_ge(mem_sq, 1)
                act.activation(mem_junk[:], slot[:, t * D:(t + 1) * D], ACT.Square,
                               accum_out=m_ss[:, t:t + 1]).then_inc(mem_sq, 1)
            act.wait_ge(m_mean, 1)
            act.activation(m_ss[:], m_ss[:], ACT.Sqrt).then_inc(m_root, 1)

            for n in range(8, 16):
                split_h(n + 1)
                products(48 if n == 8 else min(52 + 5 * (n - 9), CONV_P), min(52 + 5 * (n - 8), CONV_P))
                if n == 9:
                    for h in range(4):
                        act.wait_ge(a_ready, h + 1)
                        act.activation(cH[:, h, :], cLf[:, h, :], ACT.Copy).then_inc(xh_ready, 1)
            act.wait_ge(c_mean, 1)
            act.activation(mv[:, :, 0, 1], mv[:, :, 0, 1], ACT.Sqrt).then_inc(c_root, 1)
            for j, (t0, n) in enumerate(TILES):
                src = take(f"cb{j}")
                for i in range(4):
                    last = act.activation(conv[:, i, t0:t0 + n], src[:, i * P:i * P + n], ACT.Silu,
                                          scale=cols_a[:, ROWS_A["cv_g"] + i:ROWS_A["cv_g"] + i + 1],
                                          bias=cols_a[:, ROWS_A["cv_b"] + i:ROWS_A["cv_b"] + i + 1])
                last.then_inc(ta_used, 1)
            act.wait_ge(ta_used, TA_AT[f"cb{NT - 1}"] + 1)
            for i in range(4):
                act.activation(cH[:, 4 + i, :], conv[:, i, :], ACT.Copy).then_inc(xh_ready, 1)

            act.dma_start(router[:, :, 0:NG], a["router_g"][0].rearrange("(k p) g -> p k g", p=P)).then_inc(r_w_in, 16)
            act.dma_start(router[:, :, NG:], a["router_e"][0].rearrange("(k p) g e -> p k (g e)", p=P)).then_inc(r_w_in, 16)
            for n in range(16, 20):
                split_h(n + 1)
                for k in (2 * (n - 16), 2 * (n - 16) + 1):
                    act.wait_ge(mm_used, MM_AT[("w_out", k)] + 1)
                    act.activation(xH[:, k, :], xT[:, k, :], ACT.Copy,
                                   scale=cols_a[:, ROWS_A["xa_g"] + k:ROWS_A["xa_g"] + k + 1]).then_inc(xh_ready, 1)
                    if k == 0:
                        for i in range(2):
                            act.wait_ge(k_stored[i], 32)
                    square(k, 8)
            root(1)
            for n in range(20, 24):
                split_h(n + 1)
            split_h(25)
            for b in range(2):
                src = take(f"qs{b}")
                act.activation(q_s[:, 512 * b:512 * b + 512], src[0:NS, :], ACT.Copy).then_inc(ta_used, 1)
            for j in range(4 + 1):
                if j < 4:
                    act.wait_ge(p_max, j + 1)
                    if j >= 2:
                        act.wait_ge(ta_ready, TA_AT[f"pt{j - 2}1"] + 1)
                    src = mm[MM_AT[("score", j)] % 2]
                    for h in range(HEADS):
                        last = act.activation(probs[j % 2][:, h, :], src[:, h // 2, (h % 2) * MEM:(h % 2 + 1) * MEM],
                                              ACT.Exp, bias=pmax[:, j, h:h + 1], scale=SCALE,
                                              accum_out=psum_p[:, j, h:h + 1])
                    last.then_inc(mm_used, 1)
                if j >= 1:
                    for b in range(2):
                        src = take(f"pt{j - 1}{b}").rearrange("p (h t w) -> p h t w", h=2, t=2)
                        act.activation(pT[:, 2 * b:2 * b + 2, :, (j - 1) * P:j * P], src, ACT.Copy).then_inc(ta_used, 1)
            act.wait_ge(s_max, 1)
            act.activation(s_p[:], s_p[:], ACT.Exp, bias=s_mx[0:NS * HEADS, 1:2], scale=SCALE,
                           accum_out=s_mx[0:NS * HEADS, 2:3]).then_inc(s_exp, 1)
            for h in range(4):
                m = MM_AT[("pv", h)]
                act.wait_ge(mm_ready, m + 1)
                act.activation(xH[:, 2 * h:2 * h + 2, 0:SEQ], mm[m % 2][:], ACT.Copy).then_inc(oh_ready, 1)
            act.wait_ge(tv_used, TV_AT["sp"] + 1)
            for s in range(NS):
                slot = raw_in(act, ("vc", s))
                if s >= 2:
                    act.wait_ge(v_added, s - 1)
                for h in range(HEADS):
                    c = slice(h * XH_DIM, (h + 1) * XH_DIM)
                    last = act.activation(v_part[s % 2][:, c], slot[:, c], ACT.Copy,
                                          scale=s_pT[:, 0, s * HEADS + h:s * HEADS + h + 1])
                last.then_inc(v_half, 1)
            act.wait_ge(tv_ready, TV_AT["or0"] + 1)
            act.activation(o_s[:, 0:512], tv[TV_AT["or0"] % 2][0:NS, :], ACT.Copy).then_inc(os_ready, 1)
            act.wait_ge(tv_ready, TV_AT["so"] + 1)
            act.dma_start(ffn_g[:], a["norm_ffn_g"][0:1, :].broadcast_to([P, D])).then_inc(r_in, 16)
            act.dma_start(fin_g[:], a["final_norm_g"].rearrange("(o d) -> o d", o=1).broadcast_to([P, D])).then_inc(r_in, 16)
            act.dma_start(r_bias[:, 0:NG], a["router_g_b"][0:1, :].broadcast_to([P, NG])).then_inc(r_in, 16)
            act.dma_start(r_bias[:, NG:], a["router_e_b"][0:1].rearrange("o g e -> o (g e)").broadcast_to(
                [P, EXPERTS])).then_inc(r_in, 16)
            act.activation(xH[:, :, SEQ:T], tv[TV_AT["so"] % 2][:, 0:8 * NS].rearrange("p (k s) -> p k s", k=8),
                           ACT.Copy).then_inc(oh_ready, 1)
            for n in range(24, 28):
                if 24 < n < 27:
                    split_h(n + 1)
                for k in (2 * (n - 24), 2 * (n - 24) + 1):
                    act.wait_ge(mm_used, MM_AT[("wo", k)] + 1)
                    square(k, 16)
            act.wait_ge(tv_used, TV_AT["r2"] + 1)
            act.activation(rs5[:], rs5[:], ACT.Sqrt).then_inc(r_root, 1)
            for j, (t0, n) in enumerate(TILES):
                for b in range(2):
                    src = take(f"t{j}{b}")
                    act.activation(x2[0:n, j, 512 * b:512 * b + 512], src[0:n, :], ACT.Copy).then_inc(ta_used, 1)
                if j == 1:
                    act.wait_ge(g_dif, 1)
                    act.activation(g_ex[:], g_ex[:], ACT.Exp).then_inc(g_exp, 1)
                    act.wait_ge(g_dif, 2)
                    act.activation(w_ex[:, 0, :], w_ex[:, 0, :], ACT.Exp).then_inc(g_exp, 1)

            def split_e(q, it, j, r, free):
                act.wait_ge(e_landed[3 * j + r], (it + 1) * (16 * (2 if r < 2 else 1)))
                if free:
                    act.wait_ge((e_used, hid_ready, y_done)[r], q)
                act.activation(e_h[r][:], raw_e[3 * j + r][:], ACT.Copy).then_inc(eh_ready[r], 1)

            def columns_h(q, j):
                act.wait_ge(xt_done, q + 1)
                for b in range(2):
                    last = act.activation(xeH[j][:, 4 * b:4 * b + 4, :], tv[b].rearrange("p (k t) -> p k t", k=4), ACT.Copy)
                last.then_inc(xeh_ready, 1)

            def act_h(q, old=True):
                act.wait_ge(at_done, q + 1)
                if old:
                    act.wait_ge(y_done, q)
                act.activation(aH[:], ta[0][:, 0:2 * P].rearrange("p (k t) -> p k t", k=2), ACT.Copy).then_inc(ah_ready, 1)

            def y_left(q, it, j):
                act.wait_ge(y_done, q + 1)
                act.wait_ge(y_stored[j], it * 16 + 16)
                act.activation(ye[j][:, 0:512], mm[1][:, 0, :], ACT.Copy).then_inc(ya_ready, 1)

            def step(q, it, j, first, last):
                before, after = it if j else it - 1, it if j == 0 else it + 1
                if not first:
                    y_left(q - 2, it - 1, j)
                if not (first and j == 0):
                    split_e(q - 1, before, 1 - j, 2, not first)
                    act_h(q - 1, not first)
                if not (last and j == 1):
                    split_e(q + 1, after, 1 - j, 0, True)
                    columns_h(q + 1, 1 - j)
                act.wait_ge(hid_ready, q + 1)
                if not (first and j == 0):
                    act.wait_ge(gated_ready, q)
                act.activation(silu[:], mm[0][:, j, 0:FF], ACT.Silu).then_inc(silu_ready, 1)
                if not (last and j == 1):
                    split_e(q + 1, after, 1 - j, 1, True)

            act.wait_ge(mm_ready, len(MM_ORDER))
            act.wait_ge(vm_stored, 16)
            for r in range(2):
                split_e(0, 0, 0, r, False)
            columns_h(0, 0)
            for j in range(2):
                step(j, 0, j, True, False)
            act.wait_ge(pass_ready, 1)
            extra = act.value_load(more[0:1, 0:1], min_val=0, max_val=LIST_ROWS // P - 1)
            last_it = extra * (EXPERTS // 2) + (EXPERTS // 2 - 1)
            with act.Fori(1, last_it) as it:
                for j in range(2):
                    step(it * 2 + j, it, j, False, False)
            for j in range(2):
                step(last_it * 2 + j, last_it, j, False, True)
            y_left(last_it * 2, last_it, 0)
            split_e(last_it * 2 + 1, last_it, 1, 2, True)
            act_h(last_it * 2 + 1)
            y_left(last_it * 2 + 1, last_it, 1)

            for t, (t0, n) in enumerate(TILES):
                act.wait_ge(y_sum, t + 1)
                if t:
                    act.wait_ge(y_sq, t)
                act.activation(sq_junk[0:n], x2[0:n, t, :], ACT.Square, accum_out=fin_ss[0:n, t:t + 1]).then_inc(y_sq, 1)
                act.wait_ge(y_ms, 2 * t + 1)
                act.activation(fin_ss[0:n, t:t + 1], fin_ss[0:n, t:t + 1], ACT.Sqrt).then_inc(y_root, 1)
                act.wait_ge(y_ms, 2 * t + 2)
                act.activation(yo[t][0:n], x2[0:n, t, :], ACT.Copy, scale=fin_ss[0:n, t:t + 1]).then_inc(y_scaled, 1)

        @block.vector
        def _(dve):
            own_n = [0]

            def link(ins):
                own_n[0] += 1
                ins.then_inc(own, 1)
                dve.wait_ge(own, own_n[0])

            tv_n = [0]

            def take(name):
                assert TV_ORDER[tv_n[0]] == name, (name, TV_ORDER[tv_n[0]])
                tv_n[0] += 1
                dve.wait_ge(tv_ready, tv_n[0])
                return tv[(tv_n[0] - 1) % 2]

            def split_l(n):
                dve.wait_ge(h_ready, n + 1)
                slot = raw_in(dve, WEIGHTS[n])
                if n >= 2:
                    dve.wait_ge(mm_ready, mm_after(n - 2))
                dve.tensor_tensor(w_l[n % 2][:], slot[:], w_h[n % 2][:].bitcast(F32), ALU.subtract).then_inc(l_ready, 1)

            def mm_take(key):
                m = MM_AT[key]
                dve.wait_ge(mm_ready, m + 1)
                return mm[m % 2]

            def mean(n):
                for b in range(2):
                    src = take(f"rs{2 * n + b}")
                    dve.tensor_scalar(rstd[:, b, :], src[:, 0:HT], 1.0 / D, EPS, ALU.mult, ALU.add).then_inc(tv_used, 1)
                dve.wait_ge(rs_root, n + 1)
                dve.reciprocal(rstd[:], rstd[:]).then_inc(rs_ready, 1)
                dve.wait_ge(rs_ready, n + 1)

            dve.memset(ones[:], 1.0).then_inc(dve_made, 1)
            dve.memset(mv[:], 1.0).then_inc(dve_made, 1)
            dve.memset(rs5[:], 1.0).then_inc(dve_made, 1)
            for j, (t0, n) in enumerate(TILES):
                if j == NT - 1:
                    src = take("cols_a")
                    dve.tensor_copy(cols_a[:], src[:, 0:N_ROWS_A]).then_inc(tv_used, 1)
                    src = take("cols_b")
                    dve.tensor_copy(cols_b[:].rearrange("p k i -> p (k i)"), src[:, 0:N_ROWS_B]).then_inc(tv_used, 1)
                src = take(f"x{j}")
                dve.tensor_copy(xT[:, 0:4, t0:t0 + n],
                                src.rearrange("p (k t) -> p k t", k=4)[:, :, 0:n]).then_inc(tv_used, 1)
            dve.memset(glu[:, :, 0:PAST], 0.0).then_inc(dve_made, 1)
            split_l(0)
            dve.wait_ge(tv_used, TV_AT[f"x{NT - 1}"] + 1)
            dve.wait_ge(ta_used, NT)

            def moving_l(k, n_h, row):
                dve.wait_ge(xh_ready, n_h)
                g = ROWS_A[row] + k
                dve.scalar_tensor_tensor(xL[:, k, :], xT[:, k, :], cols_a[:, g:g + 1], xH[:, k, :].bitcast(F32),
                                         ALU.mult, ALU.subtract).then_inc(xl_ready, 1)

            for k in range(8):
                moving_l(k, k + 1, "mix_g")
            split_l(1)
            mean(0)

            def taps(first, last):
                for n in range(first, min(last, CONV_V)):
                    i, k = 2 * (n // TAPS), n % TAPS
                    w = cols_b[:, k, i:i + 1]
                    src = glu[:, i, k:k + SEQ]
                    if k == 0:
                        dve.wait_ge(glu_ready, i + 1)
                        b = ROWS_A["conv_b"] + i
                        ins = dve.tensor_scalar(conv[:, i, 0:SEQ], src, w, cols_a[:, b:b + 1], ALU.mult, ALU.add)
                    else:
                        dve.wait_ge(conv_v, n)
                        ins = dve.scalar_tensor_tensor(conv[:, i, 0:SEQ], src, w, conv[:, i, 0:SEQ], ALU.mult, ALU.add)
                    ins.then_inc(conv_v, 1)

            def samples_conv(i):
                w = cols_b[:, :, i].rearrange("p (o k) -> p o k", o=1).broadcast_to([P, NS, TAPS])
                link(dve.tensor_copy(conv_s[:, i, :, PAST], glu[:, i, PAST + SEQ:PAST + T]))
                link(dve.tensor_tensor(conv_s[:, i], conv_s[:, i], w, ALU.mult))
                link(dve.tensor_reduce(conv[:, i, SEQ:T], conv_s[:, i], AX_X, ALU.add))
                b = ROWS_A["conv_b"] + i
                dve.tensor_scalar(conv[:, i, SEQ:T], conv[:, i, SEQ:T], cols_a[:, b:b + 1], None, ALU.add).then_inc(convs_done, 1)

            def gate(g):
                dve.wait_ge(z_act, g + 1)
                dve.wait_ge(mm_used, MM_AT[("w_in", LINEAR[g])] + 1)
                dve.tensor_tensor(glu[:, g, PAST:PAST + T], glu[:, g, PAST:PAST + T], zt[g % 2][:],
                                  ALU.mult).then_inc(glu_ready, 1)

            LINEAR, GATES = (0, 1, 4, 5), (2, 3, 6, 7)

            for n in range(8):
                if n >= 1:
                    split_l(n + 1)
                for m in (2 * n, 2 * n + 1):
                    src = mm_take(("w_in", m))[:, :, 0:HT]
                    if m in LINEAR:
                        if m == 0:
                            dve.wait_ge(dve_made, 4)
                        dst = glu[:, LINEAR.index(m), PAST:PAST + T]
                    else:
                        c = GATES.index(m) if m in GATES else m - 4
                        if 2 <= c < 6:
                            dve.wait_ge(glu_ready, c - 1)
                        if c >= 6:
                            dve.wait_ge(z_act, c - 1)
                        dst = zt[c % 2][:]
                    dve.tensor_tensor(dst.rearrange("p (b t) -> p b t", b=2), src, rstd[:], ALU.mult).then_inc(mm_used, 1)
                    if m - 1 in GATES:
                        gate(GATES.index(m - 1))
                    if m == 1:
                        src = take("ws")
                        dve.wait_ge(consts_in, 16 * 4)
                        dve.tensor_copy(wsT[:].rearrange("p h i -> p (h i)"), src).then_inc(tv_used, 1)
                        for c in range(2):
                            src = take(f"cc{c}")
                            dve.tensor_copy(conv_s[:, :, 4 * c:4 * c + 4, 0:PAST],
                                            src[:, 0:16 * PAST].rearrange("p (i s k) -> p i s k", i=4, s=4)).then_inc(tv_used, 1)
                    if m >= 5:
                        taps(3 * (m - 5), 3 * (m - 4))
                    if m >= 12:
                        for j in ((0, 1), (2, 3), (4,), ())[m - 12]:
                            t0, n_t = TILES[j]
                            src = take(f"v{j}")[0:n_t]
                            dve.tensor_copy(v_tok[:, j, :] if j < 4 else v_s[0:n_t], src)
                            for h in range(HEADS):
                                last = dve.bn_stats(stats[0:n_t, j, h, :], src[:, h * P:(h + 1) * P])
                            last.then_inc(tv_used, 1)
                            dve.wait_ge(tv_used, TV_AT[f"v{j}"] + 1)
                            for h in range(HEADS):
                                last = dve.bn_aggr(mv[0:n_t, j, h, :], stats[0:n_t, j, h, :])
                            link(last)
            dve.tensor_scalar(mv[:, :, :, 1], mv[:, :, :, 1], EPS, None, ALU.add).then_inc(v_mean, 1)
            for i in range(4):
                src = take(f"mem{i}").rearrange("p (k t) -> p k t", k=2)
                for kk in range(2):
                    k = 2 * i + kk
                    dve.wait_ge(xh_ready, 8 + 2 * i + 2)
                    g = ROWS_A["mem_g"] + k
                    last = dve.scalar_tensor_tensor(xL[:, k, 0:MEM], src[:, kk, :], cols_a[:, g:g + 1],
                                                    xH[:, k, 0:MEM].bitcast(F32), ALU.mult, ALU.subtract)
                last.then_inc(tv_used, 1)
            dve.wait_ge(v_root, 1)
            link(dve.reciprocal(mv[:, :, :, 1], mv[:, :, :, 1]))
            for j, (t0, n_t) in enumerate(TILES):
                for h in range(HEADS):
                    row = (v_tok[:, j, :] if j < 4 else v_s[0:n_t])[:, h * P:(h + 1) * P]
                    last = dve.tensor_scalar(row, row, mv[0:n_t, j, h, 0:1], mv[0:n_t, j, h, 1:2], ALU.subtract, ALU.mult)
                last.then_inc(v_norm, 1)

            dve.wait_ge(mem_sq, 2)
            dve.tensor_scalar(m_ss[:], m_ss[:], 1.0 / D, EPS, ALU.mult, ALU.add).then_inc(m_mean, 1)
            dve.wait_ge(m_root, 1)
            link(dve.reciprocal(m_ss[:], m_ss[:]))

            def keys_in(h):
                src = take(f"kt{h}")
                if h == 0:
                    dve.wait_ge(tail_stored, 32)
                dve.tensor_copy(kT[:, 2 * h:2 * h + 2, :], src.rearrange("p (k t) -> p k t", k=2)).then_inc(tv_used, 1)

            def gated_mix(h):
                src = take(f"mix{h}")
                bias = bs_all[:, h:h + 1, :].broadcast_to([P, 4, P])
                tmp = sumsq[:, 0:SEQ]
                dve.tensor_tensor(tmp.rearrange("p (c t) -> p c t", c=4), src.rearrange("p (c t) -> p c t", c=4),
                                  bias, ALU.add).then_inc(tv_used, 1)
                dve.wait_ge(tv_used, TV_AT[f"mix{h}"] + 1)
                dve.wait_ge(z_act, 8 + h + 1)
                link(dve.tensor_tensor(u_act[:, h, 0:SEQ], u_act[:, h, 0:SEQ], tmp, ALU.mult))
                dve.tensor_tensor(u_act[:, h, SEQ:T], u_act[:, h, SEQ:T], vsT[:, h, :], ALU.mult).then_inc(a_ready, 1)

            for n in range(8, 16):
                split_l(n + 1)
                for t in range(2):
                    m = 2 * (n - 8) + t
                    if n < 12:
                        h = n - 8
                        src = mm_take(("wk", m))
                        if h >= 2 and t == 0:
                            dve.wait_ge(k_stored[h % 2], 16)
                            dve.wait_ge(tv_ready, TV_AT[f"kt{h - 2}"] + 1)
                        dst = zt[h % 2][:, t * XH_DIM:(t + 1) * XH_DIM]
                    else:
                        src = mm_take(("wv", m - 8))
                        h = n - 12
                        dst = vm[:, t, h * XH_DIM:(h + 1) * XH_DIM]
                        if m == 8:
                            dve.wait_ge(y_stored[0], 16)
                            dve.wait_ge(y_stored[1], 16)
                    dve.tensor_scalar(dst, src[:, 0, 0:MEM], m_ss[:, t:t + 1], None, ALU.mult).then_inc(mm_used, 1)
                    taps(33 + 2 * m, 35 + 2 * m)
                    if m < 4:
                        samples_conv(m)
                if n == 8:
                    src = take("vs")
                    for h in range(HEADS):
                        last = dve.tensor_scalar(vsT[:, h, :], src[:, h * NS:(h + 1) * NS], ws00[:, h:h + 1],
                                                 bs_all[:, h, 0:1], ALU.mult, ALU.add)
                    last.then_inc(tv_used, 1)
                    dve.wait_ge(tv_used, TV_AT["vs"] + 1)
                    for h in range(HEADS):
                        gated_mix(h)
                if n == 9:
                    for h in range(HEADS):
                        dve.wait_ge(xh_ready, 16 + h + 1)
                        dve.tensor_tensor(cL[:, h, :], cLf[:, h, :], cH[:, h, :].bitcast(F32), ALU.subtract).then_inc(xl_ready, 1)
                if 9 <= n < 13:
                    keys_in(n - 9)
            dve.wait_ge(gmv_stored, 32)
            for j, (t0, n_t) in enumerate(TILES):
                src = take(f"cf{j}")[0:n_t]
                dve.tensor_copy(v_tok[:, j, :] if j < 4 else v_s[0:n_t], src)
                dve.bn_stats(stats[0:n_t, j, 0, :], src).then_inc(tv_used, 1)
                dve.wait_ge(tv_used, TV_AT[f"cf{j}"] + 1)
                link(dve.bn_aggr(mv[0:n_t, j, 0, :], stats[0:n_t, j, 0, :]))
            dve.tensor_scalar(mv[:, :, 0, 1], mv[:, :, 0, 1], EPS, None, ALU.add).then_inc(c_mean, 1)
            dve.wait_ge(c_root, 1)
            link(dve.reciprocal(mv[:, :, 0, 1], mv[:, :, 0, 1]))
            for j, (t0, n_t) in enumerate(TILES):
                row = v_tok[:, j, :] if j < 4 else v_s[0:n_t]
                dve.tensor_scalar(row, row, mv[0:n_t, j, 0, 0:1], mv[0:n_t, j, 0, 1:2], ALU.subtract,
                                  ALU.mult).then_inc(cn_ready, 1)
            for i in range(4):
                dve.wait_ge(xh_ready, 20 + i + 1)
                dve.tensor_tensor(cL[:, 4 + i, :], conv[:, i, :], cH[:, 4 + i, :].bitcast(F32), ALU.subtract).then_inc(xl_ready, 1)

            for n in range(16, 20):
                split_l(n + 1)
                for k in (2 * (n - 16), 2 * (n - 16) + 1):
                    src = mm_take(("w_out", k))[:, :, 0:HT]
                    xk = xT[:, k, :].rearrange("p (b t) -> p b t", b=2)
                    dve.tensor_tensor(xk, src, xk, ALU.add).then_inc(mm_used, 1)
                    if k:
                        moving_l(k - 1, 24 + k, "xa_g")
            moving_l(7, 32, "xa_g")
            mean(1)
            dve.wait_ge(r_w_in, 32)
            fg = cols_a[:, ROWS_A["ffn_g"]:ROWS_A["ffn_g"] + 8].rearrange("p (k o) -> p k o", o=1).broadcast_to(
                [P, 8, NG + EXPERTS])
            dve.tensor_tensor(router[:], router[:], fg, ALU.mult).then_inc(rg_ready, 1)
            for n in range(20, 24):
                split_l(n + 1)
                for k in (2 * (n - 20), 2 * (n - 20) + 1):
                    src = mm_take(("wq", k))[:, :, 0:HT]
                    dve.tensor_tensor(qT[:, k, :].rearrange("p (b t) -> p b t", b=2), src, rstd[:], ALU.mult).then_inc(mm_used, 1)
            split_l(25)

            def score_max(j):
                src = mm_take(("score", j))
                link(dve.tensor_reduce(pmax[:, j, :], src[:].rearrange("p b (h m) -> p (b h) m", h=2), AX_X, ALU.max))
                dve.tensor_scalar(pmax[:, j, :], pmax[:, j, :], -SCALE, None, ALU.mult).then_inc(p_max, 1)

            def score_norm(j):
                dve.wait_ge(mm_used, MM_AT[("score", j)] + 1)
                link(dve.reciprocal(psum_p[:, j, :], psum_p[:, j, :]))
                for h in range(HEADS):
                    last = dve.tensor_scalar(probs[j % 2][:, h, :], probs[j % 2][:, h, :], psum_p[:, j, h:h + 1], None, ALU.mult)
                last.then_inc(p_ready, 1)

            def sample_scores(s):
                keys = raw_in(dve, ("kc", s))
                for b in range(2):
                    src = take(f"qb{s}{b}")
                    for h in (2 * b, 2 * b + 1):
                        for t in range(2):
                            if ttr_n[0]:
                                dve.wait_ge(ttr_done, ttr_n[0])
                            last = dve.tensor_tensor_reduce(
                                ttr_out[:], keys[:, t * D + h * XH_DIM:t * D + (h + 1) * XH_DIM],
                                src[:, (h % 2) * XH_DIM:(h % 2 + 1) * XH_DIM], 1.0, 0.0, ALU.mult, ALU.add,
                                s_sc[:, t, s * HEADS + h:s * HEADS + h + 1])
                            if (h, t) != (2 * b + 1, 1):
                                ttr_n[0] += 1
                                last.then_inc(ttr_done, 1)
                    last.then_inc(tv_used, 1)
                    dve.wait_ge(tv_used, TV_AT[f"qb{s}{b}"] + 1)

            ttr_n = [0]
            score_max(0)
            score_max(1)
            for j in range(4):
                score_norm(j)
                sample_scores(2 * j)
                sample_scores(2 * j + 1)
                if j < 2:
                    score_max(j + 2)
            R = NS * HEADS
            src = take("ss")
            dve.tensor_reduce(s_mx[0:R, 0:1], src[0:R, 0:MEM], AX_X, ALU.max)
            dve.tensor_copy(s_p[:], src[0:R, 0:MEM]).then_inc(tv_used, 1)
            dve.wait_ge(tv_used, TV_AT["ss"] + 1)
            dve.tensor_scalar(s_mx[0:R, 1:2], s_mx[0:R, 0:1], -SCALE, None, ALU.mult).then_inc(s_max, 1)
            dve.wait_ge(s_exp, 1)
            link(dve.reciprocal(s_mx[0:R, 3:4], s_mx[0:R, 2:3]))
            dve.tensor_scalar(s_p[:], s_p[:], s_mx[0:R, 3:4], None, ALU.mult).then_inc(s_norm, 1)
            src = take("sp")
            dve.tensor_copy(s_pT[:].rearrange("p t r -> p (t r)"), src[:, 0:2 * R]).then_inc(tv_used, 1)
            for h in range(HEADS):
                m = MM_AT[("pv", h)]
                dve.wait_ge(oh_ready, h + 1)
                dve.tensor_tensor(xL[:, 2 * h:2 * h + 2, 0:SEQ], mm[m % 2][:], xH[:, 2 * h:2 * h + 2, 0:SEQ].bitcast(F32),
                                  ALU.subtract).then_inc(mm_used, 1)
            def sample_values(s):
                slot = raw_in(dve, ("vc", s))
                dve.wait_ge(v_half, s + 1)
                for h in range(HEADS):
                    c = slice(h * XH_DIM, (h + 1) * XH_DIM)
                    last = dve.scalar_tensor_tensor(v_part[s % 2][:, c], slot[:, D + h * XH_DIM:D + (h + 1) * XH_DIM],
                                                    s_pT[:, 1, s * HEADS + h:s * HEADS + h + 1], v_part[s % 2][:, c],
                                                    ALU.mult, ALU.add)
                last.then_inc(v_both, 1)

            for s in range(NS):
                sample_values(s)
            take("or0")
            dve.wait_ge(os_ready, 1)
            dve.tensor_copy(one_junk[:], ones[0:NS, 0:1]).then_inc(tv_used, 1)
            src = take("or1")
            dve.tensor_copy(o_s[:, 512:D], src[0:NS, :]).then_inc(tv_used, 1)
            src = take("so")[:, 0:8 * NS].rearrange("p (k s) -> p k s", k=8)
            dve.wait_ge(oh_ready, 5)
            dve.tensor_tensor(xL[:, :, SEQ:T], src, xH[:, :, SEQ:T].bitcast(F32), ALU.subtract).then_inc(tv_used, 1)
            for n in range(24, 28):
                if 24 < n < 27:
                    split_l(n + 1)
                for k in (2 * (n - 24), 2 * (n - 24) + 1):
                    src = mm_take(("wo", k))[:, :, 0:HT]
                    xk = xT[:, k, :].rearrange("p (b t) -> p b t", b=2)
                    dve.tensor_tensor(xk, src, xk, ALU.add).then_inc(mm_used, 1)
            for b in range(2):
                src = take(f"lg{b}")
                dve.tensor_copy(lg_rows[:, b * HT:(b + 1) * HT], src[0:NG + EXPERTS, 0:HT]).then_inc(tv_used, 1)
            src = take("r2")
            dve.tensor_scalar(rs5[:, 0:4], src[:, 0:4], 1.0 / D, EPS, ALU.mult, ALU.add)
            dve.tensor_scalar(rs5[0:NS, 4:5], src[0:NS, 4:5], 1.0 / D, EPS, ALU.mult, ALU.add).then_inc(tv_used, 1)
            link(dve.memset(logits[:], 0.0))
            dve.wait_ge(r_root, 1)
            link(dve.reciprocal(rs5[:], rs5[:]))
            dve.wait_ge(r_in, 16 * 4)
            W = NG + EXPERTS
            src = take("lg")
            for j, (t0, n_t) in enumerate(TILES):
                last = dve.scalar_tensor_tensor(logits[0:n_t, j, :], src[0:n_t, j * W:(j + 1) * W], rs5[0:n_t, j:j + 1],
                                                r_bias[0:n_t], ALU.mult, ALU.add)
            last.then_inc(tv_used, 1)
            dve.wait_ge(tv_used, TV_AT["lg"] + 1)
            def over(x, w):
                return x.rearrange("p (t o) -> p t o", o=1).broadcast_to([P, NT, w])

            g_log = logits[:, :, 0:NG]
            link(dve.tensor_reduce(g_max[:], g_log, AX_X, ALU.max))
            dve.tensor_tensor(g_ex[:], g_log, over(g_max[:], NG), ALU.subtract).then_inc(g_dif, 1)

            def first_of(out, values, largest, tmp, w):
                dve.wait_ge(route_made, 3)
                pr = prio[:, 8 - w:8].rearrange("p (o w) -> p o w", o=1).broadcast_to([P, NT, w])
                link(dve.tensor_tensor(tmp, values, over(largest, w), ALU.is_equal))
                link(dve.tensor_tensor(tmp, tmp, pr, ALU.mult))
                link(dve.tensor_reduce(e_m[:], tmp, AX_X, ALU.max))
                link(dve.tensor_tensor(out, tmp, over(e_m[:], w), ALU.is_equal))

            first_of(g_sel[:], g_log, g_max[:], e_tmp[:, :, 0:NG], NG)
            e_log = logits[:, :, NG:].rearrange("p t (g e) -> p t g e", g=NG)
            sel4 = g_sel[:].rearrange("p t (g o) -> p t g o", o=1).broadcast_to([P, NT, NG, NE])
            for j in range(NT):
                last = dve.tensor_tensor(e_all[:, j], e_log[:, j], sel4[:, j], ALU.mult)
            link(last)
            link(dve.tensor_reduce(e_sel[:], e_all[:].rearrange("p t g e -> p t e g"), AX_X, ALU.add))
            link(dve.tensor_reduce(e_max[:, 0, :], e_sel[:], AX_X, ALU.max))
            first_of(e_one[:, 0], e_sel[:], e_max[:, 0, :], e_tmp[:], NE)
            link(dve.scalar_tensor_tensor(e_sel[:], e_one[:, 0], -1e30, e_sel[:], ALU.mult, ALU.add))
            link(dve.tensor_reduce(e_max[:, 1, :], e_sel[:], AX_X, ALU.max))
            first_of(e_one[:, 1], e_sel[:], e_max[:, 1, :], e_tmp[:], NE)
            dve.wait_ge(g_exp, 1)
            dve.tensor_tensor(w_ex[:, 0, :], e_max[:, 1, :], e_max[:, 0, :], ALU.subtract).then_inc(g_dif, 1)
            for i in range(2):
                for j in range(NT):
                    one = e_one[:, i, j:j + 1, :].broadcast_to([P, NG, NE])
                    last = dve.tensor_tensor(who[i][:, j, :].rearrange("p (g e) -> p g e", g=NG), one, sel4[:, j], ALU.mult)
                link(last)
            dve.tensor_tensor(both[:], who[0][:], who[1][:], ALU.add).then_inc(who_ready, 1)
            link(dve.tensor_reduce(g_sum[:], g_ex[:], AX_X, ALU.add))
            dve.wait_ge(g_exp, 2)
            link(dve.tensor_scalar(w_ex[:, 1, :], w_ex[:, 0, :], 1.0, None, ALU.add))
            link(dve.tensor_tensor(w_ex[:, 1, :], w_ex[:, 1, :], g_sum[:], ALU.mult))
            link(dve.reciprocal(wgt[:, 0, :], w_ex[:, 1, :]))
            link(dve.tensor_tensor(wgt[:, 1, :], wgt[:, 0, :], w_ex[:, 0, :], ALU.mult))
            src = take("pos")[:, 0:NT * EXPERTS].rearrange("p (t e) -> p t e", t=NT)
            e_b = e_num[:].rearrange("p (o e) -> p o e", o=1).broadcast_to([P, NT, EXPERTS])
            link(dve.tensor_scalar(ptmp[:], src, float(EXPERTS), None, ALU.mult))
            dve.tensor_tensor(ptmp[:], ptmp[:], e_b, ALU.add).then_inc(tv_used, 1)
            dve.wait_ge(tv_used, TV_AT["pos"] + 1)
            for i in range(2):
                link(dve.tensor_tensor(who[i][:], who[i][:], ptmp[:], ALU.mult))
                link(dve.tensor_reduce(place[:, i, :], who[i][:], AX_X, ALU.add))
            dve.tensor_copy(place_i[:], place[:]).then_inc(place_ready, 1)
            src = take("cnt")
            for c in range(LIST_ROWS // P):
                link(dve.tensor_scalar(full_f[:, c, :], src[:, 0:EXPERTS], float(P * c + P // 2), None, ALU.is_gt))
                dve.scalar_tensor_tensor(full_f[:, c, :], src[:, 0:EXPERTS], float(P * c + P // 4), full_f[:, c, :],
                                         ALU.is_gt, ALU.add)
            dve.tensor_reduce(c_max[:, 0:1], src[:, 0:EXPERTS], AX_X, ALU.max).then_inc(tv_used, 1)
            dve.wait_ge(tv_used, TV_AT["cnt"] + 1)
            link(dve.memset(c_max[:, 1:2], 0.0))
            for i in range(1, LIST_ROWS // P):
                link(dve.scalar_tensor_tensor(c_max[:, 1:2], c_max[:, 0:1], float(P * i), c_max[:, 1:2], ALU.is_gt, ALU.add))
            dve.tensor_copy(full[:], full_f[:])
            dve.tensor_copy(more[:], c_max[:, 1:2]).then_inc(pass_ready, 1)
            for j, (t0, n_t) in enumerate(TILES):
                dve.wait_ge(ta_used, TA_AT[f"t{j}1"] + 1)
                if j >= 3:
                    dve.wait_ge(xn_stored[j - 3], 16)
                dve.scalar_tensor_tensor(xn[j % 3][0:n_t], x2[0:n_t, j, :], rs5[0:n_t, j:j + 1], ffn_g[0:n_t],
                                         ALU.mult, ALU.mult).then_inc(xn_ready, 1)
            dve.wait_ge(list_in, 16)
            dve.tensor_scalar(gids[:], ids[:], 1, None, ALU.arith_shift_right).then_inc(gids_ready, 1)

            def split_e(q, it, j, r):
                dve.wait_ge(eh_ready[r], q + 1)
                dve.tensor_tensor(e_l[r][:], raw_e[3 * j + r][:], e_h[r][:].bitcast(F32), ALU.subtract).then_inc(el_ready[r], 1)

            def columns_l(q, j):
                dve.wait_ge(xeh_ready, q + 1)
                for b in range(2):
                    last = dve.tensor_tensor(xeL[j][:, 4 * b:4 * b + 4, :], tv[b].rearrange("p (k t) -> p k t", k=4),
                                             xeH[j][:, 4 * b:4 * b + 4, :].bitcast(F32), ALU.subtract)
                last.then_inc(xel_ready, 1)

            def act_l(q):
                dve.wait_ge(ah_ready, q + 1)
                dve.tensor_tensor(aL[:], ta[0][:, 0:2 * P].rearrange("p (k t) -> p k t", k=2), aH[:].bitcast(F32),
                                  ALU.subtract).then_inc(al_ready, 1)

            def y_right(q, it, j):
                dve.wait_ge(y_done, q + 1)
                dve.wait_ge(y_stored[j], it * 16 + 16)
                dve.tensor_copy(ye[j][:, 512:D], mm[1][:, 1, :]).then_inc(yv_ready, 1)

            def step(q, it, j, first, last):
                before, after = it if j else it - 1, it if j == 0 else it + 1
                if not first:
                    y_right(q - 2, it - 1, j)
                if not (first and j == 0):
                    split_e(q - 1, before, 1 - j, 2)
                    act_l(q - 1)
                if not (last and j == 1):
                    split_e(q + 1, after, 1 - j, 0)
                    columns_l(q + 1, 1 - j)
                dve.wait_ge(silu_ready, q + 1)
                if not (first and j == 0):
                    dve.wait_ge(at_done, q)
                dve.tensor_tensor(gated[:], mm[0][:, j, FF:2 * FF], silu[:], ALU.mult).then_inc(gated_ready, 1)
                if not (last and j == 1):
                    split_e(q + 1, after, 1 - j, 1)

            for r in range(2):
                split_e(0, 0, 0, r)
            columns_l(0, 0)
            for j in range(2):
                step(j, 0, j, True, False)
            extra = dve.value_load(more[0:1, 0:1], min_val=0, max_val=LIST_ROWS // P - 1)
            last_it = extra * (EXPERTS // 2) + (EXPERTS // 2 - 1)
            with dve.Fori(1, last_it) as it:
                for j in range(2):
                    step(it * 2 + j, it, j, False, False)
            for j in range(2):
                step(last_it * 2 + j, last_it, j, False, True)
            y_right(last_it * 2, last_it, 0)
            split_e(last_it * 2 + 1, last_it, 1, 2)
            act_l(last_it * 2 + 1)
            y_right(last_it * 2 + 1, last_it, 1)

            def add_experts(t):
                n = TILES[t][1]
                dve.wait_ge(yr_in[t], 16)
                link(dve.scalar_tensor_tensor(x2[0:n, t, :], yr[t][0:n, 0, :], wgt[0:n, 0, t:t + 1], x2[0:n, t, :],
                                              ALU.mult, ALU.add))
                dve.scalar_tensor_tensor(x2[0:n, t, :], yr[t][0:n, 1, :], wgt[0:n, 1, t:t + 1], x2[0:n, t, :],
                                         ALU.mult, ALU.add).then_inc(y_sum, 1)

            def mean_square(t):
                n = TILES[t][1]
                dve.wait_ge(y_sq, t + 1)
                dve.tensor_scalar(fin_ss[0:n, t:t + 1], fin_ss[0:n, t:t + 1], 1.0 / D, EPS, ALU.mult, ALU.add).then_inc(y_ms, 1)
                dve.wait_ge(y_root, t + 1)
                dve.reciprocal(fin_ss[0:n, t:t + 1], fin_ss[0:n, t:t + 1]).then_inc(y_ms, 1)

            add_experts(0)
            for t, (t0, n) in enumerate(TILES):
                if t + 1 < NT:
                    add_experts(t + 1)
                mean_square(t)
            for t in LAST_BY_DVE:
                n = TILES[t][1]
                dve.wait_ge(y_scaled, t + 1)
                dve.tensor_tensor(yo[t][0:n], yo[t][0:n], fin_g[0:n], ALU.mult).then_inc(y_out[t], 1)

        @block.tensor
        def _(pe):
            tv_n, ta_n = [0], [0]

            def open_tv(name):
                assert TV_ORDER[tv_n[0]] == name, (name, TV_ORDER[tv_n[0]])
                if tv_n[0] >= 2:
                    pe.wait_ge(tv_used, tv_n[0] - 1)
                tv_n[0] += 1
                return tv[(tv_n[0] - 1) % 2]

            def open_ta(name):
                assert TA_ORDER[ta_n[0]] == name, (name, TA_ORDER[ta_n[0]])
                if ta_n[0] >= 2:
                    pe.wait_ge(ta_used, ta_n[0] - 1)
                ta_n[0] += 1
                return ta[(ta_n[0] - 1) % 2]

            def open_mm(key):
                m = MM_AT[key]
                if m >= 2:
                    pe.wait_ge(mm_used, m - 1)
                return mm[m % 2]

            def turn(out, src, n=P):
                return pe.transpose(out, src, ident[0:n, 0:n])

            def three(out, h1, l1, h2, l2, start, stop):
                pe.matmul(out, h1, h2, start=start, stop=False)
                pe.matmul(out, l1, h2, start=False, stop=False)
                return pe.matmul(out, h1, l2, start=False, stop=stop)

            def project(kind, i, mH, mL, ready=None):
                key = (kind, i // 2)
                n = W_AT[key]
                pe.wait_ge(l_ready, n + 1)
                out = open_mm((kind, i))
                wh = w_h[n % 2][:].rearrange("p (k c) -> p k c", k=8)
                wl = w_l[n % 2][:].rearrange("p (k c) -> p k c", k=8)
                c = slice((i % 2) * P, (i % 2 + 1) * P)
                for k in range(8):
                    if ready:
                        ready(k)
                    for b in range(2):
                        tok = slice(b * HT, (b + 1) * HT)
                        last = three(out[:, b, 0:HT], wh[:, k, c], wl[:, k, c], mH[:, k, tok], mL[:, k, tok],
                                     k == 0, k == 7)
                last.then_inc(mm_ready, 1)

            def sums(n):
                pe.wait_ge(sq_added, 8 * (n + 1))
                for b in range(2):
                    out = open_tv(f"rs{2 * n + b}")
                    pe.matmul(out[:, 0:HT], ones[:], sumsq[:, b * HT:(b + 1) * HT], start=True, stop=True).then_inc(tv_ready, 1)

            pe.wait_ge(pool_made, 2)
            pe.wait_ge(dve_made, 1)
            for j, (t0, n) in enumerate(TILES):
                if j == NT - 1:
                    pe.wait_ge(params_in, 16 * 9)
                    out = open_tv("cols_a")
                    turn(out[:, 0:N_ROWS_A], rows_a[:], N_ROWS_A).then_inc(tv_ready, 1)
                    out = open_tv("cols_b")
                    turn(out[:, 0:N_ROWS_B], rows_b[:], N_ROWS_B).then_inc(tv_ready, 1)
                src = xs_rows[:] if j == NT - 1 else raw_in(pe, ("x", j // 2))[:, (j % 2) * D:(j % 2 + 1) * D]
                for half, (openb, done) in enumerate(((open_tv, tv_ready), (open_ta, ta_ready))):
                    out = openb(f"x{j}")
                    for k in range(4):
                        c = (4 * half + k) * P
                        last = turn(out[:, k * P:k * P + n], src[:, c:c + P], n)
                    last.then_inc(done, 1)

            for m in range(16):
                project("w_in", m, xH, xL, (lambda k: pe.wait_ge(xl_ready, k + 1)) if m == 0 else None)
                if m == 1:
                    sums(0)
                    pe.wait_ge(masked, 1)
                    out = open_tv("ws")
                    for h in range(HEADS):
                        last = turn(out[:, h * P:(h + 1) * P], ws_rows[:, h, :])
                    last.then_inc(tv_ready, 1)
                    pe.wait_ge(rows_in, 32)
                    for c in range(2):
                        out = open_tv(f"cc{c}")
                        for i in range(4):
                            last = turn(out[:, i * 4 * PAST:(i + 1) * 4 * PAST], cache_rows[:, c, i * P:(i + 1) * P], 4 * PAST)
                        last.then_inc(tv_ready, 1)
                if m == 10:
                    pe.wait_ge(glu_ready, 4)
                    out = open_ta("tail")
                    for i in range(4):
                        last = turn(out[0:PAST + NS, i * P:(i + 1) * P], glu[:, i, SEQ:PAST + T])
                    last.then_inc(ta_ready, 1)
                if m >= 12:
                    if m == 12:
                        pe.wait_ge(z_act, 8)
                    for j in ((0, 1), (2, 3), (4,), ())[m - 12]:
                        t0, n = TILES[j]
                        out = open_tv(f"v{j}")
                        for i in range(4):
                            last = turn(out[0:n, i * P:(i + 1) * P], v_raw[:, i, t0:t0 + n])
                        last.then_inc(tv_ready, 1)
            slot = raw_in(pe, ("mem", 0))
            for i in range(4):
                out = open_tv(f"mem{i}")
                for kk in range(2):
                    for t in range(2):
                        c = t * D + (2 * i + kk) * P
                        last = turn(out[:, (2 * kk + t) * P:(2 * kk + t + 1) * P], slot[:, c:c + P])
                last.then_inc(tv_ready, 1)

            def conv_rows(j):
                t0, n = TILES[j]
                out = open_tv(f"cf{j}")
                for i in range(4):
                    last = turn(out[0:n, i * P:(i + 1) * P], conv[:, i, t0:t0 + n])
                last.then_inc(tv_ready, 1)

            def keys_turned(h):
                out = open_tv(f"kt{h}")
                for kk in range(2):
                    for t in range(2):
                        c = t * XH_DIM + kk * P
                        last = turn(out[:, (2 * kk + t) * P:(2 * kk + t + 1) * P], zt[h % 2][:, c:c + P])
                last.then_inc(tv_ready, 1)

            pe.wait_ge(tv_used, TV_AT["mem3"] + 1)
            for n in range(8, 16):
                pe.wait_ge(l_ready, n + 1)
                wh = w_h[n % 2][:].rearrange("p (k c) -> p k c", k=8)
                wl = w_l[n % 2][:].rearrange("p (k c) -> p k c", k=8)
                for t in range(2):
                    m = 2 * (n - 8) + t
                    out = open_mm(("wk", m) if n < 12 else ("wv", m - 8))
                    for k in range(8):
                        last = three(out[:, 0, 0:MEM], xH[:, k, t * P:(t + 1) * P], xL[:, k, t * P:(t + 1) * P],
                                     wh[:, k, :], wl[:, k, :], k == 0, k == 7)
                    last.then_inc(mm_ready, 1)
                if n == 8:
                    pe.wait_ge(v_ready, NT)
                    out = open_tv("vs")
                    for h in range(HEADS):
                        last = turn(out[:, h * NS:(h + 1) * NS], v_s[0:NS, h * P:(h + 1) * P], NS)
                    last.then_inc(tv_ready, 1)
                    for h in range(HEADS):
                        out = open_tv(f"mix{h}")
                        for c in range(4):
                            last = pe.matmul(out[:, c * P:(c + 1) * P], v_tok[:, c, h * P:(h + 1) * P], wsT[:, h, :],
                                             start=True, stop=True)
                        last.then_inc(tv_ready, 1)
                if 9 <= n < 13:
                    pe.wait_ge(mm_used, MM_AT[("wk", 2 * (n - 9) + 1)] + 1)
                    keys_turned(n - 9)
            pe.wait_ge(conv_v, CONV_V)
            pe.wait_ge(conv_p, CONV_P - 2)
            pe.wait_ge(convs_done, 4)
            for j in range(NT):
                conv_rows(j)
            for j, (t0, n) in enumerate(TILES):
                pe.wait_ge(cn_ready, j + 1)
                out = open_ta(f"cb{j}")
                row = v_tok[:, j, :] if j < 4 else v_s[0:n]
                for i in range(4):
                    last = turn(out[:, i * P:i * P + n], row[:, i * P:(i + 1) * P], n)
                last.then_inc(ta_ready, 1)
            for k in range(8):
                project("w_out", k, cH, cL, (lambda kk: pe.wait_ge(xl_ready, 8 + kk + 1)) if k == 0 else None)
            for k in range(8):
                project("wq", k, xH, xL, (lambda kk: pe.wait_ge(xl_ready, 16 + kk + 1)) if k == 0 else None)
                if k == 1:
                    sums(1)
            pe.wait_ge(mm_used, MM_AT[("wq", 7)] + 1)
            for b in range(2):
                out = open_ta(f"qs{b}")
                for k in range(4):
                    last = turn(out[0:NS, k * P:(k + 1) * P], qT[:, 4 * b + k, SEQ:T])
                last.then_inc(ta_ready, 1)

            def scores(j):
                out = open_mm(("score", j))
                for h in range(HEADS):
                    for kk in range(2):
                        last = pe.matmul(out[:, h // 2, (h % 2) * MEM:(h % 2 + 1) * MEM],
                                         qT[:, 2 * h + kk, j * P:(j + 1) * P], kT[:, 2 * h + kk, :],
                                         start=kk == 0, stop=kk == 1)
                last.then_inc(mm_ready, 1)

            def query_rows(s):
                for b in range(2):
                    out = open_tv(f"qb{s}{b}")
                    pe.matmul(out, pick[:, s, :], q_s[:, 512 * b:512 * b + 512], start=True, stop=True).then_inc(tv_ready, 1)

            scores(0)
            scores(1)
            pe.wait_ge(ta_used, TA_AT["qs1"] + 1)
            pe.wait_ge(pick_made, 2)
            for j in range(4):
                query_rows(2 * j)
                pe.wait_ge(p_ready, j + 1)
                for b in range(2):
                    out = open_ta(f"pt{j}{b}")
                    for hh in range(2):
                        for t in range(2):
                            last = turn(out[:, (2 * hh + t) * P:(2 * hh + t + 1) * P],
                                        probs[j % 2][:, 2 * b + hh, t * P:(t + 1) * P])
                    last.then_inc(ta_ready, 1)
                query_rows(2 * j + 1)
                if j < 2:
                    scores(j + 2)
            def values(h):
                out = open_mm(("pv", h))
                for kk in range(2):
                    for t in range(2):
                        c = (2 * h + kk) * P
                        last = pe.matmul(out[:, kk, :], vm[:, t, c:c + P], pT[:, h, t, :], start=t == 0, stop=t == 1)
                last.then_inc(mm_ready, 1)

            R = NS * HEADS
            pe.wait_ge(tv_used, TV_AT["qb71"] + 1)
            out = open_tv("ss")
            for t in range(2):
                last = turn(out[0:R, t * P:(t + 1) * P], s_sc[:, t, :])
            last.then_inc(tv_ready, 1)
            pe.wait_ge(ta_used, TA_AT["pt31"] + 1)
            values(0)
            values(1)
            pe.wait_ge(s_norm, 1)
            out = open_tv("sp")
            for t in range(2):
                last = turn(out[:, t * R:(t + 1) * R], s_p[:, t * P:(t + 1) * P], R)
            last.then_inc(tv_ready, 1)
            values(2)
            values(3)
            pe.wait_ge(col_made, 2)
            out0, out1 = open_tv("or0"), open_tv("or1")
            for s in range(NS):
                pe.wait_ge(v_both, s + 1)
                first = pe.matmul(out0[0:NS, :], one_col[:, s, :], v_part[s % 2][:, 0:512], start=s == 0, stop=s == NS - 1)
                if s == NS - 1:
                    first.then_inc(tv_ready, 1)
                last = pe.matmul(out1[0:NS, :], one_col[:, s, :], v_part[s % 2][:, 512:D], start=s == 0, stop=s == NS - 1)
                last.then_inc(v_added if s < NS - 1 else tv_ready, 1)
            pe.wait_ge(tv_used, TV_AT["or1"] + 1)
            out = open_tv("so")
            for k in range(8):
                last = turn(out[:, k * NS:(k + 1) * NS], o_s[:, k * P:(k + 1) * P], NS)
            last.then_inc(tv_ready, 1)
            pe.wait_ge(mm_used, MM_AT[("pv", 3)] + 1)
            pe.wait_ge(tv_used, TV_AT["so"] + 1)
            W = NG + EXPERTS
            logit = []

            def logits_of(k):
                if k == 0:
                    pe.wait_ge(rg_ready, 1)
                    logit.extend((open_tv("lg0"), open_tv("lg1")))
                pe.wait_ge(mm_used, MM_AT[("wo", k)] + 1)
                for b in range(2):
                    last = pe.matmul(logit[b][0:W, 0:HT], router[:, k, :], xT[:, k, b * HT:(b + 1) * HT],
                                     start=k == 0, stop=k == 7)
                    if k == 7:
                        last.then_inc(tv_ready, 1)

            for k in range(8):
                project("wo", k, xH, xL)
                if k:
                    logits_of(k - 1)
            logits_of(7)
            pe.wait_ge(sq_added, 24)
            out = open_tv("r2")
            for j, (t0, n) in enumerate(TILES):
                last = pe.matmul(out[0:n, j:j + 1], sumsq[:, t0:t0 + n], ones[:, 0:1], start=True, stop=True)
            last.then_inc(tv_ready, 1)
            out = open_tv("lg")
            pe.wait_ge(tv_used, TV_AT["lg1"] + 1)
            for j, (t0, n) in enumerate(TILES):
                last = turn(out[0:n, j * W:(j + 1) * W], lg_rows[:, t0:t0 + n], W)
            last.then_inc(tv_ready, 1)
            for j, (t0, n) in enumerate(TILES):
                for b in range(2):
                    out = open_ta(f"t{j}{b}")
                    for k in range(4):
                        last = turn(out[0:n, k * P:(k + 1) * P], xT[:, 4 * b + k, t0:t0 + n])
                    last.then_inc(ta_ready, 1)
            pe.wait_ge(who_ready, 1)
            out = open_tv("pos")
            for j, (_, n) in enumerate(TILES):
                o = out[:, j * EXPERTS:(j + 1) * EXPERTS]
                for i in range(j):
                    pe.matmul(o, ones[:], both[:, i, :], start=i == 0, stop=False)
                last = pe.matmul(o, upper[0:n, :], both[0:n, j, :], start=j == 0, stop=True)
            last.then_inc(tv_ready, 1)
            out = open_tv("cnt")
            for j, (_, n) in enumerate(TILES):
                last = pe.matmul(out[:, 0:EXPERTS], ones[0:n, :], both[0:n, j, :], start=j == 0, stop=j == NT - 1)
            last.then_inc(tv_ready, 1)

            def hidden(q, j, r, old):
                if r == 0:
                    pe.wait_ge(xel_ready, q + 1)
                    if old:
                        pe.wait_ge(gated_ready, q - 1)
                pe.wait_ge(el_ready[r], q + 1)
                wh = e_h[r][:].rearrange("p (k c) -> p k c", k=4)
                wl = e_l[r][:].rearrange("p (k c) -> p k c", k=4)
                for kk in range(4):
                    k = 4 * r + kk
                    last = three(mm[0][:, j, :], xeH[j][:, k, :], xeL[j][:, k, :], wh[:, kk, :], wl[:, kk, :], k == 0, k == 7)
                last.then_inc(hid_ready if r else e_used, 1)

            def gathered_columns(q, it, j, old):
                pe.wait_ge(xe_landed[j], (it + 1) * 16)
                if old:
                    pe.wait_ge(xel_ready, q)
                rows = xe[j][:].rearrange("s (p k) -> s k p", k=KT_D)
                for k in range(KT_D):
                    last = turn(tv[k // 4][:, (k % 4) * P:(k % 4 + 1) * P], rows[:, k, :])
                last.then_inc(xt_done, 1)

            def act_columns(q, old):
                pe.wait_ge(gated_ready, q + 1)
                if old:
                    pe.wait_ge(al_ready, q)
                rows = gated[:].rearrange("s (p k) -> s k p", k=2)
                for k in range(2):
                    last = turn(ta[0][:, k * P:(k + 1) * P], rows[:, k, :])
                last.then_inc(at_done, 1)

            def down(q, old):
                pe.wait_ge(al_ready, q + 1)
                pe.wait_ge(el_ready[2], q + 1)
                if old:
                    pe.wait_ge(ya_ready, q)
                    pe.wait_ge(yv_ready, q)
                wh = e_h[2][:].rearrange("p (k d) -> p k d", k=2)
                wl = e_l[2][:].rearrange("p (k d) -> p k d", k=2)
                for b in range(2):
                    c = slice(512 * b, 512 * b + 512)
                    for k in range(2):
                        last = three(mm[1][:, b, :], aH[:, k, :], aL[:, k, :], wh[:, k, c], wl[:, k, c], k == 0, k == 1)
                last.then_inc(y_done, 1)

            def step(q, it, j, first, last):
                lag = not (first and j == 0)
                hidden(q, j, 0, not first)
                if lag:
                    act_columns(q - 1, not (first and j == 1))
                if not (last and j == 1):
                    gathered_columns(q + 1, it if j == 0 else it + 1, 1 - j, True)
                hidden(q, j, 1, not first)
                if lag:
                    down(q - 1, not (first and j == 1))

            pe.wait_ge(tv_used, len(TV_ORDER))
            pe.wait_ge(ta_used, len(TA_ORDER))
            gathered_columns(0, 0, 0, False)
            for j in range(2):
                step(j, 0, j, True, False)
            pe.wait_ge(pass_ready, 1)
            extra = pe.value_load(more[0:1, 0:1], min_val=0, max_val=LIST_ROWS // P - 1)
            last_it = extra * (EXPERTS // 2) + (EXPERTS // 2 - 1)
            with pe.Fori(1, last_it) as it:
                for j in range(2):
                    step(it * 2 + j, it, j, False, False)
            for j in range(2):
                step(last_it * 2 + j, last_it, j, False, True)
            act_columns(last_it * 2 + 1, True)
            down(last_it * 2 + 1, True)

        @block.gpsimd
        def _(pool):
            def wait(s, value):
                pool.wait_ge(s, value)
                pool.sem_inc(pool_waits, 1)

            pool.memset(ident[:], 0.0).then_inc(pool_made, 1)
            pool.wait_ge(pool_made, 1)
            pool.affine_select(out=ident[:], in_=ident[:], compare_op=ALU.not_equal, fill=1.0, base=0,
                               pattern=[[-1, P]], channel_multiplier=1).then_inc(pool_made, 1)
            pool.memset(upper[:], 1.0).then_inc(pool_made, 1)
            pool.wait_ge(pool_made, 3)
            pool.affine_select(out=upper[:], in_=upper[:], compare_op=ALU.is_gt, fill=0.0, base=0,
                               pattern=[[1, P]], channel_multiplier=-1).then_inc(pool_made, 1)
            pool.memset(list_init[:], NOBODY).then_inc(pool_made, 1)
            pool.wait_ge(pool_made, 5)
            blank = id_list.rearrange("(c p n) o -> c p (n o)", c=2, p=P)
            for i in range(2):
                pool.dma_start(blank[i], list_init[:]).then_inc(y_stored[i], 16)
            pool.memset(one_col[:], 0.0).then_inc(col_made, 1)
            pool.wait_ge(col_made, 1)
            pool.memset(one_col[:].rearrange("p a b -> p (a b)")[:, ::NS + 1], 1.0).then_inc(col_made, 1)
            pool.wait_ge(rows_in, 32)
            pool.affine_select(out=ws_rows[:], in_=ws_rows[:], compare_op=ALU.is_ge, fill=0.0, base=0,
                               pattern=[[0, HEADS], [-1, P]], channel_multiplier=1).then_inc(masked, 1)

            def add_squares(n):
                for k in range(8):
                    pool.wait_ge(sq_ready, 8 * n + k + 1)
                    if k == 0:
                        ins = pool.tensor_copy(sumsq[:], zt[0][:])
                    else:
                        pool.wait_ge(sq_added, 8 * n + k)
                        ins = pool.tensor_tensor(sumsq[:], sumsq[:], zt[k % 2][:], ALU.add)
                    ins.then_inc(sq_added, 1)

            add_squares(0)
            def add_products(n0, n1):
                for n in range(n0, n1):
                    i, k = tap_p(n)
                    if k:
                        p = n - min(n // TAPS, 1) - 1
                        pool.wait_ge(tap_scaled, n + 1)
                        if i == 2:
                            pool.wait_ge(conv_v, CONV_V)
                        if p:
                            pool.wait_ge(conv_p, p)
                        pool.tensor_tensor(conv[:, i, 0:SEQ], conv[:, i, 0:SEQ], scaled[p % 4][:], ALU.add).then_inc(conv_p, 1)

            add_products(0, 48)
            pool.wait_ge(consts_in, 16 * 4)
            for j, (_, n) in enumerate(TILES):
                row = v_tok[:, j, :] if j < 4 else v_s[0:n]
                pool.wait_ge(v_norm, j + 1)
                pool.tensor_tensor(row, row, ln_g[0:n], ALU.mult).then_inc(v_scaled, 1)
                pool.wait_ge(v_scaled, j + 1)
                pool.tensor_tensor(row, row, ln_b[0:n], ALU.add).then_inc(v_ready, 1)
            add_products(48, CONV_P)
            pool.wait_ge(ta_ready, TA_AT[f"cb{NT - 1}"] + 1)
            pool.memset(pick[:], 0.0).then_inc(pick_made, 1)
            pool.wait_ge(pick_made, 1)
            pool.affine_select(out=pick[:], in_=pick[:], compare_op=ALU.not_equal, fill=1.0, base=0,
                               pattern=[[-1, NS], [0, P]], channel_multiplier=1).then_inc(pick_made, 1)
            add_squares(1)
            pool.wait_ge(ta_ready, TA_AT["pt31"] + 1)
            pool.iota(prio[:], pattern=[[-1, 8]], base=8, channel_multiplier=0,
                      allow_small_or_imprecise_dtypes=True).then_inc(route_made, 1)
            pool.iota(e_num[:], pattern=[[1, EXPERTS]], base=0, channel_multiplier=0,
                      allow_small_or_imprecise_dtypes=True).then_inc(route_made, 1)
            pool.iota(ident_no[:], pattern=[[1, 2], [2 * P, NT]], base=0, channel_multiplier=2).then_inc(route_made, 1)
            add_squares(2)
            pool.wait_ge(place_ready, 1)
            pool.wait_ge(route_made, 3)
            pool.wait_ge(y_stored[0], 16)
            pool.wait_ge(y_stored[1], 16)
            for i in range(2):
                for j, (_, n) in enumerate(TILES):
                    pool.indirect_dma_start(
                        out=id_list, out_offset=bass.IndirectOffsetOnAxis(ap=place_i[0:n, i, j:j + 1], axis=0),
                        in_=ident_no[0:n, i, j:j + 1], in_offset=None, bounds_check=LIST_ROWS * EXPERTS - 1,
                        oob_is_err=False).then_inc(list_made, 16)
            pool.wait_ge(mm_ready, len(MM_ORDER))
            pool.memset(xe[0][:], 0.0).then_inc(xe_zero, 1)
            pool.memset(xe[1][:], 0.0).then_inc(xe_zero, 1)
            pool.wait_ge(list_made, 16 * 2 * NT)
            pool.dma_start(ids[:], id_list.rearrange("(c s e) o -> s c (e o)", c=LIST_ROWS // P, e=EXPERTS)).then_inc(list_in, 16)
            pool.wait_ge(gids_ready, 1)
            for i, stores in enumerate((2, 2, 1)):
                pool.wait_ge(xn_stored[i], 16 * stores)
            pool.wait_ge(xe_zero, 2)
            pool.wait_ge(pass_ready, 1)
            extra = pool.value_load(more[0:1, 0:1], min_val=0, max_val=LIST_ROWS // P - 1)
            last_it = extra * (EXPERTS // 2) + (EXPERTS // 2 - 1)
            ids_f = ids[:].rearrange("p c e -> p (c e)")
            gids_f = gids[:].rearrange("p c e -> p (c e)")

            full_i = full[:].rearrange("p c e -> p (c e)")

            def fullness(q):
                return pool.value_load(full_i[0:1, q:q + 1] if isinstance(q, int) else full_i[0:1, bass.ds(q, 1)],
                                       min_val=0, max_val=2)

            def gather(j, n):
                pool.indirect_dma_start(out=xe[j][0:n], out_offset=None, in_=xn_rows,
                                        in_offset=bass.IndirectOffsetOnAxis(ap=g_idx[j][0:n], axis=0),
                                        bounds_check=T - 1, oob_is_err=False).then_inc(xe_landed[j], 16)

            def scatter_rows(j, n):
                pool.indirect_dma_start(out=y_rows, out_offset=bass.IndirectOffsetOnAxis(ap=s_idx[j][0:n], axis=0),
                                        in_=ye[j][0:n], in_offset=None, bounds_check=2 * T - 1,
                                        oob_is_err=False).then_inc(y_stored[j], 16)

            def taken_only(move, q, j):
                level = fullness(q)
                with pool.If(level > 0):
                    with pool.If(level > 1):
                        move(j, P)
                    with pool.Else():
                        move(j, P // 2)
                with pool.Else():
                    move(j, P // 4)

            def step(q, it, j, first, last):
                if not last:
                    wait(xt_done, q + 1)
                    pool.tensor_copy(g_idx[j][:], gids_f[:, bass.ds(q + 2, 1)]).then_inc(gi_made[j], 1)
                    wait(gi_made[j], it + 2)
                    taken_only(gather, q + 2, j)
                if not first:
                    scatter(q - 2, it - 1, j)

            def scatter(q, it, j):
                wait(y_stored[j], it * 16 + 16)
                pool.tensor_copy(s_idx[j][:], ids_f[:, bass.ds(q, 1)]).then_inc(si_made[j], 1)
                wait(si_made[j], it + 1)
                wait(ya_ready, q + 1)
                wait(yv_ready, q + 1)
                taken_only(scatter_rows, q, j)

            for j in range(2):
                pool.tensor_copy(g_idx[j][:], gids_f[:, j:j + 1]).then_inc(gi_made[j], 1)
                pool.wait_ge(gi_made[j], 1)
                taken_only(gather, j, j)
            for j in range(2):
                step(j, 0, j, True, False)
            with pool.Fori(1, last_it) as it:
                for j in range(2):
                    step(it * 2 + j, it, j, False, False)
            for j in range(2):
                step(last_it * 2 + j, last_it, j, False, True)
            for j in range(2):
                scatter(last_it * 2 + j, last_it, j)
            for t in range(NT):
                if t not in LAST_BY_DVE:
                    n = TILES[t][1]
                    pool.wait_ge(y_scaled, t + 1)
                    pool.tensor_tensor(yo[t][0:n], yo[t][0:n], fin_g[0:n], ALU.mult).then_inc(y_out[t], 1)


_IN = ["x_prompt", "x_sample", "mem_prompt", "cache_conv", "cache_mem_k", "cache_mem_v", "norm_mix_g", "w_in",
       "gm_ln_g", "gm_ln_b", "gm_ws", "gm_bs", "conv_w", "conv_b", "cv_ln_g", "cv_ln_b", "w_out", "norm_mem_g",
       "norm_xa_g", "xa_wq", "xa_wk", "xa_wv", "xa_wo", "norm_ffn_g", "router_g", "router_g_b", "router_e",
       "router_e_b", "exp_w1", "exp_w3", "exp_w2", "final_norm_g"]
_OUT = [("y_prompt", (1, SEQ, D)), ("y_sample", (NS, 1, D)), ("conv_prompt", (1, 1, PAST, GM)),
        ("conv_sample", (1, NS, PAST, GM)), ("gmv_prompt", (1, 1, P, GM)), ("gmv_sample", (1, NS, 1, GM)),
        ("mem_k_prompt", (1, 1, MEM, HEADS, XH_DIM)), ("mem_v_prompt", (1, 1, MEM, HEADS, XH_DIM))]


def kernel(**inputs):
    import concourse.bacc as bacc
    from concourse.bass_utils import run_bass_kernel_spmd

    nc = bacc.Bacc("TRN2", target_bir_lowering=False, num_devices=1)
    arrays, args = {}, {}
    for name in _IN:
        arrays[name] = np.ascontiguousarray(inputs[name])
        args[name] = nc.dram_tensor(name, arrays[name].shape, F32, kind="ExternalInput").ap()
    outs = [nc.dram_tensor(f"out_{name}", shape, F32, kind="ExternalOutput").ap() for name, shape in _OUT]
    trunk_kernel(nc, args, outs)
    r = run_bass_kernel_spmd(nc, [arrays], core_ids=[0])
    return tuple(r.results[0][f"out_{name}"] for name, _ in _OUT)
```
